# Optimizing a Trainium2 kernel written in Bass

```python
import jax, jax.numpy as jnp
from jax import lax
import numpy as np

D_MODEL = 1024
BATCH = 1
SEQ = 256
DEPTH = 4

CHUNK = 64
Q_BLOCK = 128
N_MIXERS = 3
N_FOX = (DEPTH + 2) // 3
N_GLA = (DEPTH + 1) // 3
N_HGRN = DEPTH // 3
EPS = 1e-6

FOX_HEADS = 16
FOX_HEAD_DIM = D_MODEL // FOX_HEADS
FOX_IN = 4 * D_MODEL + FOX_HEADS

GLA_HEADS = 4
GLA_DK = D_MODEL // 2 // GLA_HEADS
GLA_DV = D_MODEL // GLA_HEADS
GLA_RANK = 16
GLA_TAU = 16.0
GLA_IN = 2 * GLA_HEADS * GLA_DK + 2 * D_MODEL + GLA_RANK

HGRN_EXPAND = 128
HGRN_HEADS = D_MODEL // HGRN_EXPAND
HGRN_DV = D_MODEL // HGRN_HEADS
HGRN_IN = 4 * D_MODEL

PEER_HEADS = 8
PEER_NKEYS = 128
PEER_EXPERTS = PEER_NKEYS * PEER_NKEYS
PEER_DQ = 256
PEER_TOPK = 16
PEER_TOKEN_BLOCK = 128

kernel_name = "hybrid_fox_gla_hgrn2_peer_trunk"

def rms_norm(x, g):
    xf = x.astype(jnp.float32)
    y = xf * lax.rsqrt(jnp.mean(xf * xf, axis=-1, keepdims=True) + EPS)
    return (y * g.astype(jnp.float32)).astype(x.dtype)

def to_heads(a, n_heads):
    B, T, W = a.shape
    return a.reshape(B, T, n_heads, W // n_heads).transpose(0, 2, 1, 3)

def from_heads(a):
    B, H, T, d = a.shape
    return a.transpose(0, 2, 1, 3).reshape(B, T, H * d)

def forgetting_attention(q, k, v, log_f):
    B, H, T, d = q.shape
    c = jnp.cumsum(log_f, axis=-1)
    scale = d ** -0.5
    outs = []
    for i in range(T // Q_BLOCK):
        lo, hi = i * Q_BLOCK, (i + 1) * Q_BLOCK
        s = jnp.einsum('bhqd,bhkd->bhqk', q[:, :, lo:hi], k[:, :, :hi]).astype(jnp.float32) * scale
        s = s + (c[:, :, lo:hi, None] - c[:, :, None, :hi])
        mask = (lo + jnp.arange(Q_BLOCK))[:, None] >= jnp.arange(hi)[None, :]
        p = jax.nn.softmax(jnp.where(mask, s, -jnp.inf), axis=-1)
        outs.append(jnp.einsum('bhqk,bhkd->bhqd', p.astype(v.dtype), v[:, :, :hi]))
    return jnp.concatenate(outs, axis=2)

def chunked_gated_linear_attention(q, k, v, log_g):
    B, H, T, dk = q.shape
    dv = v.shape[-1]
    n = T // CHUNK

    def to_chunks(a):
        return a.astype(jnp.float32).reshape(B, H, n, CHUNK, a.shape[-1]).transpose(2, 0, 1, 3, 4)

    causal = jnp.tril(jnp.ones((CHUNK, CHUNK), dtype=bool))[:, :, None]

    def step(S, inp):
        qc, kc, vc, gc = inp
        b = jnp.cumsum(gc, axis=2)
        diff = b[:, :, :, None, :] - b[:, :, None, :, :]
        decay = jnp.where(causal, jnp.exp(jnp.where(causal, diff, 0.0)), 0.0)
        scores = jnp.einsum('bhtd,bhsd,bhtsd->bhts', qc, kc, decay)
        o = jnp.einsum('bhts,bhsv->bhtv', scores, vc) + jnp.einsum('bhtd,bhdv->bhtv', qc * jnp.exp(b), S)
        b_end = b[:, :, -1:, :]
        S = S * jnp.exp(b_end[:, :, 0, :, None]) + jnp.einsum('bhsd,bhsv->bhdv', kc * jnp.exp(b_end - b), vc)
        return S, o

    S0 = jnp.zeros((B, H, dk, dv), jnp.float32)
    _, o = lax.scan(step, S0, (to_chunks(q), to_chunks(k), to_chunks(v), to_chunks(log_g)))
    return o.transpose(1, 2, 0, 3, 4).reshape(B, H, T, dv).astype(v.dtype)

def fox_mixer(x, w_in, b_f, q_gain, k_gain, w_out):
    proj = x @ w_in
    q, k, v, g, f = jnp.split(proj, [D_MODEL, 2 * D_MODEL, 3 * D_MODEL, 4 * D_MODEL], axis=-1)
    q = rms_norm(to_heads(q, FOX_HEADS), q_gain)
    k = rms_norm(to_heads(k, FOX_HEADS), k_gain)
    log_f = jax.nn.log_sigmoid((f + b_f).astype(jnp.float32)).transpose(0, 2, 1)
    o = forgetting_attention(q, k, to_heads(v, FOX_HEADS), log_f)
    o = o * jax.nn.sigmoid(to_heads(g, FOX_HEADS))
    return from_heads(o) @ w_out

def gla_mixer(x, w_in, w_up, b_alpha, out_gain, w_out):
    gk = GLA_HEADS * GLA_DK
    proj = x @ w_in
    q, k, v, r, low = jnp.split(proj, [gk, 2 * gk, 2 * gk + D_MODEL, 2 * gk + 2 * D_MODEL], axis=-1)
    log_a = jax.nn.log_sigmoid((low @ w_up + b_alpha).astype(jnp.float32)) / GLA_TAU
    o = chunked_gated_linear_attention(to_heads(q, GLA_HEADS) * (GLA_DK ** -0.5), to_heads(k, GLA_HEADS),
                                       to_heads(v, GLA_HEADS), to_heads(log_a, GLA_HEADS))
    o = rms_norm(o, out_gain[:, None, :]) * jax.nn.silu(to_heads(r, GLA_HEADS))
    return from_heads(o) @ w_out

def hgrn2_mixer(x, w_in, lb, out_gain, w_out):
    proj = x @ w_in
    q, f, i, g = jnp.split(proj, 4, axis=-1)
    gate = lb + (1.0 - lb) * jax.nn.sigmoid(f.astype(jnp.float32))
    k = 1.0 - gate
    o = chunked_gated_linear_attention(to_heads(q, HGRN_HEADS) * (HGRN_EXPAND ** -0.5), to_heads(k, HGRN_HEADS),
                                       to_heads(i, HGRN_HEADS), to_heads(jnp.log(gate), HGRN_HEADS))
    o = rms_norm(o, out_gain[:, None, :]) * jax.nn.silu(to_heads(g, HGRN_HEADS))
    return from_heads(o) @ w_out

def peer_mixer(x, w_q, sub_keys, u, v):
    B, T, D = x.shape
    N = B * T
    xt = x.reshape(N, D)
    q = (xt @ w_q).reshape(N, PEER_HEADS, 2, PEER_DQ // 2)
    s = jnp.einsum('nhpd,hpkd->nhpk', q, sub_keys).astype(jnp.float32)
    s_top, i_top = lax.top_k(s, PEER_TOPK)
    cand = (s_top[:, :, 0, :, None] + s_top[:, :, 1, None, :]).reshape(N, PEER_HEADS, PEER_TOPK * PEER_TOPK)
    cand_idx = (i_top[:, :, 0, :, None] * PEER_NKEYS + i_top[:, :, 1, None, :]).reshape(N, PEER_HEADS, PEER_TOPK * PEER_TOPK)
    best, pos = lax.top_k(cand, PEER_TOPK)
    experts = jnp.take_along_axis(cand_idx, pos, axis=-1)
    gates = jax.nn.softmax(best, axis=-1)
    n_blk = N // PEER_TOKEN_BLOCK

    def apply(args):
        xb, eb, gb = args
        h = jax.nn.gelu(jnp.einsum('tpkd,td->tpk', u[eb], xb).astype(jnp.float32), approximate=False)
        return jnp.einsum('tpk,tpkd->td', (gb * h).astype(v.dtype), v[eb])

    y = lax.map(apply, (xt.reshape(n_blk, PEER_TOKEN_BLOCK, D),
                        experts.reshape(n_blk, PEER_TOKEN_BLOCK, PEER_HEADS, PEER_TOPK),
                        gates.reshape(n_blk, PEER_TOKEN_BLOCK, PEER_HEADS, PEER_TOPK)))
    return y.reshape(B, T, D)

def setup_inputs(seed: int = 0) -> dict:
    key = jax.random.key(seed)
    ks = jax.random.split(key, 24)
    nrm = jax.random.normal
    D = D_MODEL
    f32 = jnp.float32
    return {
        "x": nrm(ks[0], (BATCH, SEQ, D), f32),
        "norm_mix": 1.0 + 0.05 * nrm(ks[1], (DEPTH, D), f32),
        "norm_ffn": 1.0 + 0.05 * nrm(ks[2], (DEPTH, D), f32),
        "fox_w_in": nrm(ks[3], (N_FOX, D, FOX_IN), f32) * D ** -0.5,
        "fox_b_f": 2.0 + 0.5 * nrm(ks[4], (N_FOX, FOX_HEADS), f32),
        "fox_q_gain": 1.0 + 0.05 * nrm(ks[5], (N_FOX, FOX_HEAD_DIM), f32),
        "fox_k_gain": 1.0 + 0.05 * nrm(ks[6], (N_FOX, FOX_HEAD_DIM), f32),
        "fox_w_out": nrm(ks[7], (N_FOX, D, D), f32) * D ** -0.5,
        "gla_w_in": nrm(ks[8], (N_GLA, D, GLA_IN), f32) * D ** -0.5,
        "gla_w_up": nrm(ks[9], (N_GLA, GLA_RANK, GLA_HEADS * GLA_DK), f32) * GLA_RANK ** -0.5,
        "gla_b_alpha": 0.1 * nrm(ks[10], (N_GLA, GLA_HEADS * GLA_DK), f32),
        "gla_out_gain": 1.0 + 0.05 * nrm(ks[11], (N_GLA, GLA_HEADS, GLA_DV), f32),
        "gla_w_out": nrm(ks[12], (N_GLA, D, D), f32) * D ** -0.5,
        "hgrn_w_in": nrm(ks[13], (N_HGRN, D, HGRN_IN), f32) * D ** -0.5,
        "hgrn_lb_logits": 0.5 * nrm(ks[14], (DEPTH, D), f32),
        "hgrn_out_gain": 1.0 + 0.05 * nrm(ks[15], (N_HGRN, HGRN_HEADS, HGRN_DV), f32),
        "hgrn_w_out": nrm(ks[16], (N_HGRN, D, D), f32) * D ** -0.5,
        "peer_w_q": nrm(ks[17], (DEPTH, D, PEER_HEADS * PEER_DQ), f32) * D ** -0.5,
        "peer_sub_keys": nrm(ks[18], (DEPTH, PEER_HEADS, 2, PEER_NKEYS, PEER_DQ // 2), f32) * (PEER_DQ // 2) ** -0.5,
        "peer_u": nrm(ks[19], (DEPTH, PEER_EXPERTS, D), f32) * D ** -0.5,
        "peer_v": nrm(ks[20], (DEPTH, PEER_EXPERTS, D), f32) * (PEER_HEADS * PEER_TOPK) ** -0.5,
    }

def reference(x, norm_mix, norm_ffn, fox_w_in, fox_b_f, fox_q_gain, fox_k_gain, fox_w_out,
              gla_w_in, gla_w_up, gla_b_alpha, gla_out_gain, gla_w_out,
              hgrn_w_in, hgrn_lb_logits, hgrn_out_gain, hgrn_w_out,
              peer_w_q, peer_sub_keys, peer_u, peer_v):
    p = jax.nn.softmax(hgrn_lb_logits.astype(jnp.float32), axis=0)
    lower_bounds = jnp.cumsum(p, axis=0) - p[0:1]
    h = x
    for i in range(DEPTH):
        m, j = i % N_MIXERS, i // N_MIXERS
        hn = rms_norm(h, norm_mix[i])
        if m == 0:
            y = fox_mixer(hn, fox_w_in[j], fox_b_f[j], fox_q_gain[j], fox_k_gain[j], fox_w_out[j])
        elif m == 1:
            y = gla_mixer(hn, gla_w_in[j], gla_w_up[j], gla_b_alpha[j], gla_out_gain[j], gla_w_out[j])
        else:
            y = hgrn2_mixer(hn, hgrn_w_in[j], lower_bounds[i], hgrn_out_gain[j], hgrn_w_out[j])
        h = h + y.astype(h.dtype)
        h = h + peer_mixer(rms_norm(h, norm_ffn[i]), peer_w_q[i], peer_sub_keys[i], peer_u[i], peer_v[i]).astype(h.dtype)
    return h


_drawn_inputs = setup_inputs


def setup_inputs(seed=0):
    import zlib

    import numpy as np

    out = dict(_drawn_inputs(seed))
    spreads = {}
    factors = {'fox_k_gain': 2.739}
    for name, (base, spread) in spreads.items():
        noise = np.random.default_rng([zlib.crc32(name.encode()), seed]).standard_normal(out[name].shape)
        drawn = base * np.exp(spread * noise) if base else spread * noise
        out[name] = __import__('jax').numpy.asarray(drawn.astype(out[name].dtype))
    for name, factor in factors.items():
        out[name] = (out[name] * factor).astype(out[name].dtype)
    return out
```

```python
from contextlib import ExitStack

import numpy as np

import concourse.bass as bass
from concourse import mybir

ALU = mybir.AluOpType
ACT = mybir.ActivationFunctionType
F32 = mybir.dt.float32
F32R = mybir.dt.float32r
U32 = mybir.dt.uint32
AX = mybir.AxisListType

P = 128
D = 1024
SEQ = 256
TT = SEQ // P
DC = D // P
DEPTH = 4
EPS = 1e-6
NEG = -1e30
FOX_HEADS, FOX_DH = 16, 64
GLA_HEADS, GLA_DK, GLA_RANK, GLA_TAU = 4, 128, 16, 16.0
HGRN_HEADS = 8
PH, NK, TOPK = 8, 128, 16
NCH = NK
HALF = NCH // 2
LEVELS = 7

RAW, HI, LO = 4, 4, 2

SCORES_AT = 24
EXP_AT = [28, 60]

KIND = ["fox", "gla", "hgrn", "fox"]
GROUPS = {"fox": 4, "gla": 3, "hgrn": 4}
SMALL = {"fox": 1, "gla": 1, "hgrn": 0}
HEADS = {"fox": FOX_HEADS, "gla": GLA_HEADS, "hgrn": HGRN_HEADS}


HANDED = [(0, 0), (1, 1), (2, 2), (5, 4)]


class Plan:

    def __init__(self):
        self.layers = []
        n = ev = tq = gu = 0
        fox = small = 0
        for l, kind in enumerate(KIND):
            L = {"l": l, "kind": kind, "ev": ev, "tq": tq, "gu": gu, "fox": fox, "smallno": small}
            L["small"] = n
            n += SMALL[kind]
            L["in"] = n
            n += GROUPS[kind] * DC
            L["out"] = n
            n += DC
            L["wq"] = n
            n += 2 * PH
            L["u"] = n
            n += NCH
            L["v"] = n
            n += NCH
            L["end"] = n
            ev += 4 * GROUPS[kind]
            tq += 2 if kind == "gla" else 4
            if kind == "fox":
                fox += 1
            else:
                gu += 2 * HEADS[kind]
            small += SMALL[kind]
            self.layers.append(L)
        self.slabs = n


PLAN = Plan()

PRM = {}
_at = 0
for _name, _w in (("mix", DEPTH * DC), ("ffn", DEPTH * DC), ("gla_gain", DC), ("hgrn_gain", DC),
                  ("qg", 2), ("kg", 2), ("bf", 2), ("lb", DEPTH * DC)):
    PRM[_name] = _at
    _at += _w
NPRM = _at

O_P = 0
O_T = 8192
O_XN = 12288
O_LG = 14336
O_MC = 16384
O_MK = O_MC + 9 * P
O_ST = O_MK + 8 * P
O_SK = 20480
O_E = 22528
O_QD = 24576
O_KD = 26624
O_A = 28672
O_KS = 29696
O_SM = 30720
O_WUP = 32256
O_QT = 16384
O_CAND = 22528
O_EQ = 24576
O_TMP = 26624
O_RS = 28672


def build(nc, stream, x, prm_d, wup_d, sk_d, out):
    N = PLAN.slabs
    with ExitStack() as ctx:
        def sb(name, shape, dt=F32):
            return ctx.enter_context(nc.sbuf_tensor(name, shape, dt))

        def sem(name):
            return ctx.enter_context(nc.semaphore(name))

        resid = sb("resid", [P, TT, D])
        xhi = sb("xhi", [P, DC, SEQ], F32R)
        xlo = sb("xlo", [P, DC, SEQ], F32R)
        big = sb("big", [P, NCH * SEQ])
        raw = sb("raw", [P, RAW, D])
        hi = sb("hi", [P, HI, D], F32R)
        lo = sb("lo", [P, LO, D], F32R)
        ident = sb("ident", [P, P])
        iota = sb("iota", [P, P])
        prm = sb("prm", [P, NPRM])
        e1T = sb("e1T", [P, SEQ])
        e2T = sb("e2T", [P, SEQ])
        ghi = sb("ghi", [P, SEQ], F32R)
        glo = sb("glo", [P, SEQ], F32R)
        oh1 = sb("oh1", [P, 2, 4, P], F32R)
        oh2 = sb("oh2", [P, 2, 4, HALF])
        ohg = sb("ohg", [P, 2, 2, 4, HALF], F32R)
        sm = sb("sm", [P, 64])
        ps = ctx.enter_context(nc.psum_tensor("ps", [P, 8, 512], F32))

        s_raw = [sem(f"s_raw{i}") for i in range(RAW)]
        s_hi, s_lo, s_used = sem("s_hi"), sem("s_lo"), sem("s_used")
        s_x, s_const = sem("s_x"), sem("s_const")
        s_xn, s_tp, s_xhi, s_xlo = sem("s_xn"), sem("s_tp"), sem("s_xhi"), sem("s_xlo")
        s_ss, s_sq = sem("s_ss"), sem("s_sq")
        s_ev = sem("s_ev")
        s_mc = sem("s_mc")
        s_tq, s_tqd, s_tqa = sem("s_tq"), sem("s_tqd"), sem("s_tqa")
        s_da, s_ab = sem("s_da"), sem("s_ab")
        s_lf, s_lft, s_lfc, s_qk = sem("s_lf"), sem("s_lft"), sem("s_lfc"), sem("s_qk")
        s_s, s_mx, s_exp, s_pt, s_pte, s_pv, s_o = (sem(n) for n in (
            "s_s", "s_mx", "s_exp", "s_pt", "s_pte", "s_pv", "s_o"))
        s_low, s_wup, s_z, s_lg = sem("s_low"), sem("s_wup"), sem("s_z"), sem("s_lg")
        s_lb, s_lbr, s_lbc, s_hk = sem("s_lb"), sem("s_lbr"), sem("s_lbc"), sem("s_hk")
        s_gd, s_gx, s_gq, s_gk, s_gs, s_gm, s_gr, s_gp, s_go = (sem(n) for n in (
            "s_gd", "s_gx", "s_gq", "s_gk", "s_gs", "s_gm", "s_gr", "s_gp", "s_go"))
        s_sk, s_sc, s_rt, s_ge, s_gn, s_route = (sem(n) for n in (
            "s_sk", "s_sc", "s_rt", "s_ge", "s_gn", "s_route"))
        s_cev = sem("s_cev")
        s_whi, s_wlo = sem("s_whi"), sem("s_wlo")
        s_eq, s_ohg, s_g, s_hm = sem("s_eq"), sem("s_ohg"), sem("s_g"), sem("s_hm")
        s_dve, s_act, s_pc = sem("s_dve"), sem("s_act"), sem("s_pc")
        s_done, s_out = sem("s_done"), sem("s_out")

        block = ctx.enter_context(nc.Block())

        def B(off, n):
            return big[:, off:off + n]

        PR = B(O_P, 8192).rearrange("p (t n) -> p t n", t=TT)
        TR = B(O_T, 4096).rearrange("p (c t) -> p c t", t=SEQ)
        XN = B(O_XN, 2048).rearrange("p (t n) -> p t n", t=TT)
        LG = B(O_LG, 2048).rearrange("p (t n) -> p t n", t=TT)
        MC = B(O_MC, 9 * P).rearrange("p (l t) -> p l t", t=P)
        MK = B(O_MK, 8 * P).rearrange("p (l t) -> p l t", t=P)
        ST = B(O_ST, 4 * P).rearrange("p (b t) -> p b t", t=P)
        EB = B(O_E, 2048).rearrange("p (b l t) -> p b l t", b=2, t=P)
        QD = B(O_QD, 2048).rearrange("p (b l t) -> p b l t", b=2, t=P)
        KD = B(O_KD, 2048).rearrange("p (b l t) -> p b l t", b=2, t=P)
        AM = B(O_A, 1024).rearrange("p (l t) -> p l t", t=P)
        KS = B(O_KS, 256).rearrange("p (b t) -> p b t", t=P)
        NU = B(O_MC, 256)
        MASK = B(O_MC + 256, P)
        LFT = B(O_SM, 256)
        LFA = B(O_SM + 256, 256)
        LFB = B(O_SM + 512, 256)
        LF = B(O_SM + 768, 32).rearrange("p (t h) -> p t h", t=TT)
        NM = B(O_SM + 800, 32).rearrange("p (h t) -> p h t", t=TT)
        RSUM = B(O_SM + 832, 32).rearrange("p (h t) -> p h t", t=TT)
        RL = B(O_SM + 864, 32).rearrange("p (h t) -> p h t", t=TT)
        QS = B(O_SM + 896, 64)
        QR = B(O_SM + 960, 64)
        PB = B(O_KD, 768).rearrange("p (b s) -> p b s", b=2)
        PTB = B(O_KD + 768, 768).rearrange("p (b s) -> p b s", b=2)
        LOWT = B(O_SM, 256)
        WUP = B(O_WUP, 512)
        LBC = B(O_SM + 256, 64)
        SCR = B(O_E, 2048)
        SCR2 = B(O_QD, 2048).rearrange("p (t n) -> p t n", t=TT)
        LBR = B(O_KD, 1024)
        OML = B(O_KD + 1024, 1024)
        H = big[:, :].rearrange("p (j t) -> p j t", t=SEQ)
        QT = B(O_QT, 4096).rearrange("p (c t) -> p c t", t=SEQ)
        SK = B(O_SK, 2048)
        CAND = B(O_CAND, 2048)
        EQ = B(O_EQ, 2048)
        TMP = B(O_TMP, 2048).rearrange("p (c k) -> p c k", k=NK)
        VAL = B(O_RS, 256).rearrange("p (c k) -> p c k", k=TOPK)
        IDX = B(O_RS + 256, 256).rearrange("p (c k) -> p c k", k=TOPK)
        IDF = B(O_RS + 512, 256).rearrange("p (c k) -> p c k", k=TOPK)
        BEST = B(O_RS + 768, 128).rearrange("p (h k) -> p h k", k=TOPK)
        POS = B(O_RS + 896, 128).rearrange("p (h k) -> p h k", k=TOPK)
        PAB = B(O_RS + 1024, 256).rearrange("p (s c) -> p s c", s=2)
        PAF = B(O_RS + 1280, 256).rearrange("p (s c) -> p s c", s=2)
        ROUT = [B(O_RS + 1536 + 3 * P * t, 3 * P).rearrange("p (w c) -> p w c", w=3) for t in range(TT)]
        ZS = B(O_RS + 2304, 16)
        EX = B(O_RS + 2320, 128).rearrange("p (h k) -> p h k", k=TOPK)

        def steps(eng, n, body, first=False):
            lo4, hi4 = (1 if first else 0), n // 4 - 1
            if first:
                for s in range(4):
                    body(0, s, s)
            with eng.Fori(lo4, hi4) as i:
                for s in range(4):
                    body(i, s, i * 4 + s)
            for s in range(4):
                body(hi4, s, 4 * hi4 + s)

        def chunk(j):
            return H[:, j, :] if isinstance(j, int) else H[:, bass.ds(j, 1), :].rearrange("p c t -> p (c t)")

        @block.sync
        def _(sp):
            for s in range(RAW):
                sp.dma_start(raw[:, s, :], stream[s]).then_inc(s_raw[s], 16)
            full = N // RAW

            def load(n, s):
                sp.wait_ge(s_lo, n - RAW + 1)
                sp.dma_start(raw[:, s, :], stream[bass.ds(n, 1)].rearrange("o p c -> p (o c)")
                             if not isinstance(n, int) else stream[n]).then_inc(s_raw[s], 16)

            with sp.Fori(1, full) as i:
                for s in range(RAW):
                    load(i * RAW + s, s)
            for n in range(full * RAW, N):
                load(n, n % RAW)
            sp.wait_ge(s_done, 1)
            sp.dma_start(out.rearrange("(t p) d -> p t d", p=P), resid[:]).then_inc(s_out, 16)
            sp.wait_ge(s_out, 16)

        @block.gpsimd
        def _(pool):
            chain = [0]

            def link(ins):
                chain[0] += 1
                ins.then_inc(s_pc, 1)
                pool.wait_ge(s_pc, chain[0])

            pool.dma_start(resid[:], x.rearrange("(t p) d -> p t d", p=P)).then_inc(s_x, 16)
            pool.dma_start(prm[:], prm_d).then_inc(s_x, 16)
            link(nc.gpsimd.memset(ident[:], 0.0))
            link(nc.gpsimd.affine_select(out=ident[:], in_=ident[:], compare_op=ALU.not_equal, fill=1.0,
                                         base=0, pattern=[[-1, P]], channel_multiplier=1))
            nc.gpsimd.iota(iota[:], pattern=[[1, P]], base=0, channel_multiplier=0,
                           allow_small_or_imprecise_dtypes=True).then_inc(s_const, 1)

            def keep(ap, pattern, base, cm, fill=0.0, last=None):
                ins = nc.gpsimd.affine_select(out=ap, in_=ap, compare_op=ALU.is_ge, fill=fill,
                                              base=base, pattern=pattern, channel_multiplier=cm)
                link(ins)

            def fox_constants():
                link(nc.gpsimd.memset(NU, -1.0))
                keep(NU[:, 0:P], [[1, P]], 0, -1)
                link(nc.gpsimd.memset(MASK, 0.0))
                keep(MASK, [[-1, P]], 0, 1, fill=NEG)

            def linear_constants():
                link(nc.gpsimd.memset(MC, 1.0))
                link(nc.gpsimd.memset(MK, 0.0))
                keep(MC[:, 0, :], [[-1, P]], -1, 1)
                keep(MC[:, 8, :], [[1, P]], 0, -1)
                for l in range(LEVELS):
                    h = 1 << l
                    v = MC[:, 1 + l, :].rearrange("p (b s x) -> p b s x", s=2, x=h)
                    m = MK[:, l, :].rearrange("p (b s x) -> p b s x", s=2, x=h)
                    nb = P // (2 * h)
                    pat = [[2 * h, nb], [1, h]]
                    neg = [[-2 * h, nb], [-1, h]]
                    blk = [[2 * h, nb], [0, h]]
                    nblk = [[-2 * h, nb], [0, h]]
                    keep(v[:, :, 1, :], nblk, -h, 1)
                    keep(v[:, :, 1, :], pat, h, -1)
                    keep(v[:, :, 0, :], neg, -1, 1)
                    keep(v[:, :, 0, :], blk, h - 1, -1)
                    link(nc.gpsimd.memset(m[:, :, 1, :], 1.0))
                    keep(m[:, :, 1, :], nblk, 0, 1)
                    keep(m[:, :, 1, :], blk, h - 1, -1)
                link(nc.gpsimd.affine_select(out=MK[:, 7, :], in_=MK[:, 7, :], compare_op=ALU.not_equal,
                                             fill=1.0, base=0, pattern=[[-1, P]], channel_multiplier=1))

            def decayed_keys(L):
                H_ = HEADS[L["kind"]]
                for u in range(2 * H_):
                    h, tt, g = u // 2, u % 2, L["gu"] + u
                    pool.wait_ge(s_gx, g + 1)
                    if u >= 2:
                        pool.wait_ge(s_gs, g - 1)
                    if u == 0:
                        pool.wait_ge(s_tqa, L["tq"] + (2 if L["kind"] == "gla" else 4))
                    kT = TR[:, H_ + h, tt * P:(tt + 1) * P]
                    if tt == 0:
                        nc.gpsimd.tensor_tensor(KS[:, h % 2, :], EB[:, u % 2, 0, :], kT, ALU.mult)
                    lv = 1 - tt
                    nc.gpsimd.tensor_tensor(KD[:, u % 2, lv:lv + LEVELS, :], EB[:, u % 2, lv:lv + LEVELS, :],
                                            kT.unsqueeze(1).broadcast_to([P, LEVELS, P]),
                                            ALU.mult).then_inc(s_gk, 1)

            for L in PLAN.layers:
                l, kind = L["l"], L["kind"]
                if l:
                    pool.wait_ge(s_used, L["small"])
                pool.dma_start(SK, sk_d[l]).then_inc(s_sk, 16)
                if kind == "gla":
                    pool.dma_start(WUP[0:GLA_RANK + 1, :], wup_d).then_inc(s_wup, 16)
                if kind == "fox":
                    fox_constants()
                else:
                    linear_constants()
                nc.gpsimd.memset(sm[:, 60:61], 0.0).then_inc(s_mc, 1)
                if kind != "fox":
                    decayed_keys(L)
                n0 = L["u"]
                pool.wait_ge(s_lo, n0)
                with pool.Fori(0, HALF // 4) as i:
                    for s in range(4):
                        n = i * 4 + (n0 + s)
                        pool.wait_ge(s_hi, n + 1)
                        pool.wait_ge(s_used, n - LO + 1)
                        nc.gpsimd.tensor_tensor(lo[:, (n0 + s) % LO, :], raw[:, (n0 + s) % RAW, :],
                                                hi[:, (n0 + s) % HI, :], ALU.subtract).then_inc(s_lo, 1)
                for half in range(2):
                    with pool.Fori(0, HALF // 2) as i:
                        for s in range(2):
                            g4 = lambda g: g[:, bass.ds(i * 8 + 4 * s, 4)].unsqueeze(2).broadcast_to([P, 4, HALF])
                            pool.wait_ge(s_eq, i * 2 + (HALF * (2 * l + half) + s + 1))
                            nc.gpsimd.tensor_tensor(ohg[:, s, 0], oh2[:, s], g4(ghi), ALU.mult)
                            nc.gpsimd.tensor_tensor(ohg[:, s, 1], oh2[:, s], g4(glo), ALU.mult).then_inc(s_ohg, 1)

        @block.scalar
        def _(act):
            chain = [0]

            def link(ins):
                chain[0] += 1
                ins.then_inc(s_act, 1)
                act.wait_ge(s_act, chain[0])

            def round_slab(n, base):
                k = base % RAW
                act.wait_ge(s_raw[k], landed(n, base))
                if not (isinstance(n, int) and n < HI):
                    act.wait_ge(s_used, n - HI + 1)
                nc.scalar.copy(hi[:, base % HI, :], raw[:, k, :]).then_inc(s_hi, 1)

            def landed(n, base):
                return 16 * (n // RAW + 1) if isinstance(n, int) else (n + (RAW - base % RAW)) * (16 // RAW)

            def transposed(tau, gain):
                for c in range(DC):
                    act.wait_ge(s_tp, DC * tau + (c | 1) + 1)
                    nc.scalar.activation(xhi[:, c, :], ps[:, c // 2, (c % 2) * SEQ:(c % 2 + 1) * SEQ], ACT.Copy,
                                         scale=1.0 if gain is None else prm[:, gain + c:gain + c + 1]
                                         ).then_inc(s_xhi, 1)

            def root(count, view_out, view_in):
                act.wait_ge(s_ss, count)
                nc.scalar.activation(view_out, view_in, ACT.Sqrt).then_inc(s_sq, 1)

            def evacuate(L, g):
                fn = ACT.Copy
                if L["kind"] == "fox" and g == 3:
                    fn = ACT.Sigmoid
                if L["kind"] == "gla" and g == 2 or L["kind"] == "hgrn" and g == 3:
                    fn = ACT.Silu
                if L["kind"] == "hgrn" and g == 1:
                    fn = ACT.Sigmoid
                act.wait_ge(s_used, L["in"] + DC * (g + 1))
                for tt in range(TT):
                    for nh in range(2):
                        nc.scalar.activation(PR[:, tt, g * D + nh * 512:g * D + (nh + 1) * 512],
                                             ps[:, (g % 2) * 4 + 2 * tt + nh, :], fn).then_inc(s_ev, 1)

            def project_in(L):
                G = GROUPS[L["kind"]]
                for n in range(L["small"] + 2, L["out"] + 2):
                    round_slab(n, n)
                    g, k = divmod(n - L["in"] - 2, DC)
                    if k == 0 and g >= 1:
                        evacuate(L, g - 1)
                evacuate(L, G - 1)

            def fox(L):
                f = L["fox"]
                act.wait_ge(s_da, ab["da"] + 1)
                link(nc.scalar.activation(LFB[0:16, :], LFA[0:16, :], ACT.Exp))
                nc.scalar.activation(LFA[0:16, :], LFB[0:16, :], ACT.Ln, bias=1.0).then_inc(s_ab, 1)
                ab["da"] += 1
                root(ab["ss"] + 1, QR, QS)
                ab["ss"] += 1
                for b in range(4):
                    act.wait_ge(s_tq, 2 * L["tq"] + 5 + b)
                    nc.scalar.activation(TR[:, 8 + 2 * b:10 + 2 * b, :].rearrange("p c t -> p (c t)"),
                                         ps[:, 4 + b, :], ACT.Copy,
                                         scale=prm[:, PRM["kg"] + f:PRM["kg"] + f + 1]).then_inc(s_tqa, 1)
                b0 = FOX_HEADS * f
                for h in range(FOX_HEADS + 1):
                    if h < FOX_HEADS:
                        act.wait_ge(s_mx, b0 + h + 1)
                        if h >= 2:
                            act.wait_ge(s_pt, b0 + h - 1)
                        nc.scalar.activation(PB[:, h % 2, 0:P], ps[:, h % 2, 0:P], ACT.Exp,
                                             bias=NM[:, h, 0:1], accum_out=RSUM[:, h, 0:1])
                        nc.scalar.activation(PB[:, h % 2, P:3 * P], ps[:, h % 2, P:3 * P], ACT.Exp,
                                             bias=NM[:, h, 1:2], accum_out=RSUM[:, h, 1:2]).then_inc(s_exp, 1)
                    if h >= 1:
                        g = h - 1
                        act.wait_ge(s_pt, b0 + g + 1)
                        if g >= 2:
                            act.wait_ge(s_pv, b0 + g - 1)
                        nc.scalar.copy(PTB[:, g % 2, :], ps[:, 2 + g % 2, 0:3 * P]).then_inc(s_pte, 1)

            def linear(L):
                kind, H_ = L["kind"], HEADS[L["kind"]]
                dv = D // H_
                if kind == "gla":
                    act.wait_ge(s_da, ab["da"] + 1)
                    link(nc.scalar.activation(XN[:, :, 0:512], XN[:, :, 0:512], ACT.Exp))
                    nc.scalar.activation(XN[:, :, 512:1024], XN[:, :, 0:512], ACT.Ln, bias=1.0).then_inc(s_ab, 1)
                    ab["da"] += 1
                else:
                    act.wait_ge(s_da, ab["da"] + 3)
                    nc.scalar.activation(LG, SCR2, ACT.Ln).then_inc(s_ab, 1)
                    ab["da"] += 3
                nb = H_ // 2
                for b in range(nb):
                    act.wait_ge(s_tq, 2 * L["tq"] + nb + 1 + b)
                    nc.scalar.activation(TR[:, H_ + 2 * b:H_ + 2 * b + 2, :].rearrange("p c t -> p (c t)"),
                                         ps[:, nb + b, :], ACT.Copy).then_inc(s_tqa, 1)
                U = 2 * H_
                for u in range(U + 2):
                    if u < U:
                        g = L["gu"] + u
                        act.wait_ge(s_gd, g + 1)
                        if u >= 2:
                            act.wait_ge(s_gq, g - 1)
                            act.wait_ge(s_gk, g - 1)
                        nc.scalar.activation(EB[:, u % 2].rearrange("p l t -> p (l t)"),
                                             ps[:, 0:2, :].rearrange("p b c -> p (b c)"), ACT.Exp).then_inc(s_gx, 1)
                    if u >= 2:
                        w = u - 2
                        g, h, tt = L["gu"] + w, w // 2, w % 2
                        act.wait_ge(s_gp, g + 1)
                        o = ps[:, 7, (w % 2) * 256:(w % 2) * 256 + dv]
                        nc.scalar.activation(XN[:, tt, h * dv:(h + 1) * dv], o, ACT.Square,
                                             accum_out=sm[:, 8 + tt * H_ + h:9 + tt * H_ + h])
                        nc.scalar.copy(PR[:, tt, h * dv:(h + 1) * dv], o).then_inc(s_go, 1)
                root(ab["ss"] + 1, sm[:, 40:40 + 2 * H_], sm[:, 24:24 + 2 * H_])
                ab["ss"] += 1

            ab = {"da": 0, "ss": 0}
            act.wait_ge(s_const, 1)
            act.wait_ge(s_x, 32)
            for n in range(2):
                round_slab(n, n)
            for L in PLAN.layers:
                l, kind = L["l"], L["kind"]
                root(ab["ss"] + 1, sm[:, 4:6], sm[:, 2:4])
                ab["ss"] += 1
                transposed(3 * l, PRM["mix"] + DC * l)
                if kind == "hgrn":
                    act.wait_ge(s_da, ab["da"] + 1)
                    nc.scalar.activation(LBC[:, 0:32], LBC[:, 0:32], ACT.Exp).then_inc(s_ab, 1)
                project_in(L)
                if kind == "fox":
                    fox(L)
                else:
                    linear(L)
                transposed(3 * l + 1, None if kind == "fox" else PRM[kind + "_gain"])
                for n in range(L["out"] + 2, L["wq"] + 2):
                    round_slab(n, n)
                root(ab["ss"] + 1, sm[:, 4:6], sm[:, 2:4])
                ab["ss"] += 1
                transposed(3 * l + 2, PRM["ffn"] + DC * l)
                for m in range(PH):
                    for s in range(2):
                        round_slab(L["wq"] + 2 * m + 2 + s, L["wq"] + 2 * m + 2 + s)
                    act.wait_ge(s_used, L["wq"] + 2 * m + 2)
                    nc.scalar.copy(QT[:, 2 * m:2 * m + 2, :].rearrange("p c t -> p (c t)"),
                                   ps[:, 4 + m % 2, :]).then_inc(s_cev, 1)
                n0 = L["u"]

                def u_steps(j0, j1):
                    with act.Fori(j0 // 4, j1 // 4) as i:
                        for s in range(4):
                            round_slab(i * 4 + (n0 + s + 2), n0 + s + 2)
                            if s % 2:
                                act.wait_ge(s_used, i * 4 + (n0 + s + 1))
                                nc.scalar.activation(H[:, bass.ds(i * 4 + (s - 1), 2), :].rearrange(
                                    "p c t -> p (c t)"), ps[:, 4 + s // 2, :], ACT.Gelu).then_inc(s_cev, 1)

                j0 = 0
                for tt in range(TT):
                    u_steps(j0, EXP_AT[tt])
                    j0 = EXP_AT[tt]
                    act.wait_ge(s_ge, TT * l + tt + 1)
                    nc.scalar.activation(EX, BEST, ACT.Exp).then_inc(s_gn, 1)
                u_steps(j0, HALF)
                act.wait_ge(s_hm, (NCH + 2) * l + 2)
                u_steps(HALF, NCH)
                n0 = L["v"]

                def round_w(j, s, wait=True):
                    if wait:
                        act.wait_ge(s_used, j + (n0 - 3))
                    nc.scalar.copy(xhi[:, s, :], chunk(j)).then_inc(s_whi, 1)

                act.wait_ge(s_used, n0)
                for half in range(2):
                    j0 = half * HALF
                    act.wait_ge(s_hm, (NCH + 2) * l + 2 + j0 + HALF)
                    for s in range(2):
                        round_w(j0 + s, s, wait=half == 1)

                    def v_step(i, s, k):
                        n = k + (n0 + j0 + 2)
                        if not isinstance(i, int) or n < N:
                            round_slab(n, n0 + s + 2)
                        if not isinstance(i, int) or i == 0 or s < 2:
                            round_w(k + (j0 + 2), (s + 2) % 4, wait=not (isinstance(i, int) and half == 0 and k < 2))

                    steps(act, HALF, v_step, first=True)

        @block.vector
        def _(dve):
            chain = [0]

            def mark(ins):
                chain[0] += 1
                ins.then_inc(s_dve, 1)

            def join():
                dve.wait_ge(s_dve, chain[0])

            def link(ins):
                mark(ins)
                join()

            def split_slab(n, base):
                dve.wait_ge(s_hi, n + 1)
                if not (isinstance(n, int) and n < LO):
                    dve.wait_ge(s_used, n - LO + 1)
                nc.vector.tensor_tensor(lo[:, base % LO, :], raw[:, base % RAW, :], hi[:, base % HI, :],
                                        ALU.subtract).then_inc(s_lo, 1)

            def transposed(tau, gain):
                for c in range(DC):
                    dve.wait_ge(s_xhi, DC * tau + (c | 1) + 1)
                    nc.vector.scalar_tensor_tensor(
                        out=xlo[:, c, :], in0=ps[:, c // 2, (c % 2) * SEQ:(c % 2 + 1) * SEQ],
                        scalar=1.0 if gain is None else prm[:, gain + c:gain + c + 1], in1=xhi[:, c, :],
                        op0=ALU.mult, op1=ALU.subtract).then_inc(s_xlo, 1)

            def norm():
                for tt in range(TT):
                    mark(nc.vector.tensor_tensor_reduce(
                        out=XN[:, tt, :], in0=resid[:, tt, :], in1=resid[:, tt, :], scale=1.0, scalar=0.0,
                        op0=ALU.mult, op1=ALU.add, accum_out=sm[:, tt:tt + 1]))
                join()
                nc.vector.tensor_scalar(sm[:, 2:4], sm[:, 0:2], 1.0 / D, EPS, ALU.mult, ALU.add).then_inc(s_ss, 1)
                ab["sq"] += 1
                dve.wait_ge(s_sq, ab["sq"])
                link(nc.vector.reciprocal(sm[:, 6:8], sm[:, 4:6]))
                for tt in range(TT):
                    nc.vector.tensor_scalar(XN[:, tt, :], resid[:, tt, :], sm[:, 6 + tt:7 + tt], None,
                                            ALU.mult).then_inc(s_xn, 1)

            def add_residual(n):
                dve.wait_ge(s_used, n)
                for tt in range(TT):
                    for nh in range(2):
                        r = resid[:, tt, nh * 512:(nh + 1) * 512]
                        mark(nc.vector.tensor_tensor(r, ps[:, 2 * tt + nh, :], r, ALU.add))
                join()

            def forget_gates(L):
                bias = prm[0:FOX_HEADS, PRM["bf"] + L["fox"]:PRM["bf"] + L["fox"] + 1]
                dve.wait_ge(s_used, L["small"] + 1)
                link(nc.vector.tensor_scalar(LFT[0:16, :], ps[0:16, 7, 0:SEQ], bias, None, ALU.add))
                nc.vector.scalar_tensor_tensor(out=LFA[0:16, :], in0=LFT[0:16, :], scalar=-1.0, in1=LFT[0:16, :],
                                               op0=ALU.mult, op1=ALU.min).then_inc(s_da, 1)
                ab["da"] += 1

            def fox_core(L):
                f = L["fox"]
                ab["ab"] += 1
                dve.wait_ge(s_ab, ab["ab"])
                nc.vector.scalar_tensor_tensor(out=LFB[0:16, :], in0=LFT[0:16, :], scalar=0.0, in1=LFA[0:16, :],
                                               op0=ALU.min, op1=ALU.subtract).then_inc(s_lf, 1)
                dve.wait_ge(s_ev, L["ev"] + 8)
                for tt in range(TT):
                    link(nc.vector.tensor_tensor(SCR, PR[:, tt, 0:2 * D], PR[:, tt, 0:2 * D], ALU.mult))
                    link(nc.vector.tensor_reduce(QS[:, 32 * tt:32 * tt + 32],
                                                 SCR.rearrange("p (h d) -> p h d", d=FOX_DH), AX.X, ALU.add))
                nc.vector.tensor_scalar(QS, QS, 1.0 / FOX_DH, EPS, ALU.mult, ALU.add).then_inc(s_ss, 1)
                ab["sq"] += 1
                dve.wait_ge(s_sq, ab["sq"])
                link(nc.vector.reciprocal(QR, QR))
                for tt in range(TT):
                    v = PR[:, tt, 0:2 * D].rearrange("p (h d) -> p h d", d=FOX_DH)
                    nc.vector.tensor_tensor(v, v, QR[:, 32 * tt:32 * tt + 32].unsqueeze(2).broadcast_to([P, 32, FOX_DH]),
                                            ALU.mult).then_inc(s_qk, 1)
                dve.wait_ge(s_lft, f + 1)
                nc.vector.tensor_copy(LF, ps[:, 0, 0:32].rearrange("p (t h) -> p t h", t=TT)).then_inc(s_lfc, 1)
                for b in range(4):
                    dve.wait_ge(s_tq, 2 * L["tq"] + 1 + b)
                    nc.vector.tensor_scalar(TR[:, 2 * b:2 * b + 2, :].rearrange("p c t -> p (c t)"), ps[:, b, :],
                                            prm[:, PRM["qg"] + f:PRM["qg"] + f + 1], FOX_DH ** -0.5,
                                            ALU.mult, ALU.mult).then_inc(s_tqd, 1)
                b0 = FOX_HEADS * f
                for h in range(FOX_HEADS + 2):
                    if h < FOX_HEADS:
                        dve.wait_ge(s_s, b0 + h + 1)
                        nc.vector.tensor_reduce(NM[:, h, 0:1], ps[:, h % 2, 0:P], AX.X, ALU.max, negate=True)
                        nc.vector.tensor_reduce(NM[:, h, 1:2], ps[:, h % 2, P:3 * P], AX.X, ALU.max,
                                                negate=True).then_inc(s_mx, 1)
                    if 1 <= h <= FOX_HEADS:
                        dve.wait_ge(s_exp, b0 + h)
                        mark(nc.vector.reciprocal(RL[:, h - 1, :], RSUM[:, h - 1, :]))
                    if h >= 2:
                        g = h - 2
                        dve.wait_ge(s_pv, b0 + g + 1)
                        join()
                        for tt in range(TT):
                            gate = PR[:, tt, 3 * D + g * FOX_DH:3 * D + (g + 1) * FOX_DH]
                            ins = nc.vector.scalar_tensor_tensor(
                                out=gate, in0=ps[:, 4 + g % 2, tt * FOX_DH:(tt + 1) * FOX_DH],
                                scalar=RL[:, g, tt:tt + 1], in1=gate, op0=ALU.mult, op1=ALU.mult)
                        ins.then_inc(s_o, 1)

            def gla_gates(L):
                dve.wait_ge(s_z, 1)
                link(nc.vector.tensor_copy(LG[:, :, 0:512], ps[:, 4:6, :]))
                nc.vector.scalar_tensor_tensor(out=XN[:, :, 0:512], in0=LG[:, :, 0:512], scalar=-1.0,
                                               in1=LG[:, :, 0:512], op0=ALU.mult, op1=ALU.min).then_inc(s_da, 1)
                ab["da"] += 1
                ab["ab"] += 1
                dve.wait_ge(s_ab, ab["ab"])
                link(nc.vector.scalar_tensor_tensor(out=LG[:, :, 0:512], in0=LG[:, :, 0:512], scalar=0.0,
                                                    in1=XN[:, :, 512:1024], op0=ALU.min, op1=ALU.subtract))
                nc.vector.tensor_scalar(LG[:, :, 0:512], LG[:, :, 0:512], 1.0 / GLA_TAU, None,
                                        ALU.mult).then_inc(s_lg, 1)

            def hgrn_bounds():
                i = KIND.index("hgrn")
                lb = prm[:, PRM["lb"]:PRM["lb"] + DEPTH * DC].rearrange("p (r c) -> p r c", c=DC)
                e = LBC[:, 0:32].rearrange("p (r c) -> p r c", c=DC)
                m = LBC[:, 32:40]
                r = LBC[:, 40:48]
                link(nc.vector.tensor_reduce(m, lb.rearrange("p r c -> p c r"), AX.X, ALU.max))
                nc.vector.tensor_tensor(e, lb, m.unsqueeze(1).broadcast_to([P, DEPTH, DC]),
                                        ALU.subtract).then_inc(s_da, 1)
                ab["da"] += 1
                ab["ab"] += 1
                dve.wait_ge(s_ab, ab["ab"])
                link(nc.vector.tensor_reduce(r, e.rearrange("p r c -> p c r"), AX.X, ALU.add))
                link(nc.vector.reciprocal(r, r))
                link(nc.vector.tensor_tensor(e, e, r.unsqueeze(1).broadcast_to([P, DEPTH, DC]), ALU.mult))
                link(nc.vector.tensor_copy(m, e[:, 0, :]))
                for j in range(1, i + 1):
                    link(nc.vector.tensor_tensor(m, m, e[:, j, :], ALU.add))
                nc.vector.tensor_tensor(LBC[:, 48:56], m, e[:, 0, :], ALU.subtract).then_inc(s_lb, 1)

            def hgrn_bound_rows():
                dve.wait_ge(s_lbr, 1)
                nc.vector.tensor_copy(LBR.rearrange("p (b c) -> p b c", b=2), ps[:, 6:8, :]).then_inc(s_lbc, 1)
                nc.vector.tensor_scalar(OML.rearrange("p (b c) -> p b c", b=2), ps[:, 6:8, :], -1.0, 1.0,
                                        ALU.mult, ALU.add).then_inc(s_lbc, 1)
                dve.wait_ge(s_lbc, 2)

            def hgrn_gates(L):
                dve.wait_ge(s_ev, L["ev"] + 8)
                for tt in range(TT):
                    mark(nc.vector.tensor_tensor(SCR2[:, tt, :], PR[:, tt, D:2 * D], OML, ALU.mult))
                join()
                for tt in range(TT):
                    nc.vector.tensor_tensor(SCR2[:, tt, :], SCR2[:, tt, :], LBR, ALU.add).then_inc(s_da, 1)
                    ab["da"] += 1
                ab["ab"] += 1
                dve.wait_ge(s_da, ab["da"])
                nc.vector.tensor_scalar(PR[:, :, D:2 * D], SCR2, -1.0, 1.0, ALU.mult, ALU.add).then_inc(s_hk, 1)

            def linear_core(L):
                kind, H_ = L["kind"], HEADS[L["kind"]]
                dv = D // H_
                for b in range(H_ // 2):
                    dve.wait_ge(s_tq, 2 * L["tq"] + 1 + b)
                    nc.vector.tensor_scalar(TR[:, 2 * b:2 * b + 2, :].rearrange("p c t -> p (c t)"), ps[:, b, :],
                                            float(P) ** -0.5, None, ALU.mult).then_inc(s_tqd, 1)
                dve.wait_ge(s_tqd, L["tq"] + H_ // 2)
                dve.wait_ge(s_mc, L["l"] + 1)
                U = 2 * H_
                for u in range(U + 1):
                    if u < U:
                        g, h, tt = L["gu"] + u, u // 2, u % 2
                        dve.wait_ge(s_gx, g + 1)
                        if u >= 2:
                            dve.wait_ge(s_gs, g - 1)
                        lv, n = (1, LEVELS) if tt == 0 else (0, LEVELS + 1)
                        nc.vector.tensor_tensor(
                            QD[:, u % 2, lv:lv + n, :], EB[:, u % 2, lv:lv + n, :],
                            TR[:, h, tt * P:(tt + 1) * P].unsqueeze(1).broadcast_to([P, n, P]),
                            ALU.mult).then_inc(s_gq, 1)
                    if u >= 1:
                        w = u - 1
                        g, h, tt = L["gu"] + w, w // 2, w % 2
                        dve.wait_ge(s_gs, g + 1)
                        if g:
                            dve.wait_ge(s_gr, g)
                        b = 2 + 2 * (w % 2)
                        nc.vector.tensor_tensor(AM.rearrange("p l t -> p (l t)"),
                                                ps[:, b:b + 2, :].rearrange("p b c -> p (b c)"),
                                                MK.rearrange("p l t -> p (l t)"), ALU.mult).then_inc(s_gm, 1)
                        dve.wait_ge(s_gm, g + 1)
                        if w >= 2:
                            dve.wait_ge(s_gp, g - 1)
                        ins = nc.vector.tensor_reduce(ST[:, w % 2, :], AM.rearrange("p l t -> p t l"), AX.X, ALU.add)
                        if tt == 1:
                            mark(ins)
                            ins = nc.vector.tensor_copy(ST[:, 2 + h % 2, :], ps[:, 6, (h % 2) * P:(h % 2 + 1) * P])
                            join()
                        ins.then_inc(s_gr, 1)
                dve.wait_ge(s_go, L["gu"] + U)
                nc.vector.tensor_scalar(sm[:, 24:24 + U], sm[:, 8:8 + U], 1.0 / dv, EPS, ALU.mult, ALU.add
                                        ).then_inc(s_ss, 1)
                ab["sq"] += 1
                dve.wait_ge(s_sq, ab["sq"])
                link(nc.vector.reciprocal(sm[:, 40:40 + U], sm[:, 40:40 + U]))
                gg = (GROUPS[kind] - 1) * D
                for tt in range(TT):
                    for h in range(H_):
                        ins = nc.vector.scalar_tensor_tensor(
                            out=XN[:, tt, h * dv:(h + 1) * dv], in0=PR[:, tt, h * dv:(h + 1) * dv],
                            scalar=sm[:, 40 + tt * H_ + h:41 + tt * H_ + h],
                            in1=PR[:, tt, gg + h * dv:gg + (h + 1) * dv], op0=ALU.mult, op1=ALU.mult)
                        if h < H_ - 1:
                            mark(ins)
                    ins.then_inc(s_xn, 1)
                join()

            def top16(src, tmp, val, idx, batch):
                for c in batch:
                    mark(nc.vector.max(val[:, c, 0:8], src(c)))
                join()
                for c in batch:
                    mark(nc.vector.max_index(idx[:, c, 0:8].bitcast(U32), val[:, c, 0:8], src(c)))
                    mark(nc.vector.match_replace(tmp(c), val[:, c, 0:8], src(c), NEG))
                join()
                for c in batch:
                    mark(nc.vector.max(val[:, c, 8:16], tmp(c)))
                join()
                for c in batch:
                    mark(nc.vector.max_index(idx[:, c, 8:16].bitcast(U32), val[:, c, 8:16], tmp(c)))

            def route(L, tt):
                l = L["l"]
                for b in range(4):
                    dve.wait_ge(s_sc, 8 * l + 4 * tt + b + 1)
                    top16(lambda c: ps[:, c // 4, (c % 4) * NK:(c % 4 + 1) * NK], lambda c: TMP[:, c, :],
                          VAL, IDX, range(4 * b, 4 * b + 4))
                join()
                mark(nc.vector.tensor_copy(IDF, IDX.bitcast(U32)))
                v = VAL.rearrange("p (h s) k -> p h s k", s=2)
                cand = CAND.rearrange("p (h a b) -> p h a b", h=PH, a=TOPK)
                nc.vector.tensor_tensor(cand, v[:, :, 0, :].unsqueeze(3).broadcast_to([P, PH, TOPK, TOPK]),
                                        v[:, :, 1, :].unsqueeze(2).broadcast_to([P, PH, TOPK, TOPK]),
                                        ALU.add).then_inc(s_rt, 1)
                dve.wait_ge(s_rt, TT * l + tt + 1)
                ch = CAND.rearrange("p (h c) -> p h c", h=PH)
                eh = EQ.rearrange("p (h c) -> p h c", h=PH)
                for b in range(2):
                    top16(lambda c: ch[:, c, :], lambda c: eh[:, c, :], BEST, POS, range(4 * b, 4 * b + 4))
                join()
                mark(nc.vector.tensor_scalar(PAB[:, 0, :].bitcast(U32), POS.rearrange("p h k -> p (h k)").bitcast(U32),
                                             4, None, ALU.logical_shift_right))
                mark(nc.vector.tensor_scalar(PAB[:, 1, :].bitcast(U32), POS.rearrange("p h k -> p (h k)").bitcast(U32),
                                             15, None, ALU.bitwise_and))
                mark(nc.vector.tensor_copy(ZS[:, 0:8].unsqueeze(2), BEST[:, :, 0:1]))
                join()
                nc.vector.tensor_tensor(BEST, BEST, ZS[:, 0:8].unsqueeze(2).broadcast_to([P, PH, TOPK]),
                                        ALU.subtract).then_inc(s_ge, 1)
                link(nc.vector.tensor_copy(PAF, PAB.bitcast(U32)))
                ix = IDF.rearrange("p (h s) k -> p h s k", s=2)
                eq = EQ.rearrange("p (c a) -> p c a", a=TOPK)
                for side in range(2):
                    link(nc.vector.tensor_tensor(eq, PAF[:, side, :].unsqueeze(2).broadcast_to([P, P, TOPK]),
                                                 iota[:, 0:TOPK].unsqueeze(1).broadcast_to([P, P, TOPK]), ALU.is_equal))
                    e4 = EQ.rearrange("p (h k a) -> p h k a", h=PH, a=TOPK)
                    link(nc.vector.tensor_tensor(e4, e4, ix[:, :, side, :].unsqueeze(2).broadcast_to([P, PH, TOPK, TOPK]),
                                                 ALU.mult))
                    link(nc.vector.tensor_reduce(ROUT[tt][:, side, :], eq, AX.X, ALU.add))
                dve.wait_ge(s_gn, TT * l + tt + 1)
                link(nc.vector.tensor_reduce(ZS[:, 8:16], EX, AX.X, ALU.add))
                link(nc.vector.reciprocal(ZS[:, 8:16], ZS[:, 8:16]))
                nc.vector.tensor_tensor(ROUT[tt][:, 2, :].rearrange("p (h k) -> p h k", k=TOPK), EX,
                                        ZS[:, 8:16].unsqueeze(2).broadcast_to([P, PH, TOPK]),
                                        ALU.mult).then_inc(s_route, 1)
                dve.wait_ge(s_route, TT * l + tt + 1)

            def split_w(k, n, s):
                dve.wait_ge(s_whi, n)
                nc.vector.tensor_tensor(xlo[:, s, :], chunk(k), xhi[:, s, :], ALU.subtract).then_inc(s_wlo, 1)

            def one_hots(i, s, half, at):
                t0 = i * 16 + 4 * s
                tok = lambda e, w: e[:, bass.ds(t0, 4)].unsqueeze(2).broadcast_to([P, 4, w])
                dve.wait_ge(s_g, i * 4 + (at + s + 1))
                nc.vector.tensor_tensor(oh1[:, s % 2], iota[:].unsqueeze(1).broadcast_to([P, 4, P]),
                                        tok(e1T, P), ALU.is_equal)
                nc.vector.tensor_tensor(oh2[:, s % 2],
                                        iota[:, half * HALF:(half + 1) * HALF].unsqueeze(1).broadcast_to([P, 4, HALF]),
                                        tok(e2T, HALF), ALU.is_equal).then_inc(s_eq, 1)

            def weigh(i, s, half, at):
                dve.wait_ge(s_g, i * 4 + (at + s + 3))
                v = H[:, half * HALF:(half + 1) * HALF, bass.ds(i * 16 + 4 * s, 4)]
                nc.vector.tensor_tensor(v, ps[:, 6 + s % 2, 0:4 * HALF].rearrange("p (t j) -> p j t", t=4), v,
                                        ALU.mult).then_inc(s_hm, 1)

            ab = {"ab": 0, "sq": 0, "da": 0}
            dve.wait_ge(s_x, 32)
            dve.wait_ge(s_const, 1)
            for L in PLAN.layers:
                l, kind = L["l"], L["kind"]
                norm()
                transposed(3 * l, PRM["mix"] + DC * l)
                if kind == "hgrn":
                    hgrn_bounds()
                if kind == "gla":
                    nc.vector.memset(LOWT[0:32, :], 1.0).then_inc(s_low, 1)
                for n in range(L["small"], L["in"] + 1):
                    split_slab(n, n)
                if kind == "fox":
                    forget_gates(L)
                elif kind == "gla":
                    dve.wait_ge(s_used, L["small"] + 1)
                    dve.wait_ge(s_low, 1)
                    nc.vector.tensor_copy(LOWT[0:GLA_RANK, :], ps[0:GLA_RANK, 7, 0:SEQ]).then_inc(s_low, 1)
                else:
                    hgrn_bound_rows()
                for n in range(L["in"] + 1, L["out"]):
                    split_slab(n, n)
                if kind == "fox":
                    fox_core(L)
                else:
                    if kind == "gla":
                        gla_gates(L)
                    else:
                        hgrn_gates(L)
                    linear_core(L)
                transposed(3 * l + 1, None if kind == "fox" else PRM[kind + "_gain"])
                for n in range(L["out"], L["wq"]):
                    split_slab(n, n)
                add_residual(L["wq"])
                norm()
                transposed(3 * l + 2, PRM["ffn"] + DC * l)
                for n in range(L["wq"], L["u"]):
                    split_slab(n, n)
                for tt in range(TT):
                    route(L, tt)
                g0 = (NCH + 2) * l
                dve.wait_ge(s_g, g0 + 2)
                mark(nc.vector.tensor_copy(e1T[:], ps[:, 6, 0:SEQ]))
                mark(nc.vector.tensor_copy(ghi[:], ps[:, 7, 0:SEQ]))
                nc.vector.tensor_copy(e2T[:], ps[:, 6, SEQ:2 * SEQ]).then_inc(s_hm, 1)
                join()
                nc.vector.tensor_tensor(glo[:], ps[:, 7, 0:SEQ], ghi[:], ALU.subtract).then_inc(s_hm, 1)
                dve.wait_ge(s_hm, g0 + 2)
                dve.wait_ge(s_lo, L["u"] + HALF)
                for half in range(2):
                    n0 = (L["u"] + HALF, L["v"])[half]
                    at = g0 + half * HALF
                    if half == 0:
                        split_slab(n0, n0)
                    else:
                        split_w(0, NCH * l + 1, 0)
                    one_hots(0, 0, half, at)
                    dve.wait_ge(s_cev, (PH + HALF) * l + PH + HALF // 2 * (half + 1))

                    def g_step(i, s, k):
                        last = isinstance(k, int) and k == HALF - 1
                        split_slab(k + (n0 + 1), n0 + s + 1)
                        if half == 1 and not last:
                            split_w(k + 1, k + (NCH * l + 2), (s + 1) % 4)
                        if not last:
                            if s < 3:
                                one_hots(i, s + 1, half, at)
                            else:
                                one_hots(i + 1, 0, half, at)
                        weigh(i, s, half, at)

                    steps(dve, HALF, g_step)
                n0 = L["v"] + HALF
                split_w(HALF, NCH * l + HALF + 1, 0)

                def v_step(i, s, k):
                    if not (isinstance(k, int) and k == HALF - 1):
                        split_slab(k + (n0 + 1), n0 + s + 1)
                        split_w(k + (HALF + 1), k + (NCH * l + HALF + 2), (s + 1) % 4)

                steps(dve, HALF, v_step)
                add_residual(L["end"])
            nc.vector.tensor_copy(sm[:, 62:63], sm[:, 60:61]).then_inc(s_done, 1)

        @block.tensor
        def _(pe):
            def product(out_, lh, ll, rh, rl, start, stop):
                nc.tensor.matmul(out_, lh, rh, start=start, stop=False)
                nc.tensor.matmul(out_, lh, rl, start=False, stop=False)
                return nc.tensor.matmul(out_, ll, rh, start=False, stop=stop)

            def row_step(n, base, c, bank, start, stop):
                pe.wait_ge(s_lo, n + 1)
                for tt in range(TT):
                    t = slice(tt * P, (tt + 1) * P)
                    for nh in range(2):
                        w = slice(nh * 512, (nh + 1) * 512)
                        ins = product(ps[:, bank + 2 * tt + nh, :], xhi[:, c, t], xlo[:, c, t],
                                      hi[:, base % HI, w], lo[:, base % LO, w], start, stop)
                ins.then_inc(s_used, 1)

            def col_step(n, base, out_):
                pe.wait_ge(s_lo, n + 1)
                for c in range(DC):
                    w = slice(c * P, (c + 1) * P)
                    ins = product(out_, hi[:, base % HI, w], lo[:, base % LO, w], xhi[:, c, :], xlo[:, c, :],
                                  c == 0, c == DC - 1)
                ins.then_inc(s_used, 1)

            def transposed(tau, src):
                for c in range(DC):
                    for tt in range(TT):
                        o = (c % 2) * SEQ + tt * P
                        ins = nc.tensor.transpose(ps[:, c // 2, o:o + P], src(tt)[:, c * P:(c + 1) * P], ident[:])
                    ins.then_inc(s_tp, 1)
                pe.wait_ge(s_xlo, DC * (tau + 1))

            def norm_transposed(tau):
                xn["n"] += 2
                pe.wait_ge(s_xn, xn["n"])
                transposed(tau, lambda tt: XN[:, tt, :])

            def project_in(L):
                for n in range(L["small"], L["in"]):
                    col_step(n, n, ps[:, 7, 0:SEQ])
                if L["kind"] == "hgrn":
                    pe.wait_ge(s_lb, 1)
                    for c in range(DC):
                        ins = nc.tensor.matmul(ps[:, 6 + c // 4, (c % 4) * P:(c % 4 + 1) * P],
                                               LBC[:, 48 + c:49 + c].broadcast_to([P, P]), ident[:],
                                               start=True, stop=True)
                    ins.then_inc(s_lbr, 1)
                for g in range(GROUPS[L["kind"]]):
                    if g == 1:
                        if L["kind"] == "fox":
                            pe.wait_ge(s_da, HANDED[L["l"]][0] + 1)
                        elif L["kind"] == "gla":
                            pe.wait_ge(s_low, 2)
                        else:
                            pe.wait_ge(s_lbc, 2)
                    if g >= 2:
                        pe.wait_ge(s_ev, L["ev"] + 4 * (g - 1))
                    for c in range(DC):
                        n = L["in"] + g * DC + c
                        row_step(n, n, c, (g % 2) * 4, c == 0, c == DC - 1)

            def chunks_transposed(L, n):
                for b in range(n):
                    for c in (2 * b, 2 * b + 1):
                        for tt in range(TT):
                            o = (c % 2) * SEQ + tt * P
                            ins = nc.tensor.transpose(ps[:, b, o:o + P], PR[:, tt, c * P:(c + 1) * P], ident[:])
                    ins.then_inc(s_tq, 1)
                pe.wait_ge(s_tqd, L["tq"] + n // 2)
                pe.wait_ge(s_tqa, L["tq"] + n // 2)

            def fox(L):
                f = L["fox"]
                b0 = FOX_HEADS * f
                pe.wait_ge(s_ev, L["ev"] + 16)
                pe.wait_ge(s_lf, f + 1)
                for tt in range(TT):
                    ins = nc.tensor.transpose(ps[:, 0, 16 * tt:16 * tt + 16], LFB[0:16, tt * P:(tt + 1) * P],
                                              ident[0:16, 0:16])
                ins.then_inc(s_lft, 1)
                pe.wait_ge(s_qk, 2 * (f + 1))
                pe.wait_ge(s_lfc, f + 1)
                chunks_transposed(L, 8)
                pe.wait_ge(s_mc, L["l"] + 1)

                def logits(h):
                    if h >= 2:
                        pe.wait_ge(s_exp, b0 + h - 1)
                    c, r = h // 2, slice(64 * (h % 2), 64 * (h % 2) + 64)
                    s0, s1 = ps[:, h % 2, 0:P], ps[:, h % 2, P:3 * P]
                    gate = lambda tt: LF[:, tt, h:h + 1].broadcast_to([P, P])
                    nc.tensor.matmul(s0, TR[r, c, 0:P], TR[r, 8 + c, 0:P], start=True, stop=False)
                    nc.tensor.matmul(s0, gate(0), NU[:, 0:P], start=False, stop=False)
                    nc.tensor.matmul(s0, ident[:], MASK, start=False, stop=True)
                    nc.tensor.matmul(s1, TR[r, c, P:2 * P], TR[r, 8 + c, :], start=True, stop=False)
                    nc.tensor.matmul(s1, gate(0), NU, start=False, stop=False)
                    nc.tensor.matmul(s1[:, P:2 * P], gate(1), NU[:, 0:P], start=False, stop=False)
                    nc.tensor.matmul(s1[:, P:2 * P], ident[:], MASK, start=False, stop=True).then_inc(s_s, 1)

                logits(0)
                for h in range(FOX_HEADS + 1):
                    if h + 1 < FOX_HEADS:
                        logits(h + 1)
                    if h < FOX_HEADS:
                        pe.wait_ge(s_exp, b0 + h + 1)
                        if h >= 2:
                            pe.wait_ge(s_pte, b0 + h - 1)
                        for b in range(3):
                            ins = nc.tensor.transpose(ps[:, 2 + h % 2, b * P:(b + 1) * P],
                                                      PB[:, h % 2, b * P:(b + 1) * P], ident[:])
                        ins.then_inc(s_pt, 1)
                    if h >= 1:
                        g = h - 1
                        pe.wait_ge(s_pte, b0 + g + 1)
                        if g >= 2:
                            pe.wait_ge(s_o, b0 + g - 1)
                        v = lambda tt: PR[:, tt, 2 * D + g * FOX_DH:2 * D + (g + 1) * FOX_DH]
                        o = ps[:, 4 + g % 2, 0:2 * FOX_DH]
                        pt = lambda b: PTB[:, g % 2, b * P:(b + 1) * P]
                        nc.tensor.matmul(o[:, 0:FOX_DH], pt(0), v(0), start=True, stop=True)
                        nc.tensor.matmul(o[:, FOX_DH:], pt(1), v(0), start=True, stop=False)
                        nc.tensor.matmul(o[:, FOX_DH:], pt(2), v(1), start=False, stop=True).then_inc(s_pv, 1)
                pe.wait_ge(s_o, b0 + FOX_HEADS)
                transposed(3 * L["l"] + 1, lambda tt: PR[:, tt, 3 * D:4 * D])

            def linear(L):
                kind, H_ = L["kind"], HEADS[L["kind"]]
                dv = D // H_
                pe.wait_ge(s_ev, L["ev"] + 4 * GROUPS[kind])
                if kind == "gla":
                    pe.wait_ge(s_wup, 16)
                    for tt in range(TT):
                        ins = nc.tensor.matmul(ps[:, 4 + tt, :], LOWT[0:GLA_RANK + 1, tt * P:(tt + 1) * P],
                                               WUP[0:GLA_RANK + 1, :], start=True, stop=True)
                    ins.then_inc(s_z, 1)
                else:
                    pe.wait_ge(s_hk, 1)
                chunks_transposed(L, H_)
                pe.wait_ge(s_mc, L["l"] + 1)
                if kind == "gla":
                    pe.wait_ge(s_lg, 1)
                else:
                    pe.wait_ge(s_ab, HANDED[L["l"]][1] + 2)
                vg = (GROUPS[kind] - 2) * D
                U = 2 * H_

                def decays(u):
                    g, h, tt = L["gu"] + u, u // 2, u % 2
                    if u >= 1:
                        pe.wait_ge(s_gx, g)
                    for b in range(2):
                        ins = nc.tensor.matmul(ps[:, b, :], LG[:, tt, h * P:(h + 1) * P],
                                               MC[:, tt + 4 * b:tt + 4 * b + 4, :], start=True, stop=True)
                    ins.then_inc(s_gd, 1)

                def scores(u):
                    g, h, tt = L["gu"] + u, u // 2, u % 2
                    lv = 1 - tt
                    pe.wait_ge(s_gq, g + 1)
                    pe.wait_ge(s_gk, g + 1)
                    if u >= 2:
                        pe.wait_ge(s_gr, g - 1)
                    b = 2 + 2 * (u % 2)
                    if tt == 1:
                        nc.tensor.matmul(ps[:, 6, (h % 2) * P:(h % 2 + 1) * P], KS[:, h % 2, :],
                                         QD[:, 1, LEVELS, :], start=True, stop=True)
                    for l in range(LEVELS):
                        nc.tensor.matmul(ps[:, b + l // 4, (l % 4) * P:(l % 4 + 1) * P], KD[:, u % 2, lv + l, :],
                                         QD[:, u % 2, lv + l, :], start=True, stop=True)
                    t = slice(tt * P, (tt + 1) * P)
                    nc.tensor.matmul(ps[:, b + 1, 3 * P:4 * P], TR[:, H_ + h, t], TR[:, h, t],
                                     start=True, stop=True).then_inc(s_gs, 1)

                def values(u):
                    g, h, tt = L["gu"] + u, u // 2, u % 2
                    pe.wait_ge(s_gr, g + 1)
                    if u >= 1:
                        pe.wait_ge(s_go, g)
                    o = ps[:, 7, (u % 2) * 256:(u % 2) * 256 + dv]
                    v = lambda t: PR[:, t, vg + h * dv:vg + (h + 1) * dv]
                    ins = nc.tensor.matmul(o, ST[:, u % 2, :], v(tt), start=True, stop=tt == 0)
                    if tt == 1:
                        ins = nc.tensor.matmul(o, ST[:, 2 + h % 2, :], v(0), start=False, stop=True)
                    ins.then_inc(s_gp, 1)

                decays(0)
                for u in range(U + 1):
                    if u + 1 < U:
                        decays(u + 1)
                    if u < U:
                        scores(u)
                    if u >= 1:
                        values(u - 1)
                norm_transposed(3 * L["l"] + 1)

            def key_scores(L, tt):
                for b in range(4):
                    for q in range(4):
                        c = 4 * b + q
                        ins = nc.tensor.matmul(ps[:, b, q * NK:(q + 1) * NK], QT[:, c, tt * P:(tt + 1) * P],
                                               SK[:, c * NK:(c + 1) * NK], start=True, stop=True)
                    ins.then_inc(s_sc, 1)

            def g_product(i, s, oh, at):
                pe.wait_ge(s_ohg, i * 4 + (oh + s + 1))
                pe.wait_ge(s_hm, i * 4 + (at + s + 1))
                for t in range(4):
                    o = ps[:, 6 + s % 2, t * HALF:(t + 1) * HALF]
                    nc.tensor.matmul(o, oh1[:, s % 2, t, :], ohg[:, s % 2, 0, t, :], start=True, stop=False)
                    ins = nc.tensor.matmul(o, oh1[:, s % 2, t, :], ohg[:, s % 2, 1, t, :], start=False, stop=True)
                ins.then_inc(s_g, 1)

            xn = {"n": 0}
            for L in PLAN.layers:
                l, kind = L["l"], L["kind"]
                norm_transposed(3 * l)
                project_in(L)
                if kind == "fox":
                    fox(L)
                else:
                    linear(L)
                for c in range(DC):
                    row_step(L["out"] + c, L["out"] + c, c, 0, c == 0, c == DC - 1)
                norm_transposed(3 * l + 2)
                c0 = (PH + HALF) * l
                for c in range(2 * PH):
                    if c % 2 == 0 and c >= 4:
                        pe.wait_ge(s_cev, c0 + c // 2 - 1)
                    n = L["wq"] + c
                    col_step(n, n, ps[:, 4 + c // 2 % 2, (c % 2) * SEQ:(c % 2 + 1) * SEQ])
                pe.wait_ge(s_cev, c0 + PH)
                pe.wait_ge(s_sk, 16 * (l + 1))
                key_scores(L, 0)
                n0 = L["u"]
                c0 += PH

                def u_steps(j0, j1, with_g=False):
                    with pe.Fori(j0 // 4, j1 // 4) as i:
                        for s in range(4):
                            if s % 2 == 0:
                                pe.wait_ge(s_cev, i * 2 + (c0 + s // 2 - 1))
                            col_step(i * 4 + (n0 + s), n0 + s, ps[:, 4 + s // 2, (s % 2) * SEQ:(s % 2 + 1) * SEQ])
                            if with_g:
                                g_product(i, s, NCH * l - HALF, (NCH + 2) * l - HALF)

                u_steps(0, SCORES_AT)
                pe.wait_ge(s_rt, TT * l + 1)
                key_scores(L, 1)
                u_steps(SCORES_AT, HALF)
                pe.wait_ge(s_route, TT * (l + 1))
                for w in range(3):
                    for tt in range(TT):
                        o = (w % 2) * SEQ + tt * P
                        ins = nc.tensor.transpose(ps[:, 6 + w // 2, o:o + P], ROUT[tt][:, w, :], ident[:])
                    if w:
                        ins.then_inc(s_g, 1)
                u_steps(HALF, NCH, with_g=True)
                for half in range(2):
                    n0 = L["v"] + half * HALF

                    def v_step(i, s, k):
                        pe.wait_ge(s_wlo, k + (NCH * l + half * HALF + 1))
                        row_step(k + n0, n0 + s, s, 0, isinstance(k, int) and half == 0 and k == 0,
                                 isinstance(k, int) and half == 1 and k == HALF - 1)
                        if half == 0:
                            g_product(i, s, NCH * l + HALF, (NCH + 2) * l + HALF)

                    steps(pe, HALF, v_step, first=half == 0)


def slabs_of_rows(w):
    n = w.shape[1] // D
    return w.reshape(DC, P, n, D).transpose(2, 0, 1, 3).reshape(n * DC, P, D)


def slabs_of_columns(w):
    n = w.shape[1] // P
    return w.reshape(DC, P, n, P).transpose(2, 1, 0, 3).reshape(n, P, D)


def narrow_slab(w):
    return slabs_of_columns(np.concatenate([w, np.zeros((D, P - w.shape[1]), w.dtype)], axis=1))


def kernel(x, norm_mix, norm_ffn, fox_w_in, fox_b_f, fox_q_gain, fox_k_gain, fox_w_out,
           gla_w_in, gla_w_up, gla_b_alpha, gla_out_gain, gla_w_out,
           hgrn_w_in, hgrn_lb_logits, hgrn_out_gain, hgrn_w_out,
           peer_w_q, peer_sub_keys, peer_u, peer_v):
    import concourse.bacc as bacc
    from concourse.bass_utils import run_bass_kernel_spmd

    stream = np.empty((PLAN.slabs, P, D), np.float32)

    def put(n, slabs):
        stream[n:n + len(slabs)] = slabs

    w_in = {"fox": fox_w_in, "gla": gla_w_in, "hgrn": hgrn_w_in}
    w_out = {"fox": fox_w_out, "gla": gla_w_out, "hgrn": hgrn_w_out}
    for L in PLAN.layers:
        l, kind = L["l"], L["kind"]
        which = L["fox"] if kind == "fox" else 0
        wi, wo = np.asarray(w_in[kind][which]), np.asarray(w_out[kind][which])
        wide = GROUPS[kind] * D
        if SMALL[kind]:
            put(L["small"], narrow_slab(wi[:, wide:]))
        put(L["in"], slabs_of_rows(wi[:, :wide]))
        put(L["out"], slabs_of_rows(wo))
        put(L["wq"], slabs_of_columns(np.asarray(peer_w_q[l])))
        u = np.asarray(peer_u[l]).reshape(P, NCH, DC, P)
        put(L["u"], u.transpose(1, 3, 2, 0).reshape(NCH, P, D))
        put(L["v"], np.asarray(peer_v[l]).reshape(P, NCH, D).transpose(1, 0, 2))

    def columns(a):
        return np.asarray(a).reshape(-1, DC, P).transpose(2, 0, 1).reshape(P, -1)

    prm = np.zeros((P, NPRM), np.float32)
    for name, a in (("mix", norm_mix), ("ffn", norm_ffn), ("gla_gain", gla_out_gain), ("hgrn_gain", hgrn_out_gain),
                    ("lb", hgrn_lb_logits)):
        c = columns(a)
        prm[:, PRM[name]:PRM[name] + c.shape[1]] = c
    for name, a in (("qg", fox_q_gain), ("kg", fox_k_gain)):
        a = np.asarray(a)
        prm[:, PRM[name]:PRM[name] + 2] = np.concatenate([a, a], axis=1).T
    prm[0:FOX_HEADS, PRM["bf"]:PRM["bf"] + 2] = np.asarray(fox_b_f).T
    wup = np.concatenate([np.asarray(gla_w_up[0]), np.asarray(gla_b_alpha)], axis=0)
    sk = np.asarray(peer_sub_keys).transpose(0, 4, 1, 2, 3).reshape(DEPTH, P, 2 * PH * NK)

    nc = bacc.Bacc("TRN2", target_bir_lowering=False, num_devices=1)
    arrays = {"stream": stream, "x": np.asarray(x).reshape(SEQ, D), "prm": prm, "wup": wup, "sk": sk}
    aps = {k: nc.dram_tensor(f"in_{k}", a.shape, F32, kind="ExternalInput").ap() for k, a in arrays.items()}
    out = nc.dram_tensor("out_0", (SEQ, D), F32, kind="ExternalOutput").ap()
    build(nc, aps["stream"], aps["x"], aps["prm"], aps["wup"], aps["sk"], out)
    r = run_bass_kernel_spmd(nc, [{f"in_{k}": np.ascontiguousarray(a) for k, a in arrays.items()}], core_ids=[0])
    return r.results[0]["out_0"].reshape(1, SEQ, D)
```

```python
from contextlib import ExitStack

import numpy as np

import concourse.bass as bass
from concourse import mybir

ALU = mybir.AluOpType
ACT = mybir.ActivationFunctionType
F32 = mybir.dt.float32
F32R = mybir.dt.float32r
U32 = mybir.dt.uint32
BF16 = mybir.dt.bfloat16
F16 = mybir.dt.float16
AX = mybir.AxisListType

P = 128
D = 1024
SEQ = 256
TT = SEQ // P
DC = D // P
DEPTH = 4
EPS = 1e-6
NEG = -1e30
FOX_HEADS, FOX_DH = 16, 64
GLA_HEADS, GLA_DK, GLA_RANK, GLA_TAU = 4, 128, 16, 16.0
HGRN_HEADS = 8
PH, NK, TOPK = 8, 128, 16
GATE_SCALE = 2.0 ** 14
NCH = NK
HALF = NCH // 2
LEVELS = 7

RAW, HI, LO = 4, 4, 2

SCORES_AT = 24
EXP_AT = [28, 60]

KIND = ["fox", "gla", "hgrn", "fox"]
GROUPS = {"fox": 4, "gla": 3, "hgrn": 4}
SMALL = {"fox": 1, "gla": 1, "hgrn": 0}
HEADS = {"fox": FOX_HEADS, "gla": GLA_HEADS, "hgrn": HGRN_HEADS}


HANDED = [(0, 0), (1, 1), (2, 2), (5, 5)]
BANKS = (4, 0)


class Plan:

    def __init__(self):
        self.layers = []
        n = ev = tq = gu = 0
        fox = small = 0
        for l, kind in enumerate(KIND):
            L = {"l": l, "kind": kind, "ev": ev, "tq": tq, "gu": gu, "fox": fox, "smallno": small}
            L["small"] = n
            n += SMALL[kind]
            L["in"] = n
            n += GROUPS[kind] * DC
            L["out"] = n
            n += DC
            L["wq"] = n
            n += 2 * PH
            L["u"] = n
            n += NCH
            L["v"] = n
            n += NCH
            L["end"] = n
            ev += 4 * GROUPS[kind]
            tq += 2 if kind == "gla" else 4
            if kind == "fox":
                fox += 1
            else:
                gu += 2 * HEADS[kind]
            small += SMALL[kind]
            self.layers.append(L)
        self.slabs = n


PLAN = Plan()

PRM = {}
_at = 0
for _name, _w in (("mix", DEPTH * DC), ("ffn", DEPTH * DC), ("gla_gain", DC), ("hgrn_gain", DC),
                  ("qg", 2), ("kg", 2), ("bf", 2), ("lb", DEPTH * DC)):
    PRM[_name] = _at
    _at += _w
NPRM = _at

O_P = 0
O_T = 8192
O_XN = 12288
O_LG = 14336
O_MC = 16384
O_MK = O_MC + 9 * P
O_ST = O_MK + 8 * P
O_SK = 20480
O_E = 22528
O_QD = 24576
O_KD = 26624
O_A = 28672
O_KS = 29696
O_SM = 30720
O_WUP = 32256
O_QT = 16384
O_CAND = 22528
O_EQ = 24576
O_TMP = 26624
O_RS = 28672


def build(nc, stream, x, prm_d, wup_d, sk_d, out):
    N = PLAN.slabs
    with ExitStack() as ctx:
        def sb(name, shape, dt=F32):
            return ctx.enter_context(nc.sbuf_tensor(name, shape, dt))

        def sem(name):
            return ctx.enter_context(nc.semaphore(name))

        resid = sb("resid", [P, TT, D])
        xhi = sb("xhi", [P, DC, SEQ], F32R)
        xlo = sb("xlo", [P, DC, SEQ], F32R)
        big = sb("big", [P, NCH * SEQ])
        raw = sb("raw", [P, RAW, D])
        hi = sb("hi", [P, HI, D], F32R)
        lo = sb("lo", [P, LO, D], F32R)
        ident = sb("ident", [P, P])
        iota = sb("iota", [P, P])
        prm = sb("prm", [P, NPRM])
        e1T = sb("e1T", [P, SEQ])
        e2T = sb("e2T", [P, SEQ])
        gate2 = sb("gate2", [P, 2, SEQ], F16)
        oh1 = sb("oh1", [P, 2, 4, P], F16)
        oh2 = sb("oh2", [P, 2, 4, HALF], F16)
        ohg = sb("ohg", [P, 2, 2, 4, HALF], F16)
        nur = sb("nur", [P, 2 * P], F32R)
        maskb = sb("maskb", [P, P], BF16)
        identb = sb("identb", [P, P], BF16)
        lfh = sb("lfh", [P, TT, FOX_HEADS], F32R)
        lfl = sb("lfl", [P, TT, FOX_HEADS], F32R)
        minus_half = sb("minus_half", [P, 64])
        sm = sb("sm", [P, 64])
        ps = ctx.enter_context(nc.psum_tensor("ps", [P, 8, 512], F32))

        s_raw = [sem(f"s_raw{i}") for i in range(RAW)]
        s_hi, s_lo, s_used = sem("s_hi"), sem("s_lo"), sem("s_used")
        s_x, s_const = sem("s_x"), sem("s_const")
        s_xn, s_tp, s_xhi, s_xlo = sem("s_xn"), sem("s_tp"), sem("s_xhi"), sem("s_xlo")
        s_res, s_ssa, s_ss, s_sq = sem("s_res"), sem("s_ssa"), sem("s_ss"), sem("s_sq")
        s_ev = sem("s_ev")
        s_mc = sem("s_mc")
        s_tq, s_tqd, s_tqa = sem("s_tq"), sem("s_tqd"), sem("s_tqa")
        s_da, s_ab = sem("s_da"), sem("s_ab")
        s_lf, s_lft, s_lfc, s_qk = sem("s_lf"), sem("s_lft"), sem("s_lfc"), sem("s_qk")
        s_s, s_mx, s_exp, s_pt, s_pte, s_pv, s_o = (sem(n) for n in (
            "s_s", "s_mx", "s_exp", "s_pt", "s_pte", "s_pv", "s_o"))
        s_low, s_wup, s_z, s_lg = sem("s_low"), sem("s_wup"), sem("s_z"), sem("s_lg")
        s_lb, s_lbr, s_lbc, s_hk = sem("s_lb"), sem("s_lbr"), sem("s_lbc"), sem("s_hk")
        s_gd, s_gx, s_gq, s_gk, s_gs, s_gm, s_gr, s_gp, s_go = (sem(n) for n in (
            "s_gd", "s_gx", "s_gq", "s_gk", "s_gs", "s_gm", "s_gr", "s_gp", "s_go"))
        s_sk, s_sc, s_rt, s_ge, s_gn, s_route = (sem(n) for n in (
            "s_sk", "s_sc", "s_rt", "s_ge", "s_gn", "s_route"))
        s_cev = sem("s_cev")
        s_whi, s_wlo = sem("s_whi"), sem("s_wlo")
        s_eq, s_ohg, s_g, s_hm = sem("s_eq"), sem("s_ohg"), sem("s_g"), sem("s_hm")
        s_dve, s_act, s_pc = sem("s_dve"), sem("s_act"), sem("s_pc")
        s_done, s_out = sem("s_done"), sem("s_out")

        block = ctx.enter_context(nc.Block())

        def B(off, n):
            return big[:, off:off + n]

        PR = B(O_P, 8192).rearrange("p (t n) -> p t n", t=TT)
        TR = B(O_T, 4096).rearrange("p (c t) -> p c t", t=SEQ)
        XN = B(O_XN, 2048).rearrange("p (t n) -> p t n", t=TT)
        LG = B(O_LG, 2048).rearrange("p (t n) -> p t n", t=TT)
        MC = B(O_MC, 9 * P).rearrange("p (l t) -> p l t", t=P)
        MK = B(O_MK, 8 * P).rearrange("p (l t) -> p l t", t=P)
        ST = B(O_ST, 4 * P).rearrange("p (b t) -> p b t", t=P)
        EB = B(O_E, 2048).rearrange("p (b l t) -> p b l t", b=2, t=P)
        QD = B(O_QD, 2048).rearrange("p (b l t) -> p b l t", b=2, t=P)
        KD = B(O_KD, 2048).rearrange("p (b l t) -> p b l t", b=2, t=P)
        AM = B(O_A, 1024).rearrange("p (l t) -> p l t", t=P)
        KS = B(O_KS, 256).rearrange("p (b t) -> p b t", t=P)
        BIG0 = B(O_MC, 256)
        LFT = B(O_SM, 256)
        LFA = B(O_SM + 256, 256)
        LFB = B(O_SM + 512, 256)
        NM = B(O_SM + 800, 32).rearrange("p (h t) -> p h t", t=TT)
        RSUM = B(O_SM + 832, 32).rearrange("p (h t) -> p h t", t=TT)
        RL = B(O_SM + 864, 32).rearrange("p (h t) -> p h t", t=TT)
        QS = B(O_SM + 896, 64)
        QR = B(O_SM + 960, 64)
        PB = B(O_KD, 768).rearrange("p (b s) -> p b s", b=2)
        PTB = B(O_KD + 768, 768).rearrange("p (b s) -> p b s", b=2)
        LOWT = B(O_SM, 256)
        WUP = B(O_WUP, 512)
        LBC = B(O_SM + 256, 64)
        SCR = B(O_E, 2048)
        SCR2 = B(O_QD, 2048).rearrange("p (t n) -> p t n", t=TT)
        LBR = B(O_KD, 1024)
        OML = B(O_KD + 1024, 1024)
        H = big[:, :].rearrange("p (j t) -> p j t", t=SEQ)
        QT = B(O_QT, 4096).rearrange("p (c t) -> p c t", t=SEQ)
        SK = B(O_SK, 2048)
        CAND = B(O_CAND, 2048)
        EQ = B(O_EQ, 2048)
        TMP = B(O_TMP, 2048).rearrange("p (c k) -> p c k", k=NK)
        VAL = B(O_RS, 256).rearrange("p (c k) -> p c k", k=TOPK)
        IDX = B(O_RS + 256, 256).rearrange("p (c k) -> p c k", k=TOPK)
        IDF = B(O_RS + 512, 256).rearrange("p (c k) -> p c k", k=TOPK)
        BEST = B(O_RS + 768, 128).rearrange("p (h k) -> p h k", k=TOPK)
        POS = B(O_RS + 896, 128).rearrange("p (h k) -> p h k", k=TOPK)
        PAB = B(O_RS + 1024, 256).rearrange("p (s c) -> p s c", s=2)
        PAF = B(O_RS + 1280, 256).rearrange("p (s c) -> p s c", s=2)
        ROUT = [B(O_RS + 1536 + 3 * P * t, 3 * P).rearrange("p (w c) -> p w c", w=3) for t in range(TT)]
        ZS = B(O_RS + 2304, 16)
        EX = B(O_RS + 2320, 128).rearrange("p (h k) -> p h k", k=TOPK)

        def steps(eng, n, body, first=False):
            lo4, hi4 = (1 if first else 0), n // 4 - 1
            if first:
                for s in range(4):
                    body(0, s, s)
            with eng.Fori(lo4, hi4) as i:
                for s in range(4):
                    body(i, s, i * 4 + s)
            for s in range(4):
                body(hi4, s, 4 * hi4 + s)

        def chunk(j):
            return H[:, j, :] if isinstance(j, int) else H[:, bass.ds(j, 1), :].rearrange("p c t -> p (c t)")

        @block.sync
        def _(sp):
            for s in range(RAW):
                sp.dma_start(raw[:, s, :], stream[s]).then_inc(s_raw[s], 16)
            full = N // RAW

            def load(n, s):
                sp.wait_ge(s_lo, n - RAW + 1)
                sp.dma_start(raw[:, s, :], stream[bass.ds(n, 1)].rearrange("o p c -> p (o c)")
                             if not isinstance(n, int) else stream[n]).then_inc(s_raw[s], 16)

            with sp.Fori(1, full) as i:
                for s in range(RAW):
                    load(i * RAW + s, s)
            for n in range(full * RAW, N):
                load(n, n % RAW)
            sp.wait_ge(s_done, 1)
            sp.dma_start(out.rearrange("(t p) d -> p t d", p=P), resid[:]).then_inc(s_out, 16)
            sp.wait_ge(s_out, 16)

        @block.gpsimd
        def _(pool):
            chain = [0]

            def link(ins):
                chain[0] += 1
                ins.then_inc(s_pc, 1)
                pool.wait_ge(s_pc, chain[0])

            pool.dma_start(resid[:], x.rearrange("(t p) d -> p t d", p=P)).then_inc(s_x, 16)
            pool.dma_start(prm[:], prm_d).then_inc(s_x, 16)
            link(nc.gpsimd.memset(ident[:], 0.0))
            link(nc.gpsimd.affine_select(out=ident[:], in_=ident[:], compare_op=ALU.not_equal, fill=1.0,
                                         base=0, pattern=[[-1, P]], channel_multiplier=1))
            link(nc.gpsimd.memset(minus_half[:], -0.5))
            link(nc.gpsimd.tensor_copy(identb[:], ident[:]))
            link(nc.gpsimd.memset(BIG0, -1.0))
            link(nc.gpsimd.affine_select(out=BIG0[:, 0:P], in_=BIG0[:, 0:P], compare_op=ALU.is_ge, fill=0.0,
                                         base=0, pattern=[[1, P]], channel_multiplier=-1))
            link(nc.gpsimd.tensor_copy(nur[:], BIG0))
            link(nc.gpsimd.memset(maskb[:], 0.0))
            link(nc.gpsimd.affine_select(out=maskb[:], in_=maskb[:], compare_op=ALU.is_ge, fill=NEG,
                                         base=0, pattern=[[-1, P]], channel_multiplier=1))
            nc.gpsimd.iota(iota[:], pattern=[[1, P]], base=0, channel_multiplier=0,
                           allow_small_or_imprecise_dtypes=True).then_inc(s_const, 1)

            def keep(ap, pattern, base, cm, fill=0.0, last=None):
                ins = nc.gpsimd.affine_select(out=ap, in_=ap, compare_op=ALU.is_ge, fill=fill,
                                              base=base, pattern=pattern, channel_multiplier=cm)
                link(ins)

            norms = [0]

            def norm_power(out_, in_):
                norms[0] += 1
                pool.wait_ge(s_ss, norms[0])
                nc.gpsimd.tensor_tensor(out_, in_, minus_half[:, 0:in_.shape[1]], ALU.pow).then_inc(s_sq, 1)

            def linear_constants():
                link(nc.gpsimd.memset(MC, 1.0))
                link(nc.gpsimd.memset(MK, 0.0))
                keep(MC[:, 0, :], [[-1, P]], -1, 1)
                keep(MC[:, 8, :], [[1, P]], 0, -1)
                for l in range(LEVELS):
                    h = 1 << l
                    v = MC[:, 1 + l, :].rearrange("p (b s x) -> p b s x", s=2, x=h)
                    m = MK[:, l, :].rearrange("p (b s x) -> p b s x", s=2, x=h)
                    nb = P // (2 * h)
                    pat = [[2 * h, nb], [1, h]]
                    neg = [[-2 * h, nb], [-1, h]]
                    blk = [[2 * h, nb], [0, h]]
                    nblk = [[-2 * h, nb], [0, h]]
                    keep(v[:, :, 1, :], nblk, -h, 1)
                    keep(v[:, :, 1, :], pat, h, -1)
                    keep(v[:, :, 0, :], neg, -1, 1)
                    keep(v[:, :, 0, :], blk, h - 1, -1)
                    link(nc.gpsimd.memset(m[:, :, 1, :], 1.0))
                    keep(m[:, :, 1, :], nblk, 0, 1)
                    keep(m[:, :, 1, :], blk, h - 1, -1)
                link(nc.gpsimd.affine_select(out=MK[:, 7, :], in_=MK[:, 7, :], compare_op=ALU.not_equal,
                                             fill=1.0, base=0, pattern=[[-1, P]], channel_multiplier=1))

            def decayed_keys(L):
                H_ = HEADS[L["kind"]]
                for u in range(2 * H_):
                    h, tt, g = u // 2, u % 2, L["gu"] + u
                    pool.wait_ge(s_gx, g + 1)
                    if u >= 2:
                        pool.wait_ge(s_gs, g - 1)
                    if u == 0:
                        pool.wait_ge(s_tqa, L["tq"] + (2 if L["kind"] == "gla" else 4))
                    kT = TR[:, H_ + h, tt * P:(tt + 1) * P]
                    if tt == 0:
                        nc.gpsimd.tensor_tensor(KS[:, h % 2, :], EB[:, u % 2, 0, :], kT, ALU.mult)
                    lv = 1 - tt
                    nc.gpsimd.tensor_tensor(KD[:, u % 2, lv:lv + LEVELS, :], EB[:, u % 2, lv:lv + LEVELS, :],
                                            kT.unsqueeze(1).broadcast_to([P, LEVELS, P]),
                                            ALU.mult).then_inc(s_gk, 1)

            for L in PLAN.layers:
                l, kind = L["l"], L["kind"]
                if l:
                    pool.wait_ge(s_used, L["small"])
                pool.dma_start(SK, sk_d[l]).then_inc(s_sk, 16)
                if kind == "gla":
                    pool.dma_start(WUP[0:GLA_RANK + 1, :], wup_d).then_inc(s_wup, 16)
                norm_power(sm[:, 4:6], sm[:, 2:4])
                if kind != "fox":
                    linear_constants()
                nc.gpsimd.memset(sm[:, 60:61], 0.0).then_inc(s_mc, 1)
                if kind == "fox":
                    norm_power(QR, QS)
                else:
                    decayed_keys(L)
                    n = 2 * HEADS[kind]
                    norm_power(sm[:, 40:40 + n], sm[:, 24:24 + n])
                norm_power(sm[:, 4:6], sm[:, 2:4])
                n0 = L["u"]
                pool.wait_ge(s_lo, n0)
                with pool.Fori(0, HALF // 4) as i:
                    for s in range(4):
                        n = i * 4 + (n0 + s)
                        pool.wait_ge(s_hi, n + 1)
                        pool.wait_ge(s_used, n - LO + 1)
                        nc.gpsimd.tensor_tensor(lo[:, (n0 + s) % LO, :], raw[:, (n0 + s) % RAW, :],
                                                hi[:, (n0 + s) % HI, :], ALU.subtract).then_inc(s_lo, 1)
                def split_w(k, n, s):
                    pool.wait_ge(s_whi, n)
                    nc.gpsimd.tensor_tensor(xlo[:, s, :], chunk(k), xhi[:, s, :], ALU.subtract).then_inc(s_wlo, 1)

                for half in range(2):
                    if half == 1:
                        split_w(0, NCH * l + 1, 0)

                    def g_step(i, s, k):
                        pool.wait_ge(s_eq, k + (HALF * (2 * l + half) + 1))
                        for q in range(2):
                            g = gate2[:, q, bass.ds(i * 16 + 4 * s, 4)].unsqueeze(2).broadcast_to([P, 4, HALF])
                            ins = nc.gpsimd.tensor_tensor(ohg[:, s % 2, q], oh2[:, s % 2], g, ALU.mult)
                        ins.then_inc(s_ohg, 1)
                        if half == 1 and not (isinstance(k, int) and k == HALF - 1):
                            split_w(k + 1, k + (NCH * l + 2), (s + 1) % 4)

                    steps(pool, HALF, g_step)

        @block.scalar
        def _(act):
            chain = [0]

            def link(ins):
                chain[0] += 1
                ins.then_inc(s_act, 1)
                act.wait_ge(s_act, chain[0])

            def round_slab(n, base):
                k = base % RAW
                act.wait_ge(s_raw[k], landed(n, base))
                if not (isinstance(n, int) and n < HI):
                    act.wait_ge(s_used, n - HI + 1)
                nc.scalar.copy(hi[:, base % HI, :], raw[:, k, :]).then_inc(s_hi, 1)

            def landed(n, base):
                return 16 * (n // RAW + 1) if isinstance(n, int) else (n + (RAW - base % RAW)) * (16 // RAW)

            def transposed(tau, gain):
                for c in range(DC):
                    act.wait_ge(s_tp, DC * tau + (c | 1) + 1)
                    nc.scalar.activation(xhi[:, c, :], ps[:, c // 2, (c % 2) * SEQ:(c % 2 + 1) * SEQ], ACT.Copy,
                                         scale=1.0 if gain is None else prm[:, gain + c:gain + c + 1]
                                         ).then_inc(s_xhi, 1)

            def square(tile):
                act.wait_ge(s_res, tile + 1)
                nc.scalar.activation(XN[:, 0, :], resid[:, 0, :], ACT.Square, accum_out=sm[:, 0:1]).then_inc(s_ssa, 1)

            def evacuate(L, g):
                fn = ACT.Copy
                if L["kind"] == "fox" and g == 3:
                    fn = ACT.Sigmoid
                if L["kind"] == "gla" and g == 2 or L["kind"] == "hgrn" and g == 3:
                    fn = ACT.Silu
                if L["kind"] == "hgrn" and g == 1:
                    fn = ACT.Sigmoid
                act.wait_ge(s_used, L["in"] + DC * (g + 1))
                for tt in range(TT):
                    for nh in range(2):
                        nc.scalar.activation(PR[:, tt, g * D + nh * 512:g * D + (nh + 1) * 512],
                                             ps[:, BANKS[g % 2] + 2 * tt + nh, :], fn).then_inc(s_ev, 1)

            def project_in(L):
                G = GROUPS[L["kind"]]
                for n in range(L["small"] + 2, L["out"] + 2):
                    round_slab(n, n)
                    g, k = divmod(n - L["in"] - 2, DC)
                    if k == 0 and g >= 1:
                        evacuate(L, g - 1)
                    gates(L, n - L["in"])
                evacuate(L, G - 1)

            def gates(L, k):
                if L["kind"] == "fox" and k == 7:
                    act.wait_ge(s_da, ab["da"] + 1)
                    link(nc.scalar.activation(LFB[0:16, :], LFA[0:16, :], ACT.Exp))
                    nc.scalar.activation(LFA[0:16, :], LFB[0:16, :], ACT.Ln, bias=1.0).then_inc(s_ab, 1)
                    ab["da"] += 1
                if L["kind"] == "gla" and k == 7:
                    act.wait_ge(s_da, ab["da"] + 1)
                    link(nc.scalar.activation(XN[:, :, 0:512], XN[:, :, 0:512], ACT.Exp))
                    nc.scalar.activation(XN[:, :, 512:1024], XN[:, :, 0:512], ACT.Ln, bias=1.0).then_inc(s_ab, 1)
                    ab["da"] += 1
                if L["kind"] == "hgrn" and k in (27, 28):
                    tt = k - 27
                    act.wait_ge(s_da, ab["da"] + 1)
                    nc.scalar.activation(LG[:, tt, :], SCR2[:, tt, :], ACT.Ln).then_inc(s_ab, 1)
                    ab["da"] += 1

            def fox(L):
                f = L["fox"]
                for b in range(4):
                    act.wait_ge(s_tq, 2 * L["tq"] + 1 + b)
                    nc.scalar.activation(TR[:, 8 + 2 * b:10 + 2 * b, :].rearrange("p c t -> p (c t)"),
                                         ps[:, 4 + b, :], ACT.Copy,
                                         scale=prm[:, PRM["kg"] + f:PRM["kg"] + f + 1]).then_inc(s_tqa, 1)
                b0 = FOX_HEADS * f
                for h in range(FOX_HEADS + 1):
                    if h < FOX_HEADS:
                        act.wait_ge(s_mx, b0 + h + 1)
                        if h >= 2:
                            act.wait_ge(s_pt, b0 + h - 1)
                        nc.scalar.activation(PB[:, h % 2, 0:P], ps[:, h % 2, 0:P], ACT.Exp,
                                             bias=NM[:, h, 0:1], accum_out=RSUM[:, h, 0:1])
                        nc.scalar.activation(PB[:, h % 2, P:3 * P], ps[:, h % 2, P:3 * P], ACT.Exp,
                                             bias=NM[:, h, 1:2], accum_out=RSUM[:, h, 1:2]).then_inc(s_exp, 1)
                    if h >= 1:
                        g = h - 1
                        act.wait_ge(s_pt, b0 + g + 1)
                        if g >= 2:
                            act.wait_ge(s_pv, b0 + g - 1)
                        nc.scalar.copy(PTB[:, g % 2, :], ps[:, 2 + g % 2, 0:3 * P]).then_inc(s_pte, 1)

            def linear(L):
                kind, H_ = L["kind"], HEADS[L["kind"]]
                dv = D // H_
                nb = H_ // 2
                for b in range(nb):
                    act.wait_ge(s_tq, 2 * L["tq"] + 1 + b)
                    nc.scalar.activation(TR[:, H_ + 2 * b:H_ + 2 * b + 2, :].rearrange("p c t -> p (c t)"),
                                         ps[:, nb + b, :], ACT.Copy).then_inc(s_tqa, 1)
                U = 2 * H_
                for u in range(U + 2):
                    if u < U:
                        g = L["gu"] + u
                        act.wait_ge(s_gd, g + 1)
                        if u >= 2:
                            act.wait_ge(s_gq, g - 1)
                            act.wait_ge(s_gk, g - 1)
                        nc.scalar.activation(EB[:, u % 2].rearrange("p l t -> p (l t)"),
                                             ps[:, 0:2, :].rearrange("p b c -> p (b c)"), ACT.Exp).then_inc(s_gx, 1)
                    if u >= 2:
                        w = u - 2
                        g, h, tt = L["gu"] + w, w // 2, w % 2
                        act.wait_ge(s_gp, g + 1)
                        o = ps[:, 7, (w % 2) * 256:(w % 2) * 256 + dv]
                        nc.scalar.activation(XN[:, tt, h * dv:(h + 1) * dv], o, ACT.Square,
                                             accum_out=sm[:, 8 + tt * H_ + h:9 + tt * H_ + h])
                        nc.scalar.copy(PR[:, tt, h * dv:(h + 1) * dv], o).then_inc(s_go, 1)

            ab = {"da": 0}
            act.wait_ge(s_const, 1)
            act.wait_ge(s_x, 32)
            for n in range(2):
                round_slab(n, n)
            for L in PLAN.layers:
                l, kind = L["l"], L["kind"]
                square(2 * l)
                transposed(3 * l, PRM["mix"] + DC * l)
                if kind == "hgrn":
                    act.wait_ge(s_da, ab["da"] + 1)
                    nc.scalar.activation(LBC[:, 0:32], LBC[:, 0:32], ACT.Exp).then_inc(s_ab, 1)
                    ab["da"] += 1
                project_in(L)
                if kind == "fox":
                    fox(L)
                else:
                    linear(L)
                transposed(3 * l + 1, None if kind == "fox" else PRM[kind + "_gain"])
                for n in range(L["out"] + 2, L["wq"] + 2):
                    round_slab(n, n)
                square(2 * l + 1)
                transposed(3 * l + 2, PRM["ffn"] + DC * l)
                for m in range(PH):
                    for s in range(2):
                        round_slab(L["wq"] + 2 * m + 2 + s, L["wq"] + 2 * m + 2 + s)
                    act.wait_ge(s_used, L["wq"] + 2 * m + 2)
                    nc.scalar.copy(QT[:, 2 * m:2 * m + 2, :].rearrange("p c t -> p (c t)"),
                                   ps[:, 4 + m % 2, :]).then_inc(s_cev, 1)
                n0 = L["u"]

                def u_steps(j0, j1):
                    with act.Fori(j0 // 4, j1 // 4) as i:
                        for s in range(4):
                            round_slab(i * 4 + (n0 + s + 2), n0 + s + 2)
                            if s % 2:
                                act.wait_ge(s_used, i * 4 + (n0 + s + 1))
                                nc.scalar.activation(H[:, bass.ds(i * 4 + (s - 1), 2), :].rearrange(
                                    "p c t -> p (c t)"), ps[:, 4 + s // 2, :], ACT.Gelu).then_inc(s_cev, 1)

                def gelu_table():
                    nc.scalar.activation(sm[:, 63:64], ident[:, 0:1], ACT.Gelu)

                j0 = 0
                for tt in range(TT):
                    gelu_table()
                    u_steps(j0, EXP_AT[tt])
                    j0 = EXP_AT[tt]
                    act.wait_ge(s_ge, TT * l + tt + 1)
                    nc.scalar.activation(EX, BEST, ACT.Exp).then_inc(s_gn, 1)
                gelu_table()
                u_steps(j0, HALF)
                act.wait_ge(s_hm, (NCH + 2) * l + 2)
                u_steps(HALF, NCH)
                n0 = L["v"]

                def round_w(j, s, wait=True):
                    if wait:
                        act.wait_ge(s_used, j + (n0 - 3))
                    nc.scalar.copy(xhi[:, s, :], chunk(j)).then_inc(s_whi, 1)

                act.wait_ge(s_used, n0)
                for half in range(2):
                    j0 = half * HALF
                    act.wait_ge(s_hm, (NCH + 2) * l + 2 + j0 + HALF)
                    for s in range(2):
                        round_w(j0 + s, s, wait=half == 1)

                    def v_step(i, s, k):
                        n = k + (n0 + j0 + 2)
                        if not isinstance(i, int) or n < N:
                            round_slab(n, n0 + s + 2)
                        if not isinstance(i, int) or i == 0 or s < 2:
                            round_w(k + (j0 + 2), (s + 2) % 4, wait=not (isinstance(i, int) and half == 0 and k < 2))

                    steps(act, HALF, v_step, first=True)

        @block.vector
        def _(dve):
            chain = [0]

            def mark(ins):
                chain[0] += 1
                ins.then_inc(s_dve, 1)

            def join():
                dve.wait_ge(s_dve, chain[0])

            def link(ins):
                mark(ins)
                join()

            def split_slab(n, base):
                dve.wait_ge(s_hi, n + 1)
                if not (isinstance(n, int) and n < LO):
                    dve.wait_ge(s_used, n - LO + 1)
                nc.vector.tensor_tensor(lo[:, base % LO, :], raw[:, base % RAW, :], hi[:, base % HI, :],
                                        ALU.subtract).then_inc(s_lo, 1)

            def transposed(tau, gain):
                for c in range(DC):
                    dve.wait_ge(s_xhi, DC * tau + (c | 1) + 1)
                    nc.vector.scalar_tensor_tensor(
                        out=xlo[:, c, :], in0=ps[:, c // 2, (c % 2) * SEQ:(c % 2 + 1) * SEQ],
                        scalar=1.0 if gain is None else prm[:, gain + c:gain + c + 1], in1=xhi[:, c, :],
                        op0=ALU.mult, op1=ALU.subtract).then_inc(s_xlo, 1)

            def norm():
                link(nc.vector.tensor_tensor_reduce(
                    out=XN[:, 1, :], in0=resid[:, 1, :], in1=resid[:, 1, :], scale=1.0, scalar=0.0,
                    op0=ALU.mult, op1=ALU.add, accum_out=sm[:, 1:2]))
                ab["norm"] += 1
                dve.wait_ge(s_ssa, ab["norm"])
                mean_squares(sm[:, 2:4], sm[:, 0:2], D)
                for tt in range(TT):
                    nc.vector.tensor_scalar(XN[:, tt, :], resid[:, tt, :], sm[:, 4 + tt:5 + tt], None,
                                            ALU.mult).then_inc(s_xn, 1)

            def mean_squares(out_, in_, n):
                nc.vector.tensor_scalar(out_, in_, 1.0 / n, EPS, ALU.mult, ALU.add).then_inc(s_ss, 1)
                ab["sq"] += 1
                dve.wait_ge(s_sq, ab["sq"])

            def add_residual(n, bank):
                dve.wait_ge(s_used, n)
                for tt in range(TT):
                    for nh in range(2):
                        r = resid[:, tt, nh * 512:(nh + 1) * 512]
                        ins = nc.vector.tensor_tensor(r, ps[:, bank + 2 * tt + nh, :], r, ALU.add)
                        if (tt, nh) == (0, 1):
                            ins.then_inc(s_res, 1)
                            ab["res"] += 1
                        else:
                            mark(ins)
                dve.wait_ge(s_res, ab["res"])
                join()

            def forget_gates(L):
                bias = prm[0:FOX_HEADS, PRM["bf"] + L["fox"]:PRM["bf"] + L["fox"] + 1]
                dve.wait_ge(s_used, L["small"] + 1)
                link(nc.vector.tensor_scalar(LFT[0:16, :], ps[0:16, 0, 0:SEQ], bias, None, ALU.add))
                nc.vector.scalar_tensor_tensor(out=LFA[0:16, :], in0=LFT[0:16, :], scalar=-1.0, in1=LFT[0:16, :],
                                               op0=ALU.mult, op1=ALU.min).then_inc(s_da, 1)
                ab["da"] += 1

            def log_forget(L):
                ab["ab"] += 1
                dve.wait_ge(s_ab, ab["ab"])
                nc.vector.scalar_tensor_tensor(out=LFB[0:16, :], in0=LFT[0:16, :], scalar=0.0, in1=LFA[0:16, :],
                                               op0=ALU.min, op1=ALU.subtract).then_inc(s_lf, 1)

            def norm_qk(L, k):
                QK = {12: (0, 0), 13: (0, 1), 20: (1, 0), 21: (1, 1)}
                if k in QK:
                    side, tt = QK[k]
                    dve.wait_ge(s_ev, L["ev"] + 4 * (side + 1))
                    v = PR[:, tt, side * D:(side + 1) * D]
                    mark(nc.vector.tensor_tensor(SCR[:, tt * D:(tt + 1) * D], v, v, ALU.mult))
                if k - 2 in QK:
                    side, tt = QK[k - 2]
                    join()
                    mark(nc.vector.tensor_reduce(
                        QS[:, 32 * tt + 16 * side:32 * tt + 16 * side + 16],
                        SCR[:, tt * D:(tt + 1) * D].rearrange("p (h d) -> p h d", d=FOX_DH), AX.X, ALU.add))
                if k == 24:
                    join()
                    mean_squares(QS, QS, FOX_DH)
                if 25 <= k < 29:
                    side, tt = divmod(k - 25, 2)
                    v = PR[:, tt, side * D:(side + 1) * D].rearrange("p (h d) -> p h d", d=FOX_DH)
                    r = QR[:, 32 * tt + 16 * side:32 * tt + 16 * side + 16]
                    nc.vector.tensor_tensor(v, v, r.unsqueeze(2).broadcast_to([P, 16, FOX_DH]),
                                            ALU.mult).then_inc(s_qk, 1)

            def fox_core(L):
                f = L["fox"]
                dve.wait_ge(s_lft, f + 1)
                v = ps[:, 0, 0:32].rearrange("p (t h) -> p t h", t=TT)
                link(nc.vector.tensor_copy(lfh[:], v))
                nc.vector.tensor_tensor(lfl[:], v, lfh[:], ALU.subtract).then_inc(s_lfc, 1)
                for m, b in enumerate((1, 2, 3, 0)):
                    dve.wait_ge(s_tq, 2 * L["tq"] + 5 + m)
                    nc.vector.tensor_scalar(TR[:, 2 * b:2 * b + 2, :].rearrange("p c t -> p (c t)"), ps[:, b, :],
                                            prm[:, PRM["qg"] + f:PRM["qg"] + f + 1], FOX_DH ** -0.5,
                                            ALU.mult, ALU.mult).then_inc(s_tqd, 1)
                b0 = FOX_HEADS * f
                for h in range(FOX_HEADS + 2):
                    if h < FOX_HEADS:
                        dve.wait_ge(s_s, b0 + h + 1)
                        nc.vector.tensor_reduce(NM[:, h, 0:1], ps[:, h % 2, 0:P], AX.X, ALU.max, negate=True)
                        nc.vector.tensor_reduce(NM[:, h, 1:2], ps[:, h % 2, P:3 * P], AX.X, ALU.max,
                                                negate=True).then_inc(s_mx, 1)
                    if 1 <= h <= FOX_HEADS:
                        dve.wait_ge(s_exp, b0 + h)
                        mark(nc.vector.reciprocal(RL[:, h - 1, :], RSUM[:, h - 1, :]))
                    if h >= 2:
                        g = h - 2
                        dve.wait_ge(s_pv, b0 + g + 1)
                        join()
                        for tt in range(TT):
                            gate = PR[:, tt, 3 * D + g * FOX_DH:3 * D + (g + 1) * FOX_DH]
                            ins = nc.vector.scalar_tensor_tensor(
                                out=gate, in0=ps[:, 4 + g % 2, tt * FOX_DH:(tt + 1) * FOX_DH],
                                scalar=RL[:, g, tt:tt + 1], in1=gate, op0=ALU.mult, op1=ALU.mult)
                        ins.then_inc(s_o, 1)

            def gla_gates(L, k):
                lg = LG[:, :, 0:512]
                if k == 0:
                    dve.wait_ge(s_used, L["small"] + 1)
                    dve.wait_ge(s_low, 1)
                    nc.vector.tensor_copy(LOWT[0:GLA_RANK, :], ps[0:GLA_RANK, 0, 0:SEQ]).then_inc(s_low, 1)
                if k == 3:
                    dve.wait_ge(s_z, 1)
                    link(nc.vector.tensor_copy(lg, ps[:, 2:4, :]))
                if k == 4:
                    nc.vector.scalar_tensor_tensor(out=XN[:, :, 0:512], in0=lg, scalar=-1.0, in1=lg,
                                                   op0=ALU.mult, op1=ALU.min).then_inc(s_da, 1)
                    ab["da"] += 1
                if k == 10:
                    ab["ab"] += 1
                    dve.wait_ge(s_ab, ab["ab"])
                    mark(nc.vector.scalar_tensor_tensor(out=lg, in0=lg, scalar=0.0, in1=XN[:, :, 512:1024],
                                                        op0=ALU.min, op1=ALU.subtract))
                if k == 11:
                    join()
                    nc.vector.tensor_scalar(lg, lg, 1.0 / GLA_TAU, None, ALU.mult).then_inc(s_lg, 1)

            def hgrn_bounds():
                i = KIND.index("hgrn")
                lb = prm[:, PRM["lb"]:PRM["lb"] + DEPTH * DC].rearrange("p (r c) -> p r c", c=DC)
                e = LBC[:, 0:32].rearrange("p (r c) -> p r c", c=DC)
                m = LBC[:, 32:40]
                r = LBC[:, 40:48]
                link(nc.vector.tensor_reduce(m, lb.rearrange("p r c -> p c r"), AX.X, ALU.max))
                nc.vector.tensor_tensor(e, lb, m.unsqueeze(1).broadcast_to([P, DEPTH, DC]),
                                        ALU.subtract).then_inc(s_da, 1)
                ab["da"] += 1
                ab["ab"] += 3
                dve.wait_ge(s_ab, ab["ab"] - 2)
                link(nc.vector.tensor_reduce(r, e.rearrange("p r c -> p c r"), AX.X, ALU.add))
                link(nc.vector.reciprocal(r, r))
                link(nc.vector.tensor_tensor(e, e, r.unsqueeze(1).broadcast_to([P, DEPTH, DC]), ALU.mult))
                link(nc.vector.tensor_copy(m, e[:, 0, :]))
                for j in range(1, i + 1):
                    link(nc.vector.tensor_tensor(m, m, e[:, j, :], ALU.add))
                nc.vector.tensor_tensor(LBC[:, 48:56], m, e[:, 0, :], ALU.subtract).then_inc(s_lb, 1)

            def hgrn_bound_rows():
                dve.wait_ge(s_lbr, 1)
                nc.vector.tensor_copy(LBR.rearrange("p (b c) -> p b c", b=2), ps[:, 0:2, :]).then_inc(s_lbc, 1)
                nc.vector.tensor_scalar(OML.rearrange("p (b c) -> p b c", b=2), ps[:, 0:2, :], -1.0, 1.0,
                                        ALU.mult, ALU.add).then_inc(s_lbc, 1)
                dve.wait_ge(s_lbc, 2)

            def hgrn_gates(L, k):
                if k == 0:
                    hgrn_bound_rows()
                if k in (20, 21):
                    dve.wait_ge(s_ev, L["ev"] + 8)
                    tt = k - 20
                    mark(nc.vector.tensor_tensor(SCR2[:, tt, :], PR[:, tt, D:2 * D], OML, ALU.mult))
                if k in (22, 23):
                    tt = k - 22
                    join()
                    nc.vector.tensor_tensor(SCR2[:, tt, :], SCR2[:, tt, :], LBR, ALU.add).then_inc(s_da, 1)
                    ab["da"] += 1
                if k in (24, 25):
                    tt = k - 24
                    dve.wait_ge(s_da, ab["da"])
                    nc.vector.tensor_scalar(PR[:, tt, D:2 * D], SCR2[:, tt, :], -1.0, 1.0,
                                            ALU.mult, ALU.add).then_inc(s_hk, 1)

            def linear_core(L):
                kind, H_ = L["kind"], HEADS[L["kind"]]
                dv = D // H_
                for b in range(H_ // 2):
                    dve.wait_ge(s_tq, 2 * L["tq"] + H_ // 2 + 1 + b)
                    nc.vector.tensor_scalar(TR[:, 2 * b:2 * b + 2, :].rearrange("p c t -> p (c t)"), ps[:, b, :],
                                            float(P) ** -0.5, None, ALU.mult).then_inc(s_tqd, 1)
                dve.wait_ge(s_tqd, L["tq"] + H_ // 2)
                dve.wait_ge(s_mc, L["l"] + 1)
                U = 2 * H_
                for u in range(U + 1):
                    if u < U:
                        g, h, tt = L["gu"] + u, u // 2, u % 2
                        dve.wait_ge(s_gx, g + 1)
                        if u >= 2:
                            dve.wait_ge(s_gs, g - 1)
                        lv, n = (1, LEVELS) if tt == 0 else (0, LEVELS + 1)
                        nc.vector.tensor_tensor(
                            QD[:, u % 2, lv:lv + n, :], EB[:, u % 2, lv:lv + n, :],
                            TR[:, h, tt * P:(tt + 1) * P].unsqueeze(1).broadcast_to([P, n, P]),
                            ALU.mult).then_inc(s_gq, 1)
                    if u >= 1:
                        w = u - 1
                        g, h, tt = L["gu"] + w, w // 2, w % 2
                        dve.wait_ge(s_gs, g + 1)
                        if g:
                            dve.wait_ge(s_gr, g)
                        b = 2 + 2 * (w % 2)
                        nc.vector.tensor_tensor(AM.rearrange("p l t -> p (l t)"),
                                                ps[:, b:b + 2, :].rearrange("p b c -> p (b c)"),
                                                MK.rearrange("p l t -> p (l t)"), ALU.mult).then_inc(s_gm, 1)
                        dve.wait_ge(s_gm, g + 1)
                        if w >= 2:
                            dve.wait_ge(s_gp, g - 1)
                        ins = nc.vector.tensor_reduce(ST[:, w % 2, :], AM.rearrange("p l t -> p t l"), AX.X, ALU.add)
                        if tt == 1:
                            mark(ins)
                            ins = nc.vector.tensor_copy(ST[:, 2 + h % 2, :], ps[:, 6, (h % 2) * P:(h % 2 + 1) * P])
                            join()
                        ins.then_inc(s_gr, 1)
                dve.wait_ge(s_go, L["gu"] + U)
                mean_squares(sm[:, 24:24 + U], sm[:, 8:8 + U], dv)
                gg = (GROUPS[kind] - 1) * D
                for tt in range(TT):
                    for h in range(H_):
                        ins = nc.vector.scalar_tensor_tensor(
                            out=XN[:, tt, h * dv:(h + 1) * dv], in0=PR[:, tt, h * dv:(h + 1) * dv],
                            scalar=sm[:, 40 + tt * H_ + h:41 + tt * H_ + h],
                            in1=PR[:, tt, gg + h * dv:gg + (h + 1) * dv], op0=ALU.mult, op1=ALU.mult)
                        if h < H_ - 1:
                            mark(ins)
                    ins.then_inc(s_xn, 1)
                join()

            def top16(src, tmp, val, idx, batch):
                for c in batch:
                    mark(nc.vector.max(val[:, c, 0:8], src(c)))
                join()
                for c in batch:
                    mark(nc.vector.max_index(idx[:, c, 0:8].bitcast(U32), val[:, c, 0:8], src(c)))
                    mark(nc.vector.match_replace(tmp(c), val[:, c, 0:8], src(c), NEG))
                join()
                for c in batch:
                    mark(nc.vector.max(val[:, c, 8:16], tmp(c)))
                join()
                for c in batch:
                    mark(nc.vector.max_index(idx[:, c, 8:16].bitcast(U32), val[:, c, 8:16], tmp(c)))

            def route(L, tt):
                l = L["l"]
                for b in range(4):
                    dve.wait_ge(s_sc, 8 * l + 4 * tt + b + 1)
                    top16(lambda c: ps[:, c // 4, (c % 4) * NK:(c % 4 + 1) * NK], lambda c: TMP[:, c, :],
                          VAL, IDX, range(4 * b, 4 * b + 4))
                join()
                mark(nc.vector.tensor_copy(IDF, IDX.bitcast(U32)))
                v = VAL.rearrange("p (h s) k -> p h s k", s=2)
                cand = CAND.rearrange("p (h a b) -> p h a b", h=PH, a=TOPK)
                nc.vector.tensor_tensor(cand, v[:, :, 0, :].unsqueeze(3).broadcast_to([P, PH, TOPK, TOPK]),
                                        v[:, :, 1, :].unsqueeze(2).broadcast_to([P, PH, TOPK, TOPK]),
                                        ALU.add).then_inc(s_rt, 1)
                dve.wait_ge(s_rt, TT * l + tt + 1)
                ch = CAND.rearrange("p (h c) -> p h c", h=PH)
                eh = EQ.rearrange("p (h c) -> p h c", h=PH)
                for b in range(2):
                    top16(lambda c: ch[:, c, :], lambda c: eh[:, c, :], BEST, POS, range(4 * b, 4 * b + 4))
                join()
                mark(nc.vector.tensor_scalar(PAB[:, 0, :].bitcast(U32), POS.rearrange("p h k -> p (h k)").bitcast(U32),
                                             4, None, ALU.logical_shift_right))
                mark(nc.vector.tensor_scalar(PAB[:, 1, :].bitcast(U32), POS.rearrange("p h k -> p (h k)").bitcast(U32),
                                             15, None, ALU.bitwise_and))
                mark(nc.vector.tensor_copy(ZS[:, 0:8].unsqueeze(2), BEST[:, :, 0:1]))
                join()
                nc.vector.tensor_tensor(BEST, BEST, ZS[:, 0:8].unsqueeze(2).broadcast_to([P, PH, TOPK]),
                                        ALU.subtract).then_inc(s_ge, 1)
                link(nc.vector.tensor_copy(PAF, PAB.bitcast(U32)))
                ix = IDF.rearrange("p (h s) k -> p h s k", s=2)
                eq = EQ.rearrange("p (c a) -> p c a", a=TOPK)
                for side in range(2):
                    link(nc.vector.tensor_tensor(eq, PAF[:, side, :].unsqueeze(2).broadcast_to([P, P, TOPK]),
                                                 iota[:, 0:TOPK].unsqueeze(1).broadcast_to([P, P, TOPK]), ALU.is_equal))
                    e4 = EQ.rearrange("p (h k a) -> p h k a", h=PH, a=TOPK)
                    link(nc.vector.tensor_tensor(e4, e4, ix[:, :, side, :].unsqueeze(2).broadcast_to([P, PH, TOPK, TOPK]),
                                                 ALU.mult))
                    link(nc.vector.tensor_reduce(ROUT[tt][:, side, :], eq, AX.X, ALU.add))
                dve.wait_ge(s_gn, TT * l + tt + 1)
                link(nc.vector.tensor_reduce(ZS[:, 8:16], EX, AX.X, ALU.add))
                link(nc.vector.reciprocal(ZS[:, 8:16], ZS[:, 8:16]))
                nc.vector.tensor_tensor(ROUT[tt][:, 2, :].rearrange("p (h k) -> p h k", k=TOPK), EX,
                                        ZS[:, 8:16].unsqueeze(2).broadcast_to([P, PH, TOPK]),
                                        ALU.mult).then_inc(s_route, 1)
                dve.wait_ge(s_route, TT * l + tt + 1)

            def split_w(k, n, s):
                dve.wait_ge(s_whi, n)
                nc.vector.tensor_tensor(xlo[:, s, :], chunk(k), xhi[:, s, :], ALU.subtract).then_inc(s_wlo, 1)

            def one_hots(i, s, half, at):
                t0 = i * 16 + 4 * s
                tok = lambda e, w: e[:, bass.ds(t0, 4)].unsqueeze(2).broadcast_to([P, 4, w])
                dve.wait_ge(s_g, i * 4 + (at + s + 1))
                nc.vector.tensor_tensor(oh1[:, s % 2], iota[:].unsqueeze(1).broadcast_to([P, 4, P]),
                                        tok(e1T, P), ALU.is_equal)
                nc.vector.tensor_tensor(oh2[:, s % 2],
                                        iota[:, half * HALF:(half + 1) * HALF].unsqueeze(1).broadcast_to([P, 4, HALF]),
                                        tok(e2T, HALF), ALU.is_equal).then_inc(s_eq, 1)

            def weigh(i, s, half, at):
                dve.wait_ge(s_g, i * 4 + (at + s + 3))
                v = H[:, half * HALF:(half + 1) * HALF, bass.ds(i * 16 + 4 * s, 4)]
                nc.vector.scalar_tensor_tensor(
                    out=v, in0=ps[:, 6 + s % 2, 0:4 * HALF].rearrange("p (t j) -> p j t", t=4),
                    scalar=1.0 / GATE_SCALE, in1=v, op0=ALU.mult, op1=ALU.mult).then_inc(s_hm, 1)

            ab = {"ab": 0, "sq": 0, "da": 0, "norm": 0, "res": 1}
            dve.wait_ge(s_x, 32)
            dve.wait_ge(s_const, 1)
            nc.vector.memset(sm[:, 61:62], 0.0).then_inc(s_res, 1)
            for L in PLAN.layers:
                l, kind = L["l"], L["kind"]
                norm()
                transposed(3 * l, PRM["mix"] + DC * l)
                if kind == "hgrn":
                    hgrn_bounds()
                if kind == "gla":
                    nc.vector.memset(LOWT[0:32, :], 1.0).then_inc(s_low, 1)
                for n in range(L["small"], L["out"]):
                    k = n - L["in"]
                    split_slab(n, n)
                    if kind == "fox":
                        if k == 0:
                            forget_gates(L)
                        if k == 10:
                            log_forget(L)
                        norm_qk(L, k)
                    elif kind == "gla":
                        gla_gates(L, k)
                    else:
                        hgrn_gates(L, k)
                if kind == "fox":
                    fox_core(L)
                else:
                    linear_core(L)
                transposed(3 * l + 1, None if kind == "fox" else PRM[kind + "_gain"])
                for n in range(L["out"], L["wq"]):
                    split_slab(n, n)
                add_residual(L["wq"], 4)
                norm()
                transposed(3 * l + 2, PRM["ffn"] + DC * l)
                for n in range(L["wq"], L["u"]):
                    split_slab(n, n)
                for tt in range(TT):
                    route(L, tt)
                g0 = (NCH + 2) * l
                dve.wait_ge(s_g, g0 + 2)
                link(nc.vector.tensor_scalar(gate2[:, 0, :], ps[:, 7, 0:SEQ], GATE_SCALE, None, ALU.mult))
                mark(nc.vector.tensor_copy(e1T[:], ps[:, 6, 0:SEQ]))
                nc.vector.tensor_copy(e2T[:], ps[:, 6, SEQ:2 * SEQ]).then_inc(s_hm, 1)
                nc.vector.scalar_tensor_tensor(out=gate2[:, 1, :], in0=ps[:, 7, 0:SEQ], scalar=GATE_SCALE,
                                               in1=gate2[:, 0, :], op0=ALU.mult,
                                               op1=ALU.subtract).then_inc(s_hm, 1)
                dve.wait_ge(s_hm, g0 + 2)
                dve.wait_ge(s_lo, L["u"] + HALF)
                for half in range(2):
                    n0 = (L["u"] + HALF, L["v"])[half]
                    at = g0 + half * HALF
                    if half == 0:
                        split_slab(n0, n0)
                    one_hots(0, 0, half, at)
                    dve.wait_ge(s_cev, (PH + HALF) * l + PH + HALF // 2 * (half + 1))

                    def g_step(i, s, k):
                        last = isinstance(k, int) and k == HALF - 1
                        split_slab(k + (n0 + 1), n0 + s + 1)
                        if not last:
                            if s < 3:
                                one_hots(i, s + 1, half, at)
                            else:
                                one_hots(i + 1, 0, half, at)
                        weigh(i, s, half, at)

                    steps(dve, HALF, g_step)
                n0 = L["v"] + HALF
                dve.wait_ge(s_wlo, NCH * l + HALF)
                split_w(HALF, NCH * l + HALF + 1, 0)

                def v_step(i, s, k):
                    if not (isinstance(k, int) and k == HALF - 1):
                        split_slab(k + (n0 + 1), n0 + s + 1)
                        split_w(k + (HALF + 1), k + (NCH * l + HALF + 2), (s + 1) % 4)

                steps(dve, HALF, v_step)
                add_residual(L["end"], 0)
            nc.vector.tensor_copy(sm[:, 62:63], sm[:, 60:61]).then_inc(s_done, 1)

        @block.tensor
        def _(pe):
            def product(out_, lh, ll, rh, rl, start, stop):
                nc.tensor.matmul(out_, lh, rh, start=start, stop=False)
                nc.tensor.matmul(out_, lh, rl, start=False, stop=False)
                return nc.tensor.matmul(out_, ll, rh, start=False, stop=stop)

            def row_step(n, base, c, bank, start, stop, tau=None):
                if tau is not None:
                    pe.wait_ge(s_xlo, DC * tau + c + 1)
                pe.wait_ge(s_lo, n + 1)
                for tt in range(TT):
                    t = slice(tt * P, (tt + 1) * P)
                    for nh in range(2):
                        w = slice(nh * 512, (nh + 1) * 512)
                        ins = product(ps[:, bank + 2 * tt + nh, :], xhi[:, c, t], xlo[:, c, t],
                                      hi[:, base % HI, w], lo[:, base % LO, w], start, stop)
                ins.then_inc(s_used, 1)

            def col_step(n, base, out_, tau=None):
                pe.wait_ge(s_lo, n + 1)
                for c in range(DC):
                    if tau is not None:
                        pe.wait_ge(s_xlo, DC * tau + c + 1)
                    w = slice(c * P, (c + 1) * P)
                    ins = product(out_, hi[:, base % HI, w], lo[:, base % LO, w], xhi[:, c, :], xlo[:, c, :],
                                  c == 0, c == DC - 1)
                ins.then_inc(s_used, 1)

            def transposed(tau, src):
                for c in range(DC):
                    for tt in range(TT):
                        o = (c % 2) * SEQ + tt * P
                        ins = nc.tensor.transpose(ps[:, c // 2, o:o + P], src(tt)[:, c * P:(c + 1) * P], ident[:])
                    ins.then_inc(s_tp, 1)

            def norm_transposed(tau):
                xn["n"] += 2
                pe.wait_ge(s_xn, xn["n"])
                transposed(tau, lambda tt: XN[:, tt, :])

            def project_in(L):
                kind, tau = L["kind"], 3 * L["l"]
                for n in range(L["small"], L["in"]):
                    pe.wait_ge(s_xlo, DC * tau + 2)
                    col_step(n, n, ps[:, 0, 0:SEQ], tau)
                for g in range(GROUPS[kind]):
                    if g == 1:
                        pe.wait_ge(s_xlo, DC * (tau + 1))
                        if kind == "hgrn":
                            pe.wait_ge(s_lbc, 2)
                        else:
                            pe.wait_ge(s_da, HANDED[L["l"]][0] + 1)
                    if g >= 2:
                        pe.wait_ge(s_ev, L["ev"] + 4 * (g - 1))
                    for c in range(DC):
                        n = L["in"] + g * DC + c
                        row_step(n, n, c, BANKS[g % 2], c == 0, c == DC - 1, tau if g == 0 else None)
                        if kind == "hgrn" and n == L["in"]:
                            pe.wait_ge(s_lb, 1)
                            pe.wait_ge(s_xlo, DC * tau + 4)
                            for q in range(DC):
                                ins = nc.tensor.matmul(ps[:, q // 4, (q % 4) * P:(q % 4 + 1) * P],
                                                       LBC[:, 48 + q:49 + q].broadcast_to([P, P]), ident[:],
                                                       start=True, stop=True)
                            ins.then_inc(s_lbr, 1)
                        if kind == "gla" and n == L["in"] + 1:
                            pe.wait_ge(s_wup, 16)
                            pe.wait_ge(s_low, 2)
                            pe.wait_ge(s_xlo, DC * (tau + 1))
                            for tt in range(TT):
                                ins = nc.tensor.matmul(ps[:, 2 + tt, :], LOWT[0:GLA_RANK + 1, tt * P:(tt + 1) * P],
                                                       WUP[0:GLA_RANK + 1, :], start=True, stop=True)
                            ins.then_inc(s_z, 1)

            def chunks_transposed(L, banks):
                for b in banks:
                    if b == 0 and L["kind"] == "fox":
                        pe.wait_ge(s_lfc, L["fox"] + 1)
                    for c in (2 * b, 2 * b + 1):
                        for tt in range(TT):
                            o = (c % 2) * SEQ + tt * P
                            ins = nc.tensor.transpose(ps[:, b, o:o + P], PR[:, tt, c * P:(c + 1) * P], ident[:])
                    ins.then_inc(s_tq, 1)

            def fox(L):
                f = L["fox"]
                b0 = FOX_HEADS * f
                pe.wait_ge(s_qk, 4 * (f + 1))
                pe.wait_ge(s_ev, L["ev"] + 12)
                chunks_transposed(L, (4, 5, 6, 7))
                pe.wait_ge(s_ev, L["ev"] + 16)
                pe.wait_ge(s_lf, f + 1)
                for tt in range(TT):
                    ins = nc.tensor.transpose(ps[:, 0, 16 * tt:16 * tt + 16], LFB[0:16, tt * P:(tt + 1) * P],
                                              ident[0:16, 0:16])
                ins.then_inc(s_lft, 1)
                chunks_transposed(L, (1, 2, 3, 0))
                pe.wait_ge(s_tqd, L["tq"] + 4)
                pe.wait_ge(s_tqa, L["tq"] + 4)

                def logits(h):
                    if h >= 2:
                        pe.wait_ge(s_exp, b0 + h - 1)
                    c, r = h // 2, slice(64 * (h % 2), 64 * (h % 2) + 64)
                    s0, s1 = ps[:, h % 2, 0:P], ps[:, h % 2, P:3 * P]

                    def gates(out_, tt, n):
                        nc.tensor.matmul(out_, lfh[:, tt, h:h + 1].broadcast_to([P, P]), nur[:, 0:n],
                                         start=False, stop=False)
                        nc.tensor.matmul(out_, lfl[:, tt, h:h + 1].broadcast_to([P, P]), nur[:, 0:n],
                                         start=False, stop=False)

                    nc.tensor.matmul(s0, TR[r, c, 0:P], TR[r, 8 + c, 0:P], start=True, stop=False)
                    gates(s0, 0, P)
                    nc.tensor.matmul(s0, identb[:], maskb[:], start=False, stop=True)
                    nc.tensor.matmul(s1, TR[r, c, P:2 * P], TR[r, 8 + c, :], start=True, stop=False)
                    gates(s1, 0, 2 * P)
                    gates(s1[:, P:2 * P], 1, P)
                    nc.tensor.matmul(s1[:, P:2 * P], identb[:], maskb[:], start=False, stop=True).then_inc(s_s, 1)

                logits(0)
                for h in range(FOX_HEADS + 1):
                    if h + 1 < FOX_HEADS:
                        logits(h + 1)
                    if h < FOX_HEADS:
                        pe.wait_ge(s_exp, b0 + h + 1)
                        if h >= 2:
                            pe.wait_ge(s_pte, b0 + h - 1)
                        for b in range(3):
                            ins = nc.tensor.transpose(ps[:, 2 + h % 2, b * P:(b + 1) * P],
                                                      PB[:, h % 2, b * P:(b + 1) * P], ident[:])
                        ins.then_inc(s_pt, 1)
                    if h >= 1:
                        g = h - 1
                        pe.wait_ge(s_pte, b0 + g + 1)
                        if g >= 2:
                            pe.wait_ge(s_o, b0 + g - 1)
                        v = lambda tt: PR[:, tt, 2 * D + g * FOX_DH:2 * D + (g + 1) * FOX_DH]
                        o = ps[:, 4 + g % 2, 0:2 * FOX_DH]
                        pt = lambda b: PTB[:, g % 2, b * P:(b + 1) * P]
                        nc.tensor.matmul(o[:, 0:FOX_DH], pt(0), v(0), start=True, stop=True)
                        nc.tensor.matmul(o[:, FOX_DH:], pt(1), v(0), start=True, stop=False)
                        nc.tensor.matmul(o[:, FOX_DH:], pt(2), v(1), start=False, stop=True).then_inc(s_pv, 1)
                pe.wait_ge(s_o, b0 + FOX_HEADS)
                transposed(3 * L["l"] + 1, lambda tt: PR[:, tt, 3 * D:4 * D])

            def linear(L):
                kind, H_ = L["kind"], HEADS[L["kind"]]
                dv = D // H_
                G, nb = GROUPS[kind], H_ // 2
                pe.wait_ge(s_ev, L["ev"] + 4 * (G - 1))
                if kind == "hgrn":
                    pe.wait_ge(s_hk, 2)
                chunks_transposed(L, range(nb, 2 * nb))
                if kind == "hgrn":
                    pe.wait_ge(s_ev, L["ev"] + 4 * G)
                chunks_transposed(L, range(nb))
                pe.wait_ge(s_ev, L["ev"] + 4 * G)
                pe.wait_ge(s_tqd, L["tq"] + nb)
                pe.wait_ge(s_tqa, L["tq"] + nb)
                pe.wait_ge(s_mc, L["l"] + 1)
                if kind == "gla":
                    pe.wait_ge(s_lg, 1)
                else:
                    pe.wait_ge(s_ab, HANDED[L["l"]][1] + 3)
                vg = (GROUPS[kind] - 2) * D
                U = 2 * H_

                def decays(u):
                    g, h, tt = L["gu"] + u, u // 2, u % 2
                    if u >= 1:
                        pe.wait_ge(s_gx, g)
                    for b in range(2):
                        ins = nc.tensor.matmul(ps[:, b, :], LG[:, tt, h * P:(h + 1) * P],
                                               MC[:, tt + 4 * b:tt + 4 * b + 4, :], start=True, stop=True)
                    ins.then_inc(s_gd, 1)

                def scores(u):
                    g, h, tt = L["gu"] + u, u // 2, u % 2
                    lv = 1 - tt
                    pe.wait_ge(s_gq, g + 1)
                    pe.wait_ge(s_gk, g + 1)
                    if u >= 2:
                        pe.wait_ge(s_gr, g - 1)
                    b = 2 + 2 * (u % 2)
                    if tt == 1:
                        nc.tensor.matmul(ps[:, 6, (h % 2) * P:(h % 2 + 1) * P], KS[:, h % 2, :],
                                         QD[:, 1, LEVELS, :], start=True, stop=True)
                    for l in range(LEVELS):
                        nc.tensor.matmul(ps[:, b + l // 4, (l % 4) * P:(l % 4 + 1) * P], KD[:, u % 2, lv + l, :],
                                         QD[:, u % 2, lv + l, :], start=True, stop=True)
                    t = slice(tt * P, (tt + 1) * P)
                    nc.tensor.matmul(ps[:, b + 1, 3 * P:4 * P], TR[:, H_ + h, t], TR[:, h, t],
                                     start=True, stop=True).then_inc(s_gs, 1)

                def values(u):
                    g, h, tt = L["gu"] + u, u // 2, u % 2
                    pe.wait_ge(s_gr, g + 1)
                    if u >= 1:
                        pe.wait_ge(s_go, g)
                    o = ps[:, 7, (u % 2) * 256:(u % 2) * 256 + dv]
                    v = lambda t: PR[:, t, vg + h * dv:vg + (h + 1) * dv]
                    ins = nc.tensor.matmul(o, ST[:, u % 2, :], v(tt), start=True, stop=tt == 0)
                    if tt == 1:
                        ins = nc.tensor.matmul(o, ST[:, 2 + h % 2, :], v(0), start=False, stop=True)
                    ins.then_inc(s_gp, 1)

                decays(0)
                for u in range(U + 1):
                    if u + 1 < U:
                        decays(u + 1)
                    if u < U:
                        scores(u)
                    if u >= 1:
                        values(u - 1)
                norm_transposed(3 * L["l"] + 1)

            def key_scores(L, tt):
                for b in range(4):
                    for q in range(4):
                        c = 4 * b + q
                        ins = nc.tensor.matmul(ps[:, b, q * NK:(q + 1) * NK], QT[:, c, tt * P:(tt + 1) * P],
                                               SK[:, c * NK:(c + 1) * NK], start=True, stop=True)
                    ins.then_inc(s_sc, 1)

            def g_product(i, s, oh, at):
                pe.wait_ge(s_ohg, i * 4 + (oh + s + 1))
                pe.wait_ge(s_hm, i * 4 + (at + s + 1))
                for t in range(4):
                    o = ps[:, 6 + s % 2, t * HALF:(t + 1) * HALF]
                    for q in range(2):
                        ins = nc.tensor.matmul(o, oh1[:, s % 2, t, :], ohg[:, s % 2, q, t, :],
                                               start=q == 0, stop=q == 1)
                ins.then_inc(s_g, 1)

            xn = {"n": 0}
            for L in PLAN.layers:
                l, kind = L["l"], L["kind"]
                norm_transposed(3 * l)
                project_in(L)
                if kind == "fox":
                    fox(L)
                else:
                    linear(L)
                for c in range(DC):
                    row_step(L["out"] + c, L["out"] + c, c, BANKS[0], c == 0, c == DC - 1, 3 * l + 1)
                norm_transposed(3 * l + 2)
                c0 = (PH + HALF) * l
                for c in range(2 * PH):
                    if c % 2 == 0 and c >= 4:
                        pe.wait_ge(s_cev, c0 + c // 2 - 1)
                    n = L["wq"] + c
                    col_step(n, n, ps[:, 4 + c // 2 % 2, (c % 2) * SEQ:(c % 2 + 1) * SEQ],
                             3 * l + 2 if c == 0 else None)
                pe.wait_ge(s_cev, c0 + PH)
                pe.wait_ge(s_sk, 16 * (l + 1))
                key_scores(L, 0)
                n0 = L["u"]
                c0 += PH

                def u_steps(j0, j1, with_g=False):
                    with pe.Fori(j0 // 4, j1 // 4) as i:
                        for s in range(4):
                            if s % 2 == 0:
                                pe.wait_ge(s_cev, i * 2 + (c0 + s // 2 - 1))
                            col_step(i * 4 + (n0 + s), n0 + s, ps[:, 4 + s // 2, (s % 2) * SEQ:(s % 2 + 1) * SEQ])
                            if with_g:
                                g_product(i, s, NCH * l - HALF, (NCH + 2) * l - HALF)

                u_steps(0, SCORES_AT)
                pe.wait_ge(s_rt, TT * l + 1)
                key_scores(L, 1)
                u_steps(SCORES_AT, HALF)
                pe.wait_ge(s_route, TT * (l + 1))
                for w in range(3):
                    for tt in range(TT):
                        o = (w % 2) * SEQ + tt * P
                        ins = nc.tensor.transpose(ps[:, 6 + w // 2, o:o + P], ROUT[tt][:, w, :], ident[:])
                    if w:
                        ins.then_inc(s_g, 1)
                u_steps(HALF, NCH, with_g=True)
                for half in range(2):
                    n0 = L["v"] + half * HALF

                    def v_step(i, s, k):
                        pe.wait_ge(s_wlo, k + (NCH * l + half * HALF + 1))
                        row_step(k + n0, n0 + s, s, 0, isinstance(k, int) and half == 0 and k == 0,
                                 isinstance(k, int) and half == 1 and k == HALF - 1)
                        if half == 0:
                            g_product(i, s, NCH * l + HALF, (NCH + 2) * l + HALF)

                    steps(pe, HALF, v_step, first=half == 0)


def slabs_of_rows(w):
    n = w.shape[1] // D
    return w.reshape(DC, P, n, D).transpose(2, 0, 1, 3).reshape(n * DC, P, D)


def slabs_of_columns(w):
    n = w.shape[1] // P
    return w.reshape(DC, P, n, P).transpose(2, 1, 0, 3).reshape(n, P, D)


def narrow_slab(w):
    return slabs_of_columns(np.concatenate([w, np.zeros((D, P - w.shape[1]), w.dtype)], axis=1))


def kernel(x, norm_mix, norm_ffn, fox_w_in, fox_b_f, fox_q_gain, fox_k_gain, fox_w_out,
           gla_w_in, gla_w_up, gla_b_alpha, gla_out_gain, gla_w_out,
           hgrn_w_in, hgrn_lb_logits, hgrn_out_gain, hgrn_w_out,
           peer_w_q, peer_sub_keys, peer_u, peer_v):
    import concourse.bacc as bacc
    from concourse.bass_utils import run_bass_kernel_spmd

    stream = np.empty((PLAN.slabs, P, D), np.float32)

    def put(n, slabs):
        stream[n:n + len(slabs)] = slabs

    w_in = {"fox": fox_w_in, "gla": gla_w_in, "hgrn": hgrn_w_in}
    w_out = {"fox": fox_w_out, "gla": gla_w_out, "hgrn": hgrn_w_out}
    for L in PLAN.layers:
        l, kind = L["l"], L["kind"]
        which = L["fox"] if kind == "fox" else 0
        wi, wo = np.asarray(w_in[kind][which]), np.asarray(w_out[kind][which])
        wide = GROUPS[kind] * D
        if SMALL[kind]:
            put(L["small"], narrow_slab(wi[:, wide:]))
        put(L["in"], slabs_of_rows(wi[:, :wide]))
        put(L["out"], slabs_of_rows(wo))
        put(L["wq"], slabs_of_columns(np.asarray(peer_w_q[l])))
        u = np.asarray(peer_u[l]).reshape(P, NCH, DC, P)
        put(L["u"], u.transpose(1, 3, 2, 0).reshape(NCH, P, D))
        put(L["v"], np.asarray(peer_v[l]).reshape(P, NCH, D).transpose(1, 0, 2))

    def columns(a):
        return np.asarray(a).reshape(-1, DC, P).transpose(2, 0, 1).reshape(P, -1)

    prm = np.zeros((P, NPRM), np.float32)
    for name, a in (("mix", norm_mix), ("ffn", norm_ffn), ("gla_gain", gla_out_gain), ("hgrn_gain", hgrn_out_gain),
                    ("lb", hgrn_lb_logits)):
        c = columns(a)
        prm[:, PRM[name]:PRM[name] + c.shape[1]] = c
    for name, a in (("qg", fox_q_gain), ("kg", fox_k_gain)):
        a = np.asarray(a)
        prm[:, PRM[name]:PRM[name] + 2] = np.concatenate([a, a], axis=1).T
    prm[0:FOX_HEADS, PRM["bf"]:PRM["bf"] + 2] = np.asarray(fox_b_f).T
    wup = np.concatenate([np.asarray(gla_w_up[0]), np.asarray(gla_b_alpha)], axis=0)
    sk = np.asarray(peer_sub_keys).transpose(0, 4, 1, 2, 3).reshape(DEPTH, P, 2 * PH * NK)

    nc = bacc.Bacc("TRN2", target_bir_lowering=False, num_devices=1)
    arrays = {"stream": stream, "x": np.asarray(x).reshape(SEQ, D), "prm": prm, "wup": wup, "sk": sk}
    aps = {k: nc.dram_tensor(f"in_{k}", a.shape, F32, kind="ExternalInput").ap() for k, a in arrays.items()}
    out = nc.dram_tensor("out_0", (SEQ, D), F32, kind="ExternalOutput").ap()
    build(nc, aps["stream"], aps["x"], aps["prm"], aps["wup"], aps["sk"], out)
    r = run_bass_kernel_spmd(nc, [{f"in_{k}": np.ascontiguousarray(a) for k, a in arrays.items()}], core_ids=[0])
    return r.results[0]["out_0"].reshape(1, SEQ, D)
```

```python
from contextlib import ExitStack

import numpy as np

import concourse.bass as bass
from concourse import mybir

ALU = mybir.AluOpType
ACT = mybir.ActivationFunctionType
F32 = mybir.dt.float32
F32R = mybir.dt.float32r
U32 = mybir.dt.uint32
BF16 = mybir.dt.bfloat16
F16 = mybir.dt.float16
AX = mybir.AxisListType

P = 128
D = 1024
SEQ = 256
TT = SEQ // P
DC = D // P
DEPTH = 4
EPS = 1e-6
NEG = -1e30
FOX_HEADS, FOX_DH = 16, 64
GLA_HEADS, GLA_DK, GLA_RANK, GLA_TAU = 4, 128, 16, 16.0
HGRN_HEADS = 8
PH, NK, TOPK = 8, 128, 16
GATE_SCALE = 2.0 ** 14
NCH = NK
HALF = NCH // 2
LEVELS = 7

RAW, HI, LO = 4, 4, 2
EARLY = range(6)
LATE = range(6, DC)

SCORES_AT = 24
EXP_AT = 60

KIND = ["fox", "gla", "hgrn", "fox"]
GROUPS = {"fox": 4, "gla": 3, "hgrn": 4}
SMALL = {"fox": 1, "gla": 1, "hgrn": 0}
POWERS = 6
HEADS = {"fox": FOX_HEADS, "gla": GLA_HEADS, "hgrn": HGRN_HEADS}


HANDED = [(0, 0), (1, 1), (2, 2), (5, 5)]
BANKS = (4, 0)


class Plan:

    def __init__(self):
        self.layers = []
        n = ev = tq = gu = fox = pw = 0
        for l, kind in enumerate(KIND):
            L = {"l": l, "kind": kind, "ev": ev, "tq": tq, "gu": gu, "fox": fox, "lin": l - fox, "pw": pw}
            L["small"] = n
            n += SMALL[kind]
            L["in"] = n
            n += GROUPS[kind] * DC
            L["out"] = n
            n += DC
            L["wq"] = n
            n += 2 * PH
            L["u"] = n
            n += NCH
            L["v"] = n
            n += NCH
            L["end"] = n
            ev += 4 * GROUPS[kind]
            tq += 2 if kind == "gla" else 4
            if kind == "fox":
                fox += 1
            else:
                gu += 2 * HEADS[kind]
            pw += POWERS
            self.layers.append(L)
        self.slabs = n


PLAN = Plan()

PRM = {}
_at = 0
for _name, _w in (("mix", DEPTH * DC), ("ffn", DEPTH * DC), ("gla_gain", DC), ("hgrn_gain", DC),
                  ("qg", 2), ("kg", 2), ("bf", 2), ("lb", DEPTH * DC)):
    PRM[_name] = _at
    _at += _w
NPRM = _at

O_P = 0
O_T = 8192
O_XN = 12288
O_LG = 14336
O_MC = 16384
O_MK = O_MC + 9 * P
O_ST = O_MK + 8 * P
O_SK = 20480
O_E = 22528
O_QD = 24576
O_KD = 26624
O_A = 28672
O_KS = 29696
O_SM = 30720
O_WUP = 32256
O_QT = 16384
O_CAND = 22528
O_EQ = 24576
O_TMP = 26624
O_RS = 28672


def build(nc, stream, x, prm_d, wup_d, sk_d, out):
    N = PLAN.slabs
    with ExitStack() as ctx:
        def sb(name, shape, dt=F32):
            return ctx.enter_context(nc.sbuf_tensor(name, shape, dt))

        def sem(name):
            return ctx.enter_context(nc.semaphore(name))

        resid = sb("resid", [P, TT, D])
        xhi = sb("xhi", [P, DC, SEQ], F32R)
        xlo = sb("xlo", [P, DC, SEQ], F32R)
        big = sb("big", [P, NCH * SEQ])
        raw = sb("raw", [P, RAW, D])
        hi = sb("hi", [P, HI, D], F32R)
        lo = sb("lo", [P, LO, D], F32R)
        ident = sb("ident", [P, P])
        iota = sb("iota", [P, P])
        prm = sb("prm", [P, NPRM])
        e1T = sb("e1T", [P, SEQ])
        e2T = sb("e2T", [P, SEQ])
        gate2 = sb("gate2", [P, 2, SEQ], F16)
        oh1 = sb("oh1", [P, 2, 4, P], F16)
        oh2 = sb("oh2", [P, 2, 4, HALF], F16)
        ohg = sb("ohg", [P, 2, 2, 4, HALF], F16)
        nur = sb("nur", [P, 2 * P], F32R)
        maskb = sb("maskb", [P, P], BF16)
        identb = sb("identb", [P, P], BF16)
        lfh = sb("lfh", [P, TT, FOX_HEADS], F32R)
        lfl = sb("lfl", [P, TT, FOX_HEADS], F32R)
        minus_half = sb("minus_half", [P, 64])
        sm = sb("sm", [P, 64])
        ps = ctx.enter_context(nc.psum_tensor("ps", [P, 8, 512], F32))

        s_raw = [sem(f"s_raw{i}") for i in range(RAW)]
        s_hi, s_lo, s_used = sem("s_hi"), sem("s_lo"), sem("s_used")
        s_x, s_prm, s_const = [sem(f"s_x{tt}") for tt in range(TT)], sem("s_prm"), sem("s_const")
        s_xn, s_tp, s_xhi, s_xlo = sem("s_xn"), sem("s_tp"), sem("s_xhi"), sem("s_xlo")
        s_fin, s_res, s_ssa, s_ss, s_sq, s_xa = (sem(n) for n in (
            "s_fin", "s_res", "s_ssa", "s_ss", "s_sq", "s_xa"))
        s_xh = sem("s_xh")
        s_ev = sem("s_ev")
        s_mc = sem("s_mc")
        s_tq, s_tqd, s_tqa = sem("s_tq"), sem("s_tqd"), sem("s_tqa")
        s_da, s_ab = sem("s_da"), sem("s_ab")
        s_lf, s_lft, s_lfc, s_qk = sem("s_lf"), sem("s_lft"), sem("s_lfc"), sem("s_qk")
        s_s, s_mx, s_exp, s_pt, s_pte, s_pv, s_o = (sem(n) for n in (
            "s_s", "s_mx", "s_exp", "s_pt", "s_pte", "s_pv", "s_o"))
        s_low, s_wup, s_z, s_lg = sem("s_low"), sem("s_wup"), sem("s_z"), sem("s_lg")
        s_lb, s_lbr, s_lbc, s_hk = sem("s_lb"), sem("s_lbr"), sem("s_lbc"), sem("s_hk")
        s_gd, s_gx, s_gq, s_gk, s_gs, s_gm, s_gr, s_gp, s_go = (sem(n) for n in (
            "s_gd", "s_gx", "s_gq", "s_gk", "s_gs", "s_gm", "s_gr", "s_gp", "s_go"))
        s_sk, s_sc, s_rt, s_ge, s_gn, s_route = (sem(n) for n in (
            "s_sk", "s_sc", "s_rt", "s_ge", "s_gn", "s_route"))
        s_cev = sem("s_cev")
        s_whi, s_wlo = sem("s_whi"), sem("s_wlo")
        s_eq, s_ohg, s_g, s_hm = sem("s_eq"), sem("s_ohg"), sem("s_g"), sem("s_hm")
        s_dve, s_act, s_pc = sem("s_dve"), sem("s_act"), sem("s_pc")
        s_done, s_out = sem("s_done"), sem("s_out")

        block = ctx.enter_context(nc.Block())

        def B(off, n):
            return big[:, off:off + n]

        PR = B(O_P, 8192).rearrange("p (t n) -> p t n", t=TT)
        TR = B(O_T, 4096).rearrange("p (c t) -> p c t", t=SEQ)
        XN = B(O_XN, 2048).rearrange("p (t n) -> p t n", t=TT)
        LG = B(O_LG, 2048).rearrange("p (t n) -> p t n", t=TT)
        MC = B(O_MC, 9 * P).rearrange("p (l t) -> p l t", t=P)
        MK = B(O_MK, 8 * P).rearrange("p (l t) -> p l t", t=P)
        ST = B(O_ST, 4 * P).rearrange("p (b t) -> p b t", t=P)
        EB = B(O_E, 2048).rearrange("p (b l t) -> p b l t", b=2, t=P)
        QD = B(O_QD, 2048).rearrange("p (b l t) -> p b l t", b=2, t=P)
        KD = B(O_KD, 2048).rearrange("p (b l t) -> p b l t", b=2, t=P)
        AM = B(O_A, 1024).rearrange("p (l t) -> p l t", t=P)
        KS = B(O_KS, 256).rearrange("p (b t) -> p b t", t=P)
        BIG0 = B(O_MC, 256)
        LFT = B(O_SM, 256)
        LFA = B(O_SM + 256, 256)
        LFB = B(O_SM + 512, 256)
        NM = B(O_SM + 800, 32).rearrange("p (h t) -> p h t", t=TT)
        RSUM = B(O_SM + 832, 32).rearrange("p (h t) -> p h t", t=TT)
        RL = B(O_SM + 864, 32).rearrange("p (h t) -> p h t", t=TT)
        QS = B(O_SM + 896, 64)
        QR = B(O_SM + 960, 64)
        PB = B(O_KD, 768).rearrange("p (b s) -> p b s", b=2)
        PTB = B(O_KD + 768, 768).rearrange("p (b s) -> p b s", b=2)
        LOWT = B(O_SM, 256)
        WUP = B(O_WUP, 512)
        LBC = B(O_SM + 256, 64)
        SCR = B(O_E, 2048)
        SCR2 = B(O_QD, 2048).rearrange("p (t n) -> p t n", t=TT)
        LBR = B(O_KD, 1024)
        OML = B(O_KD + 1024, 1024)
        H = big[:, :].rearrange("p (j t) -> p j t", t=SEQ)
        QT = B(O_QT, 4096).rearrange("p (c t) -> p c t", t=SEQ)
        SK = B(O_SK, 2048)
        CAND = B(O_CAND, 2048)
        EQ = B(O_EQ, 2048)
        TMP = B(O_TMP, 2048).rearrange("p (c k) -> p c k", k=NK)
        VAL = B(O_RS, 256).rearrange("p (c k) -> p c k", k=TOPK)
        IDX = B(O_RS + 256, 256).rearrange("p (c k) -> p c k", k=TOPK)
        IDF = B(O_RS + 512, 256).rearrange("p (c k) -> p c k", k=TOPK)
        BESTS = [B(O_RS + o, 128).rearrange("p (h k) -> p h k", k=TOPK) for o in (768, 2320)]
        POS = B(O_RS + 896, 128).rearrange("p (h k) -> p h k", k=TOPK)
        PAB = B(O_RS + 1024, 256).rearrange("p (s c) -> p s c", s=2)
        PAF = B(O_RS + 1280, 256).rearrange("p (s c) -> p s c", s=2)
        ROUT = [B(O_RS + 1536 + 3 * P * t, 3 * P).rearrange("p (w c) -> p w c", w=3) for t in range(TT)]
        ZS = B(O_RS + 2304, 16)
        EXS = [B(O_RS + o, 128).rearrange("p (h k) -> p h k", k=TOPK) for o in (2448, 2576)]

        def steps(eng, n, body, first=False):
            lo4, hi4 = (1 if first else 0), n // 4 - 1
            if first:
                for s in range(4):
                    body(0, s, s)
            with eng.Fori(lo4, hi4) as i:
                for s in range(4):
                    body(i, s, i * 4 + s)
            for s in range(4):
                body(hi4, s, 4 * hi4 + s)

        def early_heads(L):
            return HEADS[L["kind"]] * len(EARLY) // DC

        def chunk(j):
            return H[:, j, :] if isinstance(j, int) else H[:, bass.ds(j, 1), :].rearrange("p c t -> p (c t)")

        @block.sync
        def _(sp):
            for tt in range(TT):
                sp.dma_start(resid[:, tt, :], x[tt * P:(tt + 1) * P, :]).then_inc(s_x[tt], 16)
            for s in range(RAW):
                sp.dma_start(raw[:, s, :], stream[s]).then_inc(s_raw[s], 16)
            full = N // RAW

            def load(n, s):
                sp.wait_ge(s_lo, n - RAW + 1)
                sp.dma_start(raw[:, s, :], stream[bass.ds(n, 1)].rearrange("o p c -> p (o c)")
                             if not isinstance(n, int) else stream[n]).then_inc(s_raw[s], 16)

            with sp.Fori(1, full) as i:
                for s in range(RAW):
                    load(i * RAW + s, s)
            for n in range(full * RAW, N):
                load(n, n % RAW)
            sp.wait_ge(s_done, 1)
            sp.dma_start(out.rearrange("(t p) d -> p t d", p=P), resid[:]).then_inc(s_out, 16)
            sp.wait_ge(s_out, 16)

        @block.gpsimd
        def _(pool):
            chain = [0]

            def link(ins):
                chain[0] += 1
                ins.then_inc(s_pc, 1)
                pool.wait_ge(s_pc, chain[0])

            pool.dma_start(prm[:], prm_d).then_inc(s_prm, 16)
            link(nc.gpsimd.memset(ident[:], 0.0))
            nc.gpsimd.affine_select(out=ident[:], in_=ident[:], compare_op=ALU.not_equal, fill=1.0,
                                    base=0, pattern=[[-1, P]], channel_multiplier=1).then_inc(s_const, 1)
            pool.wait_ge(s_const, 1)
            link(nc.gpsimd.memset(minus_half[:], -0.5))
            link(nc.gpsimd.tensor_copy(identb[:], ident[:]))
            link(nc.gpsimd.memset(BIG0, -1.0))
            link(nc.gpsimd.affine_select(out=BIG0[:, 0:P], in_=BIG0[:, 0:P], compare_op=ALU.is_ge, fill=0.0,
                                         base=0, pattern=[[1, P]], channel_multiplier=-1))
            link(nc.gpsimd.tensor_copy(nur[:], BIG0))
            link(nc.gpsimd.memset(maskb[:], 0.0))
            link(nc.gpsimd.affine_select(out=maskb[:], in_=maskb[:], compare_op=ALU.is_ge, fill=NEG,
                                         base=0, pattern=[[-1, P]], channel_multiplier=1))
            nc.gpsimd.iota(iota[:], pattern=[[1, P]], base=0, channel_multiplier=0,
                           allow_small_or_imprecise_dtypes=True).then_inc(s_const, 1)

            def keep(ap, pattern, base, cm):
                link(nc.gpsimd.affine_select(out=ap, in_=ap, compare_op=ALU.is_ge, fill=0.0,
                                             base=base, pattern=pattern, channel_multiplier=cm))

            norms = [0]

            def norm_power(out_, in_):
                norms[0] += 1
                pool.wait_ge(s_ss, norms[0])
                nc.gpsimd.tensor_tensor(out_, in_, minus_half[:, 0:in_.shape[1]], ALU.pow).then_inc(s_sq, 1)

            def split_first(n0):
                for n in (n0, n0 + 1):
                    if n:
                        pool.wait_ge(s_lo, n)
                    pool.wait_ge(s_hi, n + 1)
                    if n >= LO:
                        pool.wait_ge(s_used, n - LO + 1)
                    nc.gpsimd.tensor_tensor(lo[:, n % LO, :], raw[:, n % RAW, :], hi[:, n % HI, :],
                                            ALU.subtract).then_inc(s_lo, 1)

            def linear_constants():
                link(nc.gpsimd.memset(MC, 1.0))
                link(nc.gpsimd.memset(MK, 0.0))
                keep(MC[:, 0, :], [[-1, P]], -1, 1)
                keep(MC[:, 8, :], [[1, P]], 0, -1)
                for l in range(LEVELS):
                    h = 1 << l
                    v = MC[:, 1 + l, :].rearrange("p (b s x) -> p b s x", s=2, x=h)
                    m = MK[:, l, :].rearrange("p (b s x) -> p b s x", s=2, x=h)
                    nb = P // (2 * h)
                    pat = [[2 * h, nb], [1, h]]
                    neg = [[-2 * h, nb], [-1, h]]
                    blk = [[2 * h, nb], [0, h]]
                    nblk = [[-2 * h, nb], [0, h]]
                    keep(v[:, :, 1, :], nblk, -h, 1)
                    keep(v[:, :, 1, :], pat, h, -1)
                    keep(v[:, :, 0, :], neg, -1, 1)
                    keep(v[:, :, 0, :], blk, h - 1, -1)
                    link(nc.gpsimd.memset(m[:, :, 1, :], 1.0))
                    keep(m[:, :, 1, :], nblk, 0, 1)
                    keep(m[:, :, 1, :], blk, h - 1, -1)
                link(nc.gpsimd.affine_select(out=MK[:, 7, :], in_=MK[:, 7, :], compare_op=ALU.not_equal,
                                             fill=1.0, base=0, pattern=[[-1, P]], channel_multiplier=1))

            def decayed_keys(L):
                H_ = HEADS[L["kind"]]
                for u in range(2 * H_):
                    h, tt, g = u // 2, u % 2, L["gu"] + u
                    pool.wait_ge(s_gx, g + 1)
                    if u >= 2:
                        pool.wait_ge(s_gs, g - 1)
                    if u == 0:
                        pool.wait_ge(s_tqa, L["tq"] + (2 if L["kind"] == "gla" else 4))
                    kT = TR[:, H_ + h, tt * P:(tt + 1) * P]
                    if tt == 0:
                        nc.gpsimd.tensor_tensor(KS[:, h % 2, :], EB[:, u % 2, 0, :], kT, ALU.mult)
                    lv = 1 - tt
                    nc.gpsimd.tensor_tensor(KD[:, u % 2, lv:lv + LEVELS, :], EB[:, u % 2, lv:lv + LEVELS, :],
                                            kT.unsqueeze(1).broadcast_to([P, LEVELS, P]),
                                            ALU.mult).then_inc(s_gk, 1)

            for L in PLAN.layers:
                l, kind = L["l"], L["kind"]
                if l:
                    pool.wait_ge(s_wlo, NCH * l)
                pool.dma_start(SK, sk_d[l]).then_inc(s_sk, 16)
                if kind == "gla":
                    pool.dma_start(WUP[0:GLA_RANK + 1, :], wup_d).then_inc(s_wup, 16)
                norm_power(sm[:, 4:5], sm[:, 2:3])
                norm_power(sm[:, 5:6], sm[:, 3:4])
                split_first(L["small"])
                if kind != "fox":
                    linear_constants()
                nc.gpsimd.memset(sm[:, 60:61], 0.0).then_inc(s_mc, 1)
                if kind == "fox":
                    norm_power(QR[:, 0:32], QS[:, 0:32])
                    norm_power(QR[:, 32:64], QS[:, 32:64])
                else:
                    decayed_keys(L)
                    n, m = 2 * HEADS[kind], 2 * early_heads(L)
                    norm_power(sm[:, 40:40 + m], sm[:, 24:24 + m])
                    norm_power(sm[:, 40 + m:40 + n], sm[:, 24 + m:24 + n])
                norm_power(sm[:, 4:5], sm[:, 2:3])
                norm_power(sm[:, 5:6], sm[:, 3:4])
                split_first(L["wq"])
                n0 = L["u"]
                pool.wait_ge(s_lo, n0)
                with pool.Fori(0, HALF // 4) as i:
                    for s in range(4):
                        n = i * 4 + (n0 + s)
                        pool.wait_ge(s_hi, n + 1)
                        pool.wait_ge(s_used, n - LO + 1)
                        nc.gpsimd.tensor_tensor(lo[:, (n0 + s) % LO, :], raw[:, (n0 + s) % RAW, :],
                                                hi[:, (n0 + s) % HI, :], ALU.subtract).then_inc(s_lo, 1)
                n = n0 + HALF
                pool.wait_ge(s_hi, n + 1)
                pool.wait_ge(s_used, n - LO + 1)
                nc.gpsimd.tensor_tensor(lo[:, n % LO, :], raw[:, n % RAW, :], hi[:, n % HI, :],
                                        ALU.subtract).then_inc(s_lo, 1)
                def split_w(k, n, s):
                    pool.wait_ge(s_whi, n)
                    nc.gpsimd.tensor_tensor(xlo[:, s, :], chunk(k), xhi[:, s, :], ALU.subtract).then_inc(s_wlo, 1)

                for half in range(2):
                    def g_step(i, s, k):
                        pool.wait_ge(s_eq, k + (HALF * (2 * l + half) + 1))
                        for q in range(2):
                            g = gate2[:, q, bass.ds(i * 16 + 4 * s, 4)].unsqueeze(2).broadcast_to([P, 4, HALF])
                            ins = nc.gpsimd.tensor_tensor(ohg[:, s % 2, q], oh2[:, s % 2], g, ALU.mult)
                        ins.then_inc(s_ohg, 1)
                        if half == 1 and isinstance(k, int) and k == 0:
                            pool.wait_ge(s_wlo, NCH * l + 1)
                        if half == 1 and not (isinstance(k, int) and k == HALF - 1):
                            split_w(k + 1, k + (NCH * l + 2), (s + 1) % 4)

                    steps(pool, HALF, g_step, first=half == 1)

        @block.scalar
        def _(act):
            chain = [0]

            def link(ins):
                chain[0] += 1
                ins.then_inc(s_act, 1)
                act.wait_ge(s_act, chain[0])

            def round_slab(n, base):
                k = base % RAW
                act.wait_ge(s_raw[k], landed(n, base))
                if not (isinstance(n, int) and n < HI):
                    act.wait_ge(s_used, n - HI + 1)
                nc.scalar.copy(hi[:, base % HI, :], raw[:, k, :]).then_inc(s_hi, 1)

            def landed(n, base):
                return 16 * (n // RAW + 1) if isinstance(n, int) else (n + (RAW - base % RAW)) * (16 // RAW)

            def transposed(tau, gain, chunks=range(DC)):
                for c in chunks:
                    act.wait_ge(s_tp, DC * tau + (c | 1) + 1)
                    nc.scalar.activation(xhi[:, c, :], ps[:, c // 2, (c % 2) * SEQ:(c % 2 + 1) * SEQ], ACT.Copy,
                                         scale=1.0 if gain is None else prm[:, gain + c:gain + c + 1]
                                         ).then_inc(s_xhi, 1)

            def norm(r, power):
                act.wait_ge(s_res, 4 * r + 2)
                nc.scalar.activation(XN[:, 0, :], resid[:, 0, :], ACT.Square, accum_out=sm[:, 0:1]).then_inc(s_ssa, 1)
                act.wait_ge(s_res, 4 * r + 3)
                nc.scalar.activation(XN[:, 1, 0:512], resid[:, 1, 0:512], ACT.Square, accum_out=sm[:, 1:2])
                act.wait_ge(s_sq, power)
                nc.scalar.activation(XN[:, 0, :], resid[:, 0, :], ACT.Copy, scale=sm[:, 4:5]).then_inc(s_xa, 1)
                act.wait_ge(s_res, 4 * r + 4)
                nc.scalar.activation(XN[:, 1, 512:D], resid[:, 1, 512:D], ACT.Square,
                                     accum_out=sm[:, 6:7]).then_inc(s_ssa, 1)

            def evacuate(L, g):
                fn = ACT.Copy
                if L["kind"] == "fox" and g == 3:
                    fn = ACT.Sigmoid
                if L["kind"] == "gla" and g == 2 or L["kind"] == "hgrn" and g == 3:
                    fn = ACT.Silu
                if L["kind"] == "hgrn" and g == 1:
                    fn = ACT.Sigmoid
                act.wait_ge(s_used, L["in"] + DC * (g + 1))
                for tt in range(TT):
                    for nh in range(2):
                        nc.scalar.activation(PR[:, tt, g * D + nh * 512:g * D + (nh + 1) * 512],
                                             ps[:, BANKS[g % 2] + 2 * tt + nh, :], fn).then_inc(s_ev, 1)

            def project_in(L):
                G = GROUPS[L["kind"]]
                for n in range(L["small"] + 2, L["out"] + 2):
                    round_slab(n, n)
                    g, k = divmod(n - L["in"] - 2, DC)
                    if k == 0 and g >= 1:
                        evacuate(L, g - 1)
                    gates(L, n - L["in"])
                evacuate(L, G - 1)

            def gates(L, k):
                if L["kind"] == "fox" and k == 7:
                    act.wait_ge(s_da, ab["da"] + 1)
                    link(nc.scalar.activation(LFB[0:16, :], LFA[0:16, :], ACT.Exp))
                    nc.scalar.activation(LFA[0:16, :], LFB[0:16, :], ACT.Ln, bias=1.0).then_inc(s_ab, 1)
                    ab["da"] += 1
                if L["kind"] == "gla" and k == 7:
                    act.wait_ge(s_da, ab["da"] + 1)
                    link(nc.scalar.activation(XN[:, :, 0:512], XN[:, :, 0:512], ACT.Exp))
                    nc.scalar.activation(XN[:, :, 512:1024], XN[:, :, 0:512], ACT.Ln, bias=1.0).then_inc(s_ab, 1)
                    ab["da"] += 1
                if L["kind"] == "hgrn" and k in (27, 28):
                    tt = k - 27
                    act.wait_ge(s_da, ab["da"] + 1)
                    nc.scalar.activation(LG[:, tt, :], SCR2[:, tt, :], ACT.Ln).then_inc(s_ab, 1)
                    ab["da"] += 1

            def fox(L):
                f = L["fox"]
                for b in range(4):
                    act.wait_ge(s_tq, 2 * L["tq"] + 1 + b)
                    nc.scalar.activation(TR[:, 8 + 2 * b:10 + 2 * b, :].rearrange("p c t -> p (c t)"),
                                         ps[:, 4 + b, :], ACT.Copy,
                                         scale=prm[:, PRM["kg"] + f:PRM["kg"] + f + 1]).then_inc(s_tqa, 1)
                b0 = FOX_HEADS * f
                for h in range(FOX_HEADS + 1):
                    if h < FOX_HEADS:
                        act.wait_ge(s_mx, b0 + h + 1)
                        if h >= 2:
                            act.wait_ge(s_pt, b0 + h - 1)
                        nc.scalar.activation(PB[:, h % 2, 0:P], ps[:, h % 2, 0:P], ACT.Exp,
                                             bias=NM[:, h, 0:1], accum_out=RSUM[:, h, 0:1])
                        nc.scalar.activation(PB[:, h % 2, P:3 * P], ps[:, h % 2, P:3 * P], ACT.Exp,
                                             bias=NM[:, h, 1:2], accum_out=RSUM[:, h, 1:2]).then_inc(s_exp, 1)
                    if h >= 1:
                        g = h - 1
                        act.wait_ge(s_pt, b0 + g + 1)
                        if g >= 2:
                            act.wait_ge(s_pv, b0 + g - 1)
                        nc.scalar.copy(PTB[:, g % 2, :], ps[:, 2 + g % 2, 0:3 * P]).then_inc(s_pte, 1)

            def linear(L):
                kind, H_ = L["kind"], HEADS[L["kind"]]
                dv = D // H_
                nb = H_ // 2
                for b in range(nb):
                    act.wait_ge(s_tq, 2 * L["tq"] + 1 + b)
                    nc.scalar.activation(TR[:, H_ + 2 * b:H_ + 2 * b + 2, :].rearrange("p c t -> p (c t)"),
                                         ps[:, nb + b, :], ACT.Copy).then_inc(s_tqa, 1)
                U = 2 * H_
                for u in range(U + 2):
                    if u < U:
                        g = L["gu"] + u
                        act.wait_ge(s_gd, g + 1)
                        if u >= 2:
                            act.wait_ge(s_gq, g - 1)
                            act.wait_ge(s_gk, g - 1)
                        nc.scalar.activation(EB[:, u % 2].rearrange("p l t -> p (l t)"),
                                             ps[:, 0:2, :].rearrange("p b c -> p (b c)"), ACT.Exp).then_inc(s_gx, 1)
                    if u >= 2:
                        w = u - 2
                        g, h, tt = L["gu"] + w, w // 2, w % 2
                        act.wait_ge(s_gp, g + 1)
                        o = ps[:, 7, (w % 2) * 256:(w % 2) * 256 + dv]
                        nc.scalar.activation(XN[:, tt, h * dv:(h + 1) * dv], o, ACT.Square,
                                             accum_out=sm[:, 8 + w:9 + w])
                        nc.scalar.copy(PR[:, tt, h * dv:(h + 1) * dv], o).then_inc(s_go, 1)

            ab = {"da": 0}
            for L in PLAN.layers:
                l, kind = L["l"], L["kind"]
                norm(2 * l, L["pw"] + 1)
                if l == 0:
                    for n in range(2):
                        round_slab(n, n)
                    act.wait_ge(s_prm, 16)
                    act.wait_ge(s_const, 2)
                transposed(3 * l, PRM["mix"] + DC * l)
                if kind == "hgrn":
                    act.wait_ge(s_da, ab["da"] + 1)
                    nc.scalar.activation(LBC[:, 0:32], LBC[:, 0:32], ACT.Exp).then_inc(s_ab, 1)
                    ab["da"] += 1
                project_in(L)
                if kind == "fox":
                    fox(L)
                else:
                    linear(L)
                gain = None if kind == "fox" else PRM[kind + "_gain"]
                transposed(3 * l + 1, gain, EARLY)
                round_slab(L["out"] + 2, L["out"] + 2)
                transposed(3 * l + 1, gain, LATE)
                for n in range(L["out"] + 3, L["wq"] + 2):
                    round_slab(n, n)
                norm(2 * l + 1, L["pw"] + POWERS - 1)
                transposed(3 * l + 2, PRM["ffn"] + DC * l)
                for m in range(PH):
                    for s in range(2):
                        round_slab(L["wq"] + 2 * m + 2 + s, L["wq"] + 2 * m + 2 + s)
                    act.wait_ge(s_used, L["wq"] + 2 * m + 2)
                    nc.scalar.copy(QT[:, 2 * m:2 * m + 2, :].rearrange("p c t -> p (c t)"),
                                   ps[:, 4 + m % 2, :]).then_inc(s_cev, 1)
                n0 = L["u"]

                def u_steps(j0, j1):
                    with act.Fori(j0 // 4, j1 // 4) as i:
                        for s in range(4):
                            round_slab(i * 4 + (n0 + s + 2), n0 + s + 2)
                            if s % 2:
                                act.wait_ge(s_used, i * 4 + (n0 + s + 1))
                                nc.scalar.activation(H[:, bass.ds(i * 4 + (s - 1), 2), :].rearrange(
                                    "p c t -> p (c t)"), ps[:, 4 + s // 2, :], ACT.Gelu).then_inc(s_cev, 1)

                def gelu_table():
                    nc.scalar.activation(sm[:, 63:64], ident[:, 0:1], ACT.Gelu)

                gelu_table()
                u_steps(0, EXP_AT)
                for tt in range(TT):
                    act.wait_ge(s_ge, TT * l + tt + 1)
                    nc.scalar.activation(EXS[tt], BESTS[tt], ACT.Exp).then_inc(s_gn, 1)
                gelu_table()
                u_steps(EXP_AT, HALF)
                act.wait_ge(s_hm, (NCH + 2) * l + 2)
                u_steps(HALF, NCH)
                n0 = L["v"]

                def round_w(j, s, wait=True):
                    if wait:
                        act.wait_ge(s_used, j + (n0 - 3))
                    nc.scalar.copy(xhi[:, s, :], chunk(j)).then_inc(s_whi, 1)

                act.wait_ge(s_used, n0)
                for half in range(2):
                    j0 = half * HALF
                    act.wait_ge(s_hm, (NCH + 2) * l + 2 + j0 + HALF)
                    for s in range(2):
                        round_w(j0 + s, s, wait=half == 1)

                    def v_step(i, s, k):
                        n = k + (n0 + j0 + 2)
                        if not isinstance(i, int) or n < N:
                            round_slab(n, n0 + s + 2)
                        if not isinstance(i, int) or i == 0 or s < 2:
                            round_w(k + (j0 + 2), (s + 2) % 4, wait=not (isinstance(i, int) and half == 0 and k < 2))

                    steps(act, HALF, v_step, first=True)

        @block.vector
        def _(dve):
            chain = [0]

            def mark(ins):
                chain[0] += 1
                ins.then_inc(s_dve, 1)

            def join():
                dve.wait_ge(s_dve, chain[0])

            def link(ins):
                mark(ins)
                join()

            def split_slab(n, base):
                dve.wait_ge(s_hi, n + 1)
                if not (isinstance(n, int) and n < LO):
                    dve.wait_ge(s_used, n - LO + 1)
                nc.vector.tensor_tensor(lo[:, base % LO, :], raw[:, base % RAW, :], hi[:, base % HI, :],
                                        ALU.subtract).then_inc(s_lo, 1)

            def transposed(tau, gain, chunks=range(DC)):
                for c in chunks:
                    dve.wait_ge(s_xhi, DC * tau + (c | 1) + 1)
                    nc.vector.scalar_tensor_tensor(
                        out=xlo[:, c, :], in0=ps[:, c // 2, (c % 2) * SEQ:(c % 2 + 1) * SEQ],
                        scalar=1.0 if gain is None else prm[:, gain + c:gain + c + 1], in1=xhi[:, c, :],
                        op0=ALU.mult, op1=ALU.subtract).then_inc(s_xlo, 1)

            def mean_squares(out_, in_, n):
                nc.vector.tensor_scalar(out_, in_, 1.0 / n, EPS, ALU.mult, ALU.add).then_inc(s_ss, 1)
                ab["sq"] += 1
                return ab["sq"]

            def residual(r, n=None, bank=None, norm=True):
                for b in range(4):
                    tt, nh = divmod(b, 2)
                    if n is not None:
                        if b < 3:
                            dve.wait_ge(s_fin, 3 * (r - 1) + b + 1)
                        else:
                            dve.wait_ge(s_used, n)
                        w = resid[:, tt, nh * 512:(nh + 1) * 512]
                        nc.vector.tensor_tensor(w, ps[:, bank + b, :], w, ALU.add).then_inc(s_res, 1)
                    if b == 2 and norm:
                        dve.wait_ge(s_ssa, 2 * r + 1)
                        mean_squares(sm[:, 2:3], sm[:, 0:1], D)
                dve.wait_ge(s_res, 4 * r + 4)
                if norm:
                    dve.wait_ge(s_ssa, 2 * r + 2)
                    link(nc.vector.tensor_scalar(sm[:, 7:8], sm[:, 1:2], 1.0 / D, EPS, ALU.mult, ALU.add))
                    nc.vector.scalar_tensor_tensor(out=sm[:, 3:4], in0=sm[:, 6:7], scalar=1.0 / D,
                                                   in1=sm[:, 7:8], op0=ALU.mult, op1=ALU.add).then_inc(s_ss, 1)
                    ab["sq"] += 1
                    dve.wait_ge(s_sq, ab["sq"])
                    nc.vector.tensor_scalar(XN[:, 1, :], resid[:, 1, :], sm[:, 5:6], None,
                                            ALU.mult).then_inc(s_xn, 1)

            def forget_gates(L):
                bias = prm[0:FOX_HEADS, PRM["bf"] + L["fox"]:PRM["bf"] + L["fox"] + 1]
                dve.wait_ge(s_used, L["small"] + 1)
                link(nc.vector.tensor_scalar(LFT[0:16, :], ps[0:16, 0, 0:SEQ], bias, None, ALU.add))
                nc.vector.scalar_tensor_tensor(out=LFA[0:16, :], in0=LFT[0:16, :], scalar=-1.0, in1=LFT[0:16, :],
                                               op0=ALU.mult, op1=ALU.min).then_inc(s_da, 1)
                ab["da"] += 1

            def log_forget(L):
                ab["ab"] += 1
                dve.wait_ge(s_ab, ab["ab"])
                nc.vector.scalar_tensor_tensor(out=LFB[0:16, :], in0=LFT[0:16, :], scalar=0.0, in1=LFA[0:16, :],
                                               op0=ALU.min, op1=ALU.subtract).then_inc(s_lf, 1)

            def norm_qk(L, k):
                QK = {12: (0, 0), 13: (0, 1), 20: (1, 0), 21: (1, 1)}
                if k in QK:
                    side, tt = QK[k]
                    dve.wait_ge(s_ev, L["ev"] + 4 * (side + 1))
                    v = PR[:, tt, side * D:(side + 1) * D]
                    mark(nc.vector.tensor_tensor(SCR[:, tt * D:(tt + 1) * D], v, v, ALU.mult))
                if k - 2 in QK:
                    side, tt = QK[k - 2]
                    join()
                    mark(nc.vector.tensor_reduce(
                        QS[:, 32 * side + 16 * tt:32 * side + 16 * tt + 16],
                        SCR[:, tt * D:(tt + 1) * D].rearrange("p (h d) -> p h d", d=FOX_DH), AX.X, ALU.add))
                if k in (15, 23):
                    side = k // 16
                    join()
                    ab["qk", side] = mean_squares(QS[:, 32 * side:32 * side + 32],
                                                  QS[:, 32 * side:32 * side + 32], FOX_DH)
                SCALE = {24: (0, 0), 25: (0, 1), 27: (1, 0), 28: (1, 1)}
                if k in SCALE:
                    side, tt = SCALE[k]
                    dve.wait_ge(s_sq, ab["qk", side])
                    v = PR[:, tt, side * D:(side + 1) * D].rearrange("p (h d) -> p h d", d=FOX_DH)
                    r = QR[:, 32 * side + 16 * tt:32 * side + 16 * tt + 16]
                    nc.vector.tensor_tensor(v, v, r.unsqueeze(2).broadcast_to([P, 16, FOX_DH]),
                                            ALU.mult).then_inc(s_qk, 1)

            def fox_core(L):
                f = L["fox"]
                dve.wait_ge(s_lft, f + 1)
                v = ps[:, 0, 0:32].rearrange("p (t h) -> p t h", t=TT)
                link(nc.vector.tensor_copy(lfh[:], v))
                nc.vector.tensor_tensor(lfl[:], v, lfh[:], ALU.subtract).then_inc(s_lfc, 1)
                for m, b in enumerate((1, 2, 3, 0)):
                    dve.wait_ge(s_tq, 2 * L["tq"] + 5 + m)
                    nc.vector.tensor_scalar(TR[:, 2 * b:2 * b + 2, :].rearrange("p c t -> p (c t)"), ps[:, b, :],
                                            prm[:, PRM["qg"] + f:PRM["qg"] + f + 1], FOX_DH ** -0.5,
                                            ALU.mult, ALU.mult).then_inc(s_tqd, 1)
                b0 = FOX_HEADS * f
                for h in range(FOX_HEADS + 2):
                    if h in (2, 4):
                        n = L["out"] + h // 2 - 1
                        split_slab(n, n)
                    if h < FOX_HEADS:
                        dve.wait_ge(s_s, b0 + h + 1)
                        nc.vector.tensor_reduce(NM[:, h, 0:1], ps[:, h % 2, 0:P], AX.X, ALU.max, negate=True)
                        nc.vector.tensor_reduce(NM[:, h, 1:2], ps[:, h % 2, P:3 * P], AX.X, ALU.max,
                                                negate=True).then_inc(s_mx, 1)
                    if 1 <= h <= FOX_HEADS:
                        dve.wait_ge(s_exp, b0 + h)
                        mark(nc.vector.reciprocal(RL[:, h - 1, :], RSUM[:, h - 1, :]))
                    if h >= 2:
                        g = h - 2
                        dve.wait_ge(s_pv, b0 + g + 1)
                        join()
                        for tt in range(TT):
                            gate = PR[:, tt, 3 * D + g * FOX_DH:3 * D + (g + 1) * FOX_DH]
                            ins = nc.vector.scalar_tensor_tensor(
                                out=gate, in0=ps[:, 4 + g % 2, tt * FOX_DH:(tt + 1) * FOX_DH],
                                scalar=RL[:, g, tt:tt + 1], in1=gate, op0=ALU.mult, op1=ALU.mult)
                        ins.then_inc(s_o, 1)
                transposed(3 * L["l"] + 1, None, EARLY)
                transposed(3 * L["l"] + 1, None, LATE)

            def gla_gates(L, k):
                lg = LG[:, :, 0:512]
                if k == 0:
                    dve.wait_ge(s_used, L["small"] + 1)
                    dve.wait_ge(s_low, 1)
                    nc.vector.tensor_copy(LOWT[0:GLA_RANK, :], ps[0:GLA_RANK, 0, 0:SEQ]).then_inc(s_low, 1)
                if k == 3:
                    dve.wait_ge(s_z, 1)
                    link(nc.vector.tensor_copy(lg, ps[:, 2:4, :]))
                if k == 4:
                    nc.vector.scalar_tensor_tensor(out=XN[:, :, 0:512], in0=lg, scalar=-1.0, in1=lg,
                                                   op0=ALU.mult, op1=ALU.min).then_inc(s_da, 1)
                    ab["da"] += 1
                if k == 10:
                    ab["ab"] += 1
                    dve.wait_ge(s_ab, ab["ab"])
                    mark(nc.vector.scalar_tensor_tensor(out=lg, in0=lg, scalar=0.0, in1=XN[:, :, 512:1024],
                                                        op0=ALU.min, op1=ALU.subtract))
                if k == 11:
                    join()
                    nc.vector.tensor_scalar(lg, lg, 1.0 / GLA_TAU, None, ALU.mult).then_inc(s_lg, 1)

            def hgrn_bounds():
                i = KIND.index("hgrn")
                lb = prm[:, PRM["lb"]:PRM["lb"] + DEPTH * DC].rearrange("p (r c) -> p r c", c=DC)
                e = LBC[:, 0:32].rearrange("p (r c) -> p r c", c=DC)
                m = LBC[:, 32:40]
                r = LBC[:, 40:48]
                link(nc.vector.tensor_reduce(m, lb.rearrange("p r c -> p c r"), AX.X, ALU.max))
                nc.vector.tensor_tensor(e, lb, m.unsqueeze(1).broadcast_to([P, DEPTH, DC]),
                                        ALU.subtract).then_inc(s_da, 1)
                ab["da"] += 1
                ab["ab"] += 3
                dve.wait_ge(s_ab, ab["ab"] - 2)
                link(nc.vector.tensor_reduce(r, e.rearrange("p r c -> p c r"), AX.X, ALU.add))
                link(nc.vector.reciprocal(r, r))
                link(nc.vector.tensor_tensor(e, e, r.unsqueeze(1).broadcast_to([P, DEPTH, DC]), ALU.mult))
                link(nc.vector.tensor_copy(m, e[:, 0, :]))
                for j in range(1, i + 1):
                    link(nc.vector.tensor_tensor(m, m, e[:, j, :], ALU.add))
                nc.vector.tensor_tensor(LBC[:, 48:56], m, e[:, 0, :], ALU.subtract).then_inc(s_lb, 1)

            def hgrn_bound_rows():
                dve.wait_ge(s_lbr, 1)
                nc.vector.tensor_copy(LBR.rearrange("p (b c) -> p b c", b=2), ps[:, 0:2, :]).then_inc(s_lbc, 1)
                nc.vector.tensor_scalar(OML.rearrange("p (b c) -> p b c", b=2), ps[:, 0:2, :], -1.0, 1.0,
                                        ALU.mult, ALU.add).then_inc(s_lbc, 1)
                dve.wait_ge(s_lbc, 2)

            def hgrn_gates(L, k):
                if k == 0:
                    hgrn_bound_rows()
                if k in (20, 21):
                    dve.wait_ge(s_ev, L["ev"] + 8)
                    tt = k - 20
                    mark(nc.vector.tensor_tensor(SCR2[:, tt, :], PR[:, tt, D:2 * D], OML, ALU.mult))
                if k in (22, 23):
                    tt = k - 22
                    join()
                    nc.vector.tensor_tensor(SCR2[:, tt, :], SCR2[:, tt, :], LBR, ALU.add).then_inc(s_da, 1)
                    ab["da"] += 1
                if k in (24, 25):
                    tt = k - 24
                    dve.wait_ge(s_da, ab["da"])
                    nc.vector.tensor_scalar(PR[:, tt, D:2 * D], SCR2[:, tt, :], -1.0, 1.0,
                                            ALU.mult, ALU.add).then_inc(s_hk, 1)

            def linear_core(L):
                kind, H_ = L["kind"], HEADS[L["kind"]]
                dv = D // H_
                for b in range(H_ // 2):
                    dve.wait_ge(s_tq, 2 * L["tq"] + H_ // 2 + 1 + b)
                    nc.vector.tensor_scalar(TR[:, 2 * b:2 * b + 2, :].rearrange("p c t -> p (c t)"), ps[:, b, :],
                                            float(P) ** -0.5, None, ALU.mult).then_inc(s_tqd, 1)
                dve.wait_ge(s_tqd, L["tq"] + H_ // 2)
                dve.wait_ge(s_mc, L["l"] + 1)
                U, UA = 2 * H_, 2 * early_heads(L)
                for u in range(U + 1):
                    if u in (2, 4):
                        n = L["out"] + u // 2 - 1
                        split_slab(n, n)
                    if u == U:
                        dve.wait_ge(s_go, L["gu"] + UA)
                        early = mean_squares(sm[:, 24:24 + UA], sm[:, 8:8 + UA], dv)
                    if u < U:
                        g, h, tt = L["gu"] + u, u // 2, u % 2
                        dve.wait_ge(s_gx, g + 1)
                        if u >= 2:
                            dve.wait_ge(s_gs, g - 1)
                        lv, n = (1, LEVELS) if tt == 0 else (0, LEVELS + 1)
                        nc.vector.tensor_tensor(
                            QD[:, u % 2, lv:lv + n, :], EB[:, u % 2, lv:lv + n, :],
                            TR[:, h, tt * P:(tt + 1) * P].unsqueeze(1).broadcast_to([P, n, P]),
                            ALU.mult).then_inc(s_gq, 1)
                    if u >= 1:
                        w = u - 1
                        g, h, tt = L["gu"] + w, w // 2, w % 2
                        dve.wait_ge(s_gs, g + 1)
                        if g:
                            dve.wait_ge(s_gr, g)
                        b = 2 + 2 * (w % 2)
                        nc.vector.tensor_tensor(AM.rearrange("p l t -> p (l t)"),
                                                ps[:, b:b + 2, :].rearrange("p b c -> p (b c)"),
                                                MK.rearrange("p l t -> p (l t)"), ALU.mult).then_inc(s_gm, 1)
                        dve.wait_ge(s_gm, g + 1)
                        if w >= 2:
                            dve.wait_ge(s_gp, g - 1)
                        ins = nc.vector.tensor_reduce(ST[:, w % 2, :], AM.rearrange("p l t -> p t l"), AX.X, ALU.add)
                        if tt == 1:
                            mark(ins)
                            ins = nc.vector.tensor_copy(ST[:, 2 + h % 2, :], ps[:, 6, (h % 2) * P:(h % 2 + 1) * P])
                            join()
                        ins.then_inc(s_gr, 1)
                def normed(w0, w1):
                    gg = (GROUPS[kind] - 1) * D
                    for w in range(w0, w1):
                        h, tt = w // 2, w % 2
                        ins = nc.vector.scalar_tensor_tensor(
                            out=XN[:, tt, h * dv:(h + 1) * dv], in0=PR[:, tt, h * dv:(h + 1) * dv],
                            scalar=sm[:, 40 + w:41 + w],
                            in1=PR[:, tt, gg + h * dv:gg + (h + 1) * dv], op0=ALU.mult, op1=ALU.mult)
                    ins.then_inc(s_xh, 1)

                gain, tau = PRM[kind + "_gain"], 3 * L["l"] + 1
                dve.wait_ge(s_sq, early)
                normed(0, UA)
                dve.wait_ge(s_go, L["gu"] + U)
                late = mean_squares(sm[:, 24 + UA:24 + U], sm[:, 8 + UA:8 + U], dv)
                transposed(tau, gain, EARLY)
                dve.wait_ge(s_sq, late)
                normed(UA, U)
                transposed(tau, gain, LATE)

            def top16(src, tmp, val, idx, batch):
                for c in batch:
                    mark(nc.vector.max(val[:, c, 0:8], src(c)))
                join()
                for c in batch:
                    mark(nc.vector.max_index(idx[:, c, 0:8].bitcast(U32), val[:, c, 0:8], src(c)))
                    mark(nc.vector.match_replace(tmp(c), val[:, c, 0:8], src(c), NEG))
                join()
                for c in batch:
                    mark(nc.vector.max(val[:, c, 8:16], tmp(c)))
                join()
                for c in batch:
                    mark(nc.vector.max_index(idx[:, c, 8:16].bitcast(U32), val[:, c, 8:16], tmp(c)))

            def route(L, tt):
                l, BEST = L["l"], BESTS[tt]
                for b in range(4):
                    dve.wait_ge(s_sc, 8 * l + 4 * tt + b + 1)
                    top16(lambda c: ps[:, c // 4, (c % 4) * NK:(c % 4 + 1) * NK], lambda c: TMP[:, c, :],
                          VAL, IDX, range(4 * b, 4 * b + 4))
                join()
                mark(nc.vector.tensor_copy(IDF, IDX.bitcast(U32)))
                v = VAL.rearrange("p (h s) k -> p h s k", s=2)
                cand = CAND.rearrange("p (h a b) -> p h a b", h=PH, a=TOPK)
                nc.vector.tensor_tensor(cand, v[:, :, 0, :].unsqueeze(3).broadcast_to([P, PH, TOPK, TOPK]),
                                        v[:, :, 1, :].unsqueeze(2).broadcast_to([P, PH, TOPK, TOPK]),
                                        ALU.add).then_inc(s_rt, 1)
                dve.wait_ge(s_rt, TT * l + tt + 1)
                ch = CAND.rearrange("p (h c) -> p h c", h=PH)
                eh = EQ.rearrange("p (h c) -> p h c", h=PH)
                for b in range(2):
                    top16(lambda c: ch[:, c, :], lambda c: eh[:, c, :], BEST, POS, range(4 * b, 4 * b + 4))
                join()
                mark(nc.vector.tensor_scalar(PAB[:, 0, :].bitcast(U32), POS.rearrange("p h k -> p (h k)").bitcast(U32),
                                             4, None, ALU.logical_shift_right))
                mark(nc.vector.tensor_scalar(PAB[:, 1, :].bitcast(U32), POS.rearrange("p h k -> p (h k)").bitcast(U32),
                                             15, None, ALU.bitwise_and))
                mark(nc.vector.tensor_copy(ZS[:, 0:8].unsqueeze(2), BEST[:, :, 0:1]))
                join()
                nc.vector.tensor_tensor(BEST, BEST, ZS[:, 0:8].unsqueeze(2).broadcast_to([P, PH, TOPK]),
                                        ALU.subtract).then_inc(s_ge, 1)
                link(nc.vector.tensor_copy(PAF, PAB.bitcast(U32)))
                ix = IDF.rearrange("p (h s) k -> p h s k", s=2)
                eq = EQ.rearrange("p (c a) -> p c a", a=TOPK)
                for side in range(2):
                    link(nc.vector.tensor_tensor(eq, PAF[:, side, :].unsqueeze(2).broadcast_to([P, P, TOPK]),
                                                 iota[:, 0:TOPK].unsqueeze(1).broadcast_to([P, P, TOPK]), ALU.is_equal))
                    e4 = EQ.rearrange("p (h k a) -> p h k a", h=PH, a=TOPK)
                    link(nc.vector.tensor_tensor(e4, e4, ix[:, :, side, :].unsqueeze(2).broadcast_to([P, PH, TOPK, TOPK]),
                                                 ALU.mult))
                    link(nc.vector.tensor_reduce(ROUT[tt][:, side, :], eq, AX.X, ALU.add))

            def gate(L, tt):
                l, EX = L["l"], EXS[tt]
                dve.wait_ge(s_gn, TT * l + tt + 1)
                link(nc.vector.tensor_reduce(ZS[:, 8:16], EX, AX.X, ALU.add))
                link(nc.vector.reciprocal(ZS[:, 8:16], ZS[:, 8:16]))
                nc.vector.tensor_tensor(ROUT[tt][:, 2, :].rearrange("p (h k) -> p h k", k=TOPK), EX,
                                        ZS[:, 8:16].unsqueeze(2).broadcast_to([P, PH, TOPK]),
                                        ALU.mult).then_inc(s_route, 1)
                dve.wait_ge(s_route, TT * l + tt + 1)

            def split_w(k, n, s):
                dve.wait_ge(s_whi, n)
                nc.vector.tensor_tensor(xlo[:, s, :], chunk(k), xhi[:, s, :], ALU.subtract).then_inc(s_wlo, 1)

            def one_hots(i, s, half, at):
                t0 = i * 16 + 4 * s
                tok = lambda e, w: e[:, bass.ds(t0, 4)].unsqueeze(2).broadcast_to([P, 4, w])
                dve.wait_ge(s_g, i * 4 + (at + s + 1))
                nc.vector.tensor_tensor(oh1[:, s % 2], iota[:].unsqueeze(1).broadcast_to([P, 4, P]),
                                        tok(e1T, P), ALU.is_equal)
                nc.vector.tensor_tensor(oh2[:, s % 2],
                                        iota[:, half * HALF:(half + 1) * HALF].unsqueeze(1).broadcast_to([P, 4, HALF]),
                                        tok(e2T, HALF), ALU.is_equal).then_inc(s_eq, 1)

            def weigh(i, s, half, at):
                dve.wait_ge(s_g, i * 4 + (at + s + 3))
                v = H[:, half * HALF:(half + 1) * HALF, bass.ds(i * 16 + 4 * s, 4)]
                nc.vector.scalar_tensor_tensor(
                    out=v, in0=ps[:, 6 + s % 2, 0:4 * HALF].rearrange("p (t j) -> p j t", t=4),
                    scalar=1.0 / GATE_SCALE, in1=v, op0=ALU.mult, op1=ALU.mult).then_inc(s_hm, 1)

            ab = {"ab": 0, "sq": 0, "da": 0}
            for tt in range(TT):
                dve.wait_ge(s_x[tt], 16)
                nc.vector.memset(sm[:, 60 + tt:61 + tt], 0.0).then_inc(s_res, 2)
            residual(0)
            dve.wait_ge(s_prm, 16)
            dve.wait_ge(s_const, 2)
            for L in PLAN.layers:
                l, kind = L["l"], L["kind"]
                transposed(3 * l, PRM["mix"] + DC * l)
                if kind == "hgrn":
                    hgrn_bounds()
                if kind == "gla":
                    nc.vector.memset(LOWT[0:32, :], 1.0).then_inc(s_low, 1)
                dve.wait_ge(s_lo, L["small"] + 2)
                for n in range(L["small"], L["out"]):
                    k = n - L["in"]
                    if n >= L["small"] + 2:
                        split_slab(n, n)
                    if kind == "fox":
                        if k == 0:
                            forget_gates(L)
                        if k == 10:
                            log_forget(L)
                        norm_qk(L, k)
                    elif kind == "gla":
                        gla_gates(L, k)
                    else:
                        hgrn_gates(L, k)
                if kind == "fox":
                    fox_core(L)
                else:
                    linear_core(L)
                for n in range(L["out"] + 2, L["wq"]):
                    split_slab(n, n)
                residual(2 * l + 1, L["wq"], 4)
                transposed(3 * l + 2, PRM["ffn"] + DC * l)
                dve.wait_ge(s_lo, L["wq"] + 2)
                for n in range(L["wq"] + 2, L["u"]):
                    split_slab(n, n)
                for tt in range(TT):
                    route(L, tt)
                for tt in range(TT):
                    gate(L, tt)
                g0 = (NCH + 2) * l
                dve.wait_ge(s_g, g0 + 2)
                link(nc.vector.tensor_scalar(gate2[:, 0, :], ps[:, 7, 0:SEQ], GATE_SCALE, None, ALU.mult))
                mark(nc.vector.tensor_copy(e1T[:], ps[:, 6, 0:SEQ]))
                nc.vector.tensor_copy(e2T[:], ps[:, 6, SEQ:2 * SEQ]).then_inc(s_hm, 1)
                nc.vector.scalar_tensor_tensor(out=gate2[:, 1, :], in0=ps[:, 7, 0:SEQ], scalar=GATE_SCALE,
                                               in1=gate2[:, 0, :], op0=ALU.mult,
                                               op1=ALU.subtract).then_inc(s_hm, 1)
                dve.wait_ge(s_hm, g0 + 2)
                dve.wait_ge(s_lo, L["u"] + HALF + 1)
                for half in range(2):
                    n0 = (L["u"] + HALF, L["v"])[half]
                    at = g0 + half * HALF
                    if half == 1:
                        split_w(0, NCH * l + 1, 0)
                    one_hots(0, 0, half, at)
                    dve.wait_ge(s_cev, (PH + HALF) * l + PH + HALF // 2 * (half + 1))

                    def g_step(i, s, k):
                        last = isinstance(k, int) and k == HALF - 1
                        split_slab(k + (n0 + 1), n0 + s + 1)
                        if not last:
                            if s < 3:
                                one_hots(i, s + 1, half, at)
                            else:
                                one_hots(i + 1, 0, half, at)
                        weigh(i, s, half, at)

                    steps(dve, HALF, g_step)
                n0 = L["v"] + HALF
                dve.wait_ge(s_wlo, NCH * l + HALF)
                split_w(HALF, NCH * l + HALF + 1, 0)

                def v_step(i, s, k):
                    if not (isinstance(k, int) and k == HALF - 1):
                        split_slab(k + (n0 + 1), n0 + s + 1)
                        split_w(k + (HALF + 1), k + (NCH * l + HALF + 2), (s + 1) % 4)

                steps(dve, HALF, v_step)
                residual(2 * l + 2, L["end"], 0, norm=l < DEPTH - 1)
            nc.vector.tensor_copy(sm[:, 62:63], sm[:, 60:61]).then_inc(s_done, 1)

        @block.tensor
        def _(pe):
            def product(out_, lh, ll, rh, rl, start, stop):
                nc.tensor.matmul(out_, lh, rh, start=start, stop=False)
                nc.tensor.matmul(out_, lh, rl, start=False, stop=False)
                return nc.tensor.matmul(out_, ll, rh, start=False, stop=stop)

            def row_step(n, base, c, bank, start, stop, tau=None):
                if tau is not None:
                    pe.wait_ge(s_xlo, DC * tau + c + 1)
                pe.wait_ge(s_lo, n + 1)
                for tt in range(TT):
                    t = slice(tt * P, (tt + 1) * P)
                    for nh in range(2):
                        w = slice(nh * 512, (nh + 1) * 512)
                        ins = product(ps[:, bank + 2 * tt + nh, :], xhi[:, c, t], xlo[:, c, t],
                                      hi[:, base % HI, w], lo[:, base % LO, w], start, stop)
                ins.then_inc(s_used, 1)

            def col_step(n, base, out_, tau=None):
                pe.wait_ge(s_lo, n + 1)
                for c in range(DC):
                    if tau is not None:
                        pe.wait_ge(s_xlo, DC * tau + c + 1)
                    w = slice(c * P, (c + 1) * P)
                    ins = product(out_, hi[:, base % HI, w], lo[:, base % LO, w], xhi[:, c, :], xlo[:, c, :],
                                  c == 0, c == DC - 1)
                ins.then_inc(s_used, 1)

            def last_steps(n, c, bank):
                pe.wait_ge(s_lo, n + 2)
                for tt in range(TT):
                    t = slice(tt * P, (tt + 1) * P)
                    for nh in range(2):
                        w = slice(nh * 512, (nh + 1) * 512)
                        for q in range(2):
                            ins = product(ps[:, bank + 2 * tt + nh, :], xhi[:, c + q, t], xlo[:, c + q, t],
                                          hi[:, (n + q) % HI, w], lo[:, (n + q) % LO, w], False, q == 1)
                            if (tt, nh) == (1, 1):
                                ins.then_inc(s_used, 1)
                            elif q == 1:
                                ins.then_inc(s_fin, 1)

            def tile_transposed(c, tt, rows):
                o = (c % 2) * SEQ + tt * P
                return nc.tensor.transpose(ps[:, c // 2, o:o + P], rows[:, c * P:(c + 1) * P], ident[:])

            def transposed(chunks, src):
                for c in chunks:
                    for tt in range(TT):
                        ins = tile_transposed(c, tt, src(tt))
                    ins.then_inc(s_tp, 1)

            def norm_transposed(r):
                pe.wait_ge(s_xa, r + 1)
                for c in range(DC):
                    if c in (4, 6):
                        pe.wait_ge(s_res, 4 * r + c // 2 + 1)
                    tile_transposed(c, 0, XN[:, 0, :])
                pe.wait_ge(s_xn, r + 1)
                for c in range(DC):
                    tile_transposed(c, 1, XN[:, 1, :]).then_inc(s_tp, 1)

            def project_in(L):
                kind, tau = L["kind"], 3 * L["l"]
                for n in range(L["small"], L["in"]):
                    pe.wait_ge(s_xlo, DC * tau + 2)
                    col_step(n, n, ps[:, 0, 0:SEQ], tau)
                for g in range(GROUPS[kind]):
                    if g == 1:
                        pe.wait_ge(s_xlo, DC * (tau + 1))
                        if kind == "hgrn":
                            pe.wait_ge(s_lbc, 2)
                        else:
                            pe.wait_ge(s_da, HANDED[L["l"]][0] + 1)
                    if g >= 2:
                        pe.wait_ge(s_ev, L["ev"] + 4 * (g - 1))
                    for c in range(DC):
                        n = L["in"] + g * DC + c
                        row_step(n, n, c, BANKS[g % 2], c == 0, c == DC - 1, tau if g == 0 else None)
                        if kind == "hgrn" and n == L["in"]:
                            pe.wait_ge(s_lb, 1)
                            pe.wait_ge(s_xlo, DC * tau + 4)
                            for q in range(DC):
                                ins = nc.tensor.matmul(ps[:, q // 4, (q % 4) * P:(q % 4 + 1) * P],
                                                       LBC[:, 48 + q:49 + q].broadcast_to([P, P]), ident[:],
                                                       start=True, stop=True)
                            ins.then_inc(s_lbr, 1)
                        if kind == "gla" and n == L["in"] + 1:
                            pe.wait_ge(s_wup, 16)
                            pe.wait_ge(s_low, 2)
                            pe.wait_ge(s_xlo, DC * (tau + 1))
                            for tt in range(TT):
                                ins = nc.tensor.matmul(ps[:, 2 + tt, :], LOWT[0:GLA_RANK + 1, tt * P:(tt + 1) * P],
                                                       WUP[0:GLA_RANK + 1, :], start=True, stop=True)
                            ins.then_inc(s_z, 1)

            def chunks_transposed(L, banks):
                for b in banks:
                    if b == 0 and L["kind"] == "fox":
                        pe.wait_ge(s_lfc, L["fox"] + 1)
                    for c in (2 * b, 2 * b + 1):
                        for tt in range(TT):
                            o = (c % 2) * SEQ + tt * P
                            ins = nc.tensor.transpose(ps[:, b, o:o + P], PR[:, tt, c * P:(c + 1) * P], ident[:])
                    ins.then_inc(s_tq, 1)

            def fox(L):
                f = L["fox"]
                b0 = FOX_HEADS * f
                pe.wait_ge(s_qk, 4 * (f + 1))
                pe.wait_ge(s_ev, L["ev"] + 12)
                chunks_transposed(L, (4, 5, 6, 7))
                pe.wait_ge(s_ev, L["ev"] + 16)
                pe.wait_ge(s_lf, f + 1)
                for tt in range(TT):
                    ins = nc.tensor.transpose(ps[:, 0, 16 * tt:16 * tt + 16], LFB[0:16, tt * P:(tt + 1) * P],
                                              ident[0:16, 0:16])
                ins.then_inc(s_lft, 1)
                chunks_transposed(L, (1, 2, 3, 0))
                pe.wait_ge(s_tqd, L["tq"] + 4)
                pe.wait_ge(s_tqa, L["tq"] + 4)

                def logits(h):
                    if h >= 2:
                        pe.wait_ge(s_exp, b0 + h - 1)
                    c, r = h // 2, slice(64 * (h % 2), 64 * (h % 2) + 64)
                    s0, s1 = ps[:, h % 2, 0:P], ps[:, h % 2, P:3 * P]

                    def gates(out_, tt, n):
                        nc.tensor.matmul(out_, lfh[:, tt, h:h + 1].broadcast_to([P, P]), nur[:, 0:n],
                                         start=False, stop=False)
                        nc.tensor.matmul(out_, lfl[:, tt, h:h + 1].broadcast_to([P, P]), nur[:, 0:n],
                                         start=False, stop=False)

                    nc.tensor.matmul(s0, TR[r, c, 0:P], TR[r, 8 + c, 0:P], start=True, stop=False)
                    gates(s0, 0, P)
                    nc.tensor.matmul(s0, identb[:], maskb[:], start=False, stop=True)
                    nc.tensor.matmul(s1, TR[r, c, P:2 * P], TR[r, 8 + c, :], start=True, stop=False)
                    gates(s1, 0, 2 * P)
                    gates(s1[:, P:2 * P], 1, P)
                    nc.tensor.matmul(s1[:, P:2 * P], identb[:], maskb[:], start=False, stop=True).then_inc(s_s, 1)

                logits(0)
                for h in range(FOX_HEADS + 1):
                    if h + 1 < FOX_HEADS:
                        logits(h + 1)
                    if h < FOX_HEADS:
                        pe.wait_ge(s_exp, b0 + h + 1)
                        if h >= 2:
                            pe.wait_ge(s_pte, b0 + h - 1)
                        for b in range(3):
                            ins = nc.tensor.transpose(ps[:, 2 + h % 2, b * P:(b + 1) * P],
                                                      PB[:, h % 2, b * P:(b + 1) * P], ident[:])
                        ins.then_inc(s_pt, 1)
                    if h >= 1:
                        g = h - 1
                        pe.wait_ge(s_pte, b0 + g + 1)
                        if g >= 2:
                            pe.wait_ge(s_o, b0 + g - 1)
                        v = lambda tt: PR[:, tt, 2 * D + g * FOX_DH:2 * D + (g + 1) * FOX_DH]
                        o = ps[:, 4 + g % 2, 0:2 * FOX_DH]
                        pt = lambda b: PTB[:, g % 2, b * P:(b + 1) * P]
                        nc.tensor.matmul(o[:, 0:FOX_DH], pt(0), v(0), start=True, stop=True)
                        nc.tensor.matmul(o[:, FOX_DH:], pt(1), v(0), start=True, stop=False)
                        nc.tensor.matmul(o[:, FOX_DH:], pt(2), v(1), start=False, stop=True).then_inc(s_pv, 1)
                pe.wait_ge(s_o, b0 + FOX_HEADS)

            def project_out(L):
                for c in range(DC - 2):
                    if c < 2:
                        if L["kind"] == "fox":
                            src = lambda tt: PR[:, tt, 3 * D:4 * D]
                        else:
                            src = lambda tt: XN[:, tt, :]
                            pe.wait_ge(s_xh, 2 * L["lin"] + c + 1)
                        transposed((EARLY, LATE)[c], src)
                        if c == 0 and L["kind"] != "fox":
                            pe.wait_ge(s_go, L["gu"] + 2 * HEADS[L["kind"]])
                    row_step(L["out"] + c, L["out"] + c, c, BANKS[0], c == 0, False, 3 * L["l"] + 1)
                pe.wait_ge(s_xlo, DC * (3 * L["l"] + 2))
                last_steps(L["out"] + DC - 2, DC - 2, BANKS[0])

            def linear(L):
                kind, H_ = L["kind"], HEADS[L["kind"]]
                dv = D // H_
                G, nb = GROUPS[kind], H_ // 2
                pe.wait_ge(s_ev, L["ev"] + 4 * (G - 1))
                if kind == "hgrn":
                    pe.wait_ge(s_hk, 2)
                chunks_transposed(L, range(nb, 2 * nb))
                if kind == "hgrn":
                    pe.wait_ge(s_ev, L["ev"] + 4 * G)
                chunks_transposed(L, range(nb))
                pe.wait_ge(s_ev, L["ev"] + 4 * G)
                pe.wait_ge(s_tqd, L["tq"] + nb)
                pe.wait_ge(s_tqa, L["tq"] + nb)
                pe.wait_ge(s_mc, L["l"] + 1)
                if kind == "gla":
                    pe.wait_ge(s_lg, 1)
                else:
                    pe.wait_ge(s_ab, HANDED[L["l"]][1] + 3)
                vg = (GROUPS[kind] - 2) * D
                U = 2 * H_

                def decays(u):
                    g, h, tt = L["gu"] + u, u // 2, u % 2
                    if u >= 1:
                        pe.wait_ge(s_gx, g)
                    for b in range(2):
                        ins = nc.tensor.matmul(ps[:, b, :], LG[:, tt, h * P:(h + 1) * P],
                                               MC[:, tt + 4 * b:tt + 4 * b + 4, :], start=True, stop=True)
                    ins.then_inc(s_gd, 1)

                def scores(u):
                    g, h, tt = L["gu"] + u, u // 2, u % 2
                    lv = 1 - tt
                    pe.wait_ge(s_gq, g + 1)
                    pe.wait_ge(s_gk, g + 1)
                    if u >= 2:
                        pe.wait_ge(s_gr, g - 1)
                    b = 2 + 2 * (u % 2)
                    if tt == 1:
                        nc.tensor.matmul(ps[:, 6, (h % 2) * P:(h % 2 + 1) * P], KS[:, h % 2, :],
                                         QD[:, 1, LEVELS, :], start=True, stop=True)
                    for l in range(LEVELS):
                        nc.tensor.matmul(ps[:, b + l // 4, (l % 4) * P:(l % 4 + 1) * P], KD[:, u % 2, lv + l, :],
                                         QD[:, u % 2, lv + l, :], start=True, stop=True)
                    t = slice(tt * P, (tt + 1) * P)
                    nc.tensor.matmul(ps[:, b + 1, 3 * P:4 * P], TR[:, H_ + h, t], TR[:, h, t],
                                     start=True, stop=True).then_inc(s_gs, 1)

                def values(u):
                    g, h, tt = L["gu"] + u, u // 2, u % 2
                    pe.wait_ge(s_gr, g + 1)
                    if u >= 1:
                        pe.wait_ge(s_go, g)
                    o = ps[:, 7, (u % 2) * 256:(u % 2) * 256 + dv]
                    v = lambda t: PR[:, t, vg + h * dv:vg + (h + 1) * dv]
                    ins = nc.tensor.matmul(o, ST[:, u % 2, :], v(tt), start=True, stop=tt == 0)
                    if tt == 1:
                        ins = nc.tensor.matmul(o, ST[:, 2 + h % 2, :], v(0), start=False, stop=True)
                    ins.then_inc(s_gp, 1)

                decays(0)
                for u in range(U + 1):
                    if u + 1 < U:
                        decays(u + 1)
                    if u < U:
                        scores(u)
                    if u >= 1:
                        values(u - 1)

            def key_scores(L, tt):
                for b in range(4):
                    for q in range(4):
                        c = 4 * b + q
                        ins = nc.tensor.matmul(ps[:, b, q * NK:(q + 1) * NK], QT[:, c, tt * P:(tt + 1) * P],
                                               SK[:, c * NK:(c + 1) * NK], start=True, stop=True)
                    ins.then_inc(s_sc, 1)

            def g_product(i, s, oh, at):
                pe.wait_ge(s_ohg, i * 4 + (oh + s + 1))
                pe.wait_ge(s_hm, i * 4 + (at + s + 1))
                for t in range(4):
                    o = ps[:, 6 + s % 2, t * HALF:(t + 1) * HALF]
                    for q in range(2):
                        ins = nc.tensor.matmul(o, oh1[:, s % 2, t, :], ohg[:, s % 2, q, t, :],
                                               start=q == 0, stop=q == 1)
                ins.then_inc(s_g, 1)

            pe.wait_ge(s_const, 1)
            for L in PLAN.layers:
                l, kind = L["l"], L["kind"]
                norm_transposed(2 * l)
                project_in(L)
                if kind == "fox":
                    fox(L)
                else:
                    linear(L)
                project_out(L)
                norm_transposed(2 * l + 1)
                c0 = (PH + HALF) * l
                for c in range(2 * PH):
                    if c % 2 == 0 and c >= 4:
                        pe.wait_ge(s_cev, c0 + c // 2 - 1)
                    n = L["wq"] + c
                    col_step(n, n, ps[:, 4 + c // 2 % 2, (c % 2) * SEQ:(c % 2 + 1) * SEQ],
                             3 * l + 2 if c == 0 else None)
                pe.wait_ge(s_cev, c0 + PH)
                pe.wait_ge(s_sk, 16 * (l + 1))
                key_scores(L, 0)
                n0 = L["u"]
                c0 += PH

                def u_steps(j0, j1, with_g=False):
                    with pe.Fori(j0 // 4, j1 // 4) as i:
                        for s in range(4):
                            if s % 2 == 0:
                                pe.wait_ge(s_cev, i * 2 + (c0 + s // 2 - 1))
                            col_step(i * 4 + (n0 + s), n0 + s, ps[:, 4 + s // 2, (s % 2) * SEQ:(s % 2 + 1) * SEQ])
                            if with_g:
                                g_product(i, s, NCH * l - HALF, (NCH + 2) * l - HALF)

                u_steps(0, SCORES_AT)
                pe.wait_ge(s_rt, TT * l + 1)
                key_scores(L, 1)
                u_steps(SCORES_AT, HALF)
                pe.wait_ge(s_route, TT * (l + 1))
                for w in range(3):
                    for tt in range(TT):
                        o = (w % 2) * SEQ + tt * P
                        ins = nc.tensor.transpose(ps[:, 6 + w // 2, o:o + P], ROUT[tt][:, w, :], ident[:])
                    if w:
                        ins.then_inc(s_g, 1)
                u_steps(HALF, NCH, with_g=True)
                for half in range(2):
                    n0 = L["v"] + half * HALF

                    def v_step(i, s, k):
                        pe.wait_ge(s_wlo, k + (NCH * l + half * HALF + 1))
                        if half == 1 and isinstance(k, int) and k >= HALF - 2:
                            if k == HALF - 1:
                                last_steps(k - 1 + n0, s - 1, 0)
                            return
                        row_step(k + n0, n0 + s, s, 0, isinstance(k, int) and half == 0 and k == 0, False)
                        if half == 0:
                            g_product(i, s, NCH * l + HALF, (NCH + 2) * l + HALF)

                    steps(pe, HALF, v_step, first=half == 0)


def slabs_of_rows(w):
    n = w.shape[1] // D
    return w.reshape(DC, P, n, D).transpose(2, 0, 1, 3).reshape(n * DC, P, D)


def slabs_of_columns(w):
    n = w.shape[1] // P
    return w.reshape(DC, P, n, P).transpose(2, 1, 0, 3).reshape(n, P, D)


def narrow_slab(w):
    return slabs_of_columns(np.concatenate([w, np.zeros((D, P - w.shape[1]), w.dtype)], axis=1))


def kernel(x, norm_mix, norm_ffn, fox_w_in, fox_b_f, fox_q_gain, fox_k_gain, fox_w_out,
           gla_w_in, gla_w_up, gla_b_alpha, gla_out_gain, gla_w_out,
           hgrn_w_in, hgrn_lb_logits, hgrn_out_gain, hgrn_w_out,
           peer_w_q, peer_sub_keys, peer_u, peer_v):
    import concourse.bacc as bacc
    from concourse.bass_utils import run_bass_kernel_spmd

    stream = np.empty((PLAN.slabs, P, D), np.float32)

    def put(n, slabs):
        stream[n:n + len(slabs)] = slabs

    w_in = {"fox": fox_w_in, "gla": gla_w_in, "hgrn": hgrn_w_in}
    w_out = {"fox": fox_w_out, "gla": gla_w_out, "hgrn": hgrn_w_out}
    for L in PLAN.layers:
        l, kind = L["l"], L["kind"]
        which = L["fox"] if kind == "fox" else 0
        wi, wo = np.asarray(w_in[kind][which]), np.asarray(w_out[kind][which])
        wide = GROUPS[kind] * D
        if SMALL[kind]:
            put(L["small"], narrow_slab(wi[:, wide:]))
        put(L["in"], slabs_of_rows(wi[:, :wide]))
        put(L["out"], slabs_of_rows(wo))
        put(L["wq"], slabs_of_columns(np.asarray(peer_w_q[l])))
        u = np.asarray(peer_u[l]).reshape(P, NCH, DC, P)
        put(L["u"], u.transpose(1, 3, 2, 0).reshape(NCH, P, D))
        put(L["v"], np.asarray(peer_v[l]).reshape(P, NCH, D).transpose(1, 0, 2))

    def columns(a):
        return np.asarray(a).reshape(-1, DC, P).transpose(2, 0, 1).reshape(P, -1)

    prm = np.zeros((P, NPRM), np.float32)
    for name, a in (("mix", norm_mix), ("ffn", norm_ffn), ("gla_gain", gla_out_gain), ("hgrn_gain", hgrn_out_gain),
                    ("lb", hgrn_lb_logits)):
        c = columns(a)
        prm[:, PRM[name]:PRM[name] + c.shape[1]] = c
    for name, a in (("qg", fox_q_gain), ("kg", fox_k_gain)):
        a = np.asarray(a)
        prm[:, PRM[name]:PRM[name] + 2] = np.concatenate([a, a], axis=1).T
    prm[0:FOX_HEADS, PRM["bf"]:PRM["bf"] + 2] = np.asarray(fox_b_f).T
    wup = np.concatenate([np.asarray(gla_w_up[0]), np.asarray(gla_b_alpha)], axis=0)
    sk = np.asarray(peer_sub_keys).transpose(0, 4, 1, 2, 3).reshape(DEPTH, P, 2 * PH * NK)

    nc = bacc.Bacc("TRN2", target_bir_lowering=False, num_devices=1)
    arrays = {"stream": stream, "x": np.asarray(x).reshape(SEQ, D), "prm": prm, "wup": wup, "sk": sk}
    aps = {k: nc.dram_tensor(f"in_{k}", a.shape, F32, kind="ExternalInput").ap() for k, a in arrays.items()}
    out = nc.dram_tensor("out_0", (SEQ, D), F32, kind="ExternalOutput").ap()
    build(nc, aps["stream"], aps["x"], aps["prm"], aps["wup"], aps["sk"], out)
    r = run_bass_kernel_spmd(nc, [{f"in_{k}": np.ascontiguousarray(a) for k, a in arrays.items()}], core_ids=[0])
    return r.results[0]["out_0"].reshape(1, SEQ, D)
```
